# Optimizing a Trainium2 kernel written in Bass

```python
import math
import jax, jax.numpy as jnp
from jax import lax
import numpy as np

D_MODEL = 1024
BATCH = 1
SEQ = 256
DEPTH = 2

CHUNK = 64
EPS = 1e-6
NEG_INF = -1e30
HEAD_DIM = 64
N_Q_HEADS = 8
N_KV_HEADS = 2
Q_WIDTH = N_Q_HEADS * HEAD_DIM
KV_WIDTH = N_KV_HEADS * HEAD_DIM
WINDOW = 128
WINDOW_CHUNKS = WINDOW // CHUNK
ROPE_THETA = 500000.0
ROT_DIM = HEAD_DIM // 4
LRU_WIDTH = D_MODEL // 2
LRU_BLOCKS = 8
LRU_BLOCK = LRU_WIDTH // LRU_BLOCKS
CONV_WIDTH = 4
LRU_C = 8.0
IN_SPLITS = (Q_WIDTH, Q_WIDTH + KV_WIDTH, Q_WIDTH + 2 * KV_WIDTH, Q_WIDTH + 2 * KV_WIDTH + LRU_WIDTH)
IN_WIDTH = Q_WIDTH + 2 * KV_WIDTH + 2 * LRU_WIDTH
MIX_WIDTH = Q_WIDTH + LRU_WIDTH
SSM_GROUP = 16
SSM_GROUPS = D_MODEL // SSM_GROUP
SSM_STATE = 64
DT_MIN = 0.001
DT_MAX = 0.1
N_GROUPS = 4
EXPERTS_PER_GROUP = 4
N_EXPERTS = N_GROUPS * EXPERTS_PER_GROUP
TOP_K = 2
D_FF_EXPERT = 512
N_AB = (DEPTH + 1) // 2
N_C = DEPTH // 2

kernel_name = "hybrid_swa_rglru_s5_hmoe_block"

def _rmsnorm(x, g):
    xf = x.astype(jnp.float32)
    y = xf * lax.rsqrt(jnp.mean(xf * xf, axis=-1, keepdims=True) + EPS)
    return (y * g.astype(jnp.float32)).astype(x.dtype)

def _modulate(h, shift, scale):
    return h * (1 + scale[:, None, :]) + shift[:, None, :]

def _partial_rope(x, positions):
    half = ROT_DIM // 2
    inv_freq = ROPE_THETA ** (-jnp.arange(0, ROT_DIM, 2, dtype=jnp.float32) / ROT_DIM)
    ang = positions.astype(jnp.float32)[..., None] * inv_freq
    cos = jnp.cos(ang)[:, :, None, :]
    sin = jnp.sin(ang)[:, :, None, :]
    xr = x[..., :ROT_DIM].astype(jnp.float32)
    x1, x2 = xr[..., :half], xr[..., half:]
    rot = jnp.concatenate([x1 * cos - x2 * sin, x2 * cos + x1 * sin], axis=-1).astype(x.dtype)
    return jnp.concatenate([rot, x[..., ROT_DIM:]], axis=-1)

def _window_sink_attention(q, k, v, sinks):
    B, S = q.shape[0], q.shape[1]
    n_chunks = S // CHUNK
    grp = N_Q_HEADS // N_KV_HEADS
    qb = q.reshape(B, n_chunks, CHUNK, N_KV_HEADS, grp, HEAD_DIM)
    pad = ((0, 0), (WINDOW_CHUNKS - 1, 0), (0, 0), (0, 0), (0, 0))
    kp = jnp.pad(k.reshape(B, n_chunks, CHUNK, N_KV_HEADS, HEAD_DIM), pad)
    vp = jnp.pad(v.reshape(B, n_chunks, CHUNK, N_KV_HEADS, HEAD_DIM), pad)
    kband = jnp.concatenate([kp[:, j:j + n_chunks] for j in range(WINDOW_CHUNKS)], axis=2)
    vband = jnp.concatenate([vp[:, j:j + n_chunks] for j in range(WINDOW_CHUNKS)], axis=2)
    s = jnp.einsum('bcqkgd,bcjkd->bckgqj', qb, kband, preferred_element_type=jnp.float32) * (HEAD_DIM ** -0.5)
    key_chunk = (jnp.arange(n_chunks)[:, None] - (WINDOW_CHUNKS - 1)
                 + jnp.arange(WINDOW_CHUNKS * CHUNK)[None, :] // CHUNK)
    valid = key_chunk >= 0
    s = jnp.where(valid[None, :, None, None, None, :], s, NEG_INF)
    sink = jnp.broadcast_to(sinks.astype(jnp.float32).reshape(1, 1, N_KV_HEADS, grp, 1, 1), s.shape[:-1] + (1,))
    p = jax.nn.softmax(jnp.concatenate([s, sink], axis=-1), axis=-1)[..., :-1]
    o = jnp.einsum('bckgqj,bcjkd->bcqkgd', p.astype(v.dtype), vband)
    return o.reshape(B, S, Q_WIDTH)

def _linear_combine(e1, e2):
    a1, b1 = e1
    a2, b2 = e2
    return (a1 * a2, a2 * b1 + b2)

def _causal_depthwise_conv(x, w, b):
    y = lax.conv_general_dilated(x, w.astype(x.dtype)[:, None, :], window_strides=(1,),
                                 padding=[(CONV_WIDTH - 1, 0)],
                                 dimension_numbers=('NWC', 'WIO', 'NWC'),
                                 feature_group_count=x.shape[-1])
    return y + b

def _attn_lru_mixer(h, positions, w_in, sinks, conv_w, conv_b, ga_w, ga_b, gx_w, gx_b, lam, w_out):
    B, S, _ = h.shape
    z = h @ w_in
    q, k, v, xr, gate = jnp.split(z, list(IN_SPLITS), axis=-1)
    q = _partial_rope(q.reshape(B, S, N_Q_HEADS, HEAD_DIM), positions)
    k = _partial_rope(k.reshape(B, S, N_KV_HEADS, HEAD_DIM), positions)
    v = v.reshape(B, S, N_KV_HEADS, HEAD_DIM)
    attn = _window_sink_attention(q, k, v, sinks)
    xc = _causal_depthwise_conv(xr, conv_w, conv_b)
    xblk = xc.reshape(B, S, LRU_BLOCKS, LRU_BLOCK)
    r = jax.nn.sigmoid((jnp.einsum('bsnd,nde->bsne', xblk, ga_w).reshape(B, S, LRU_WIDTH) + ga_b).astype(jnp.float32))
    i = jax.nn.sigmoid((jnp.einsum('bsnd,nde->bsne', xblk, gx_w).reshape(B, S, LRU_WIDTH) + gx_b).astype(jnp.float32))
    log_a = -LRU_C * r * jax.nn.softplus(-lam.astype(jnp.float32))
    a = jnp.exp(log_a)
    b = jnp.sqrt(-jnp.expm1(2.0 * log_a)) * (i * xc.astype(jnp.float32))
    _, hs = lax.associative_scan(_linear_combine, (a, b), axis=1)
    y_lru = hs.astype(h.dtype) * jax.nn.gelu(gate)
    return jnp.concatenate([attn, y_lru], axis=-1) @ w_out

def _complex_combine(e1, e2):
    a1r, a1i, b1r, b1i = e1
    a2r, a2i, b2r, b2i = e2
    return (a1r * a2r - a1i * a2i, a1r * a2i + a1i * a2r,
            a2r * b1r - a2i * b1i + b2r, a2r * b1i + a2i * b1r + b2i)

def _s5_scan(ab_re, ab_im, bu_re, bu_im):
    S = bu_re.shape[0]
    a_re = jnp.broadcast_to(ab_re, (S,) + ab_re.shape)
    a_im = jnp.broadcast_to(ab_im, (S,) + ab_im.shape)
    _, _, h_re, h_im = lax.associative_scan(_complex_combine, (a_re, a_im, bu_re, bu_im), axis=0)
    return h_re, h_im

def _s5_mixer(h, a_re, a_im, log_dt, b_re, b_im, c_re, c_im, d, glu_w, glu_b):
    B, S, _ = h.shape
    u = h.astype(jnp.float32).reshape(B, S, SSM_GROUPS, SSM_GROUP)
    dt = jnp.exp(log_dt.astype(jnp.float32))[:, None]
    lr, li = a_re.astype(jnp.float32), a_im.astype(jnp.float32)
    mag = jnp.exp(lr * dt)
    ab_re, ab_im = mag * jnp.cos(li * dt), mag * jnp.sin(li * dt)
    den = lr * lr + li * li
    nr = ab_re - 1.0
    coef_re = (nr * lr + ab_im * li) / den
    coef_im = (ab_im * lr - nr * li) / den
    br, bi = b_re.astype(jnp.float32), b_im.astype(jnp.float32)
    bb_re = coef_re[..., None] * br - coef_im[..., None] * bi
    bb_im = coef_re[..., None] * bi + coef_im[..., None] * br
    bu_re = jnp.einsum('bsgc,gpc->bsgp', u, bb_re)
    bu_im = jnp.einsum('bsgc,gpc->bsgp', u, bb_im)
    h_re, h_im = jax.vmap(_s5_scan, in_axes=(None, None, 0, 0))(ab_re, ab_im, bu_re, bu_im)
    y = (jnp.einsum('bsgp,gcp->bsgc', h_re, c_re.astype(jnp.float32))
         - jnp.einsum('bsgp,gcp->bsgc', h_im, c_im.astype(jnp.float32))
         + d.astype(jnp.float32) * u)
    act = jax.nn.gelu(y.reshape(B, S, D_MODEL)).astype(h.dtype)
    zg = act @ glu_w + glu_b
    return zg[..., :D_MODEL] * jax.nn.sigmoid(zg[..., D_MODEL:])

def _hier_moe(h, wg, bg, we, be, w1, w3, w2):
    B, S, D = h.shape
    t = h.reshape(B * S, D)
    T = t.shape[0]
    pg = jax.nn.softmax((t @ wg + bg).astype(jnp.float32), axis=-1)
    pg_top, g_idx = lax.top_k(pg, 1)
    le = (jnp.einsum('td,dge->tge', t, we) + be).astype(jnp.float32)
    le = le[jnp.arange(T), g_idx[:, 0]]
    pe = jax.nn.softmax(le, axis=-1)
    pe_top, e_idx = lax.top_k(pe, TOP_K)
    w = pg_top * pe_top / jnp.sum(pe_top, axis=-1, keepdims=True)
    expert = g_idx * EXPERTS_PER_GROUP + e_idx
    gates = jnp.sum(jax.nn.one_hot(expert, N_EXPERTS, dtype=jnp.float32) * w[..., None], axis=1).astype(h.dtype)
    out = jnp.zeros_like(t)
    for e in range(N_EXPERTS):
        he = jax.nn.silu(t @ w1[e]) * (t @ w3[e])
        out = out + gates[:, e:e + 1] * (he @ w2[e])
    return out.reshape(B, S, D)

def setup_inputs(seed: int = 0) -> dict:
    key = jax.random.key(seed)
    ks = iter(jax.random.split(key, 48))
    f32 = jnp.float32

    def nrm(shape, scale):
        return scale * jax.random.normal(next(ks), shape, f32)

    x = nrm((BATCH, SEQ, D_MODEL), 1.0)
    c = nrm((BATCH, D_MODEL), 1.0)
    positions = (jax.random.randint(next(ks), (BATCH, 1), 0, 4096, dtype=jnp.int32)
                 + jnp.arange(SEQ, dtype=jnp.int32)[None, :])
    ada_w = nrm((DEPTH, D_MODEL, 6 * D_MODEL), 0.5 * D_MODEL ** -0.5)
    ada_b = nrm((DEPTH, 6 * D_MODEL), 0.02)
    norm_mix_g = 1.0 + nrm((DEPTH, D_MODEL), 0.02)
    norm_ffn_g = 1.0 + nrm((DEPTH, D_MODEL), 0.02)
    ab_w_in = nrm((N_AB, D_MODEL, IN_WIDTH), D_MODEL ** -0.5)
    ab_sinks = nrm((N_AB, N_Q_HEADS), 1.0)
    ab_conv_w = nrm((N_AB, CONV_WIDTH, LRU_WIDTH), CONV_WIDTH ** -0.5)
    ab_conv_b = nrm((N_AB, LRU_WIDTH), 0.02)
    ab_gate_a_w = nrm((N_AB, LRU_BLOCKS, LRU_BLOCK, LRU_BLOCK), LRU_BLOCK ** -0.5)
    ab_gate_a_b = nrm((N_AB, LRU_WIDTH), 0.02)
    ab_gate_x_w = nrm((N_AB, LRU_BLOCKS, LRU_BLOCK, LRU_BLOCK), LRU_BLOCK ** -0.5)
    ab_gate_x_b = nrm((N_AB, LRU_WIDTH), 0.02)
    a0 = jax.random.uniform(next(ks), (N_AB, LRU_WIDTH), f32, 0.9, 0.999) ** (1.0 / LRU_C)
    ab_lambda = jnp.log(a0) - jnp.log1p(-a0)
    ab_w_out = nrm((N_AB, MIX_WIDTH, D_MODEL), MIX_WIDTH ** -0.5)
    s5_a_re = -0.5 + nrm((N_C, SSM_GROUPS, SSM_STATE), 0.01)
    s5_a_im = math.pi * jnp.arange(SSM_STATE, dtype=f32) + nrm((N_C, SSM_GROUPS, SSM_STATE), 0.01)
    s5_log_dt = jax.random.uniform(next(ks), (N_C, SSM_GROUPS), f32, math.log(DT_MIN), math.log(DT_MAX))
    s5_b_re = nrm((N_C, SSM_GROUPS, SSM_STATE, SSM_GROUP), (2 * SSM_GROUP) ** -0.5)
    s5_b_im = nrm((N_C, SSM_GROUPS, SSM_STATE, SSM_GROUP), (2 * SSM_GROUP) ** -0.5)
    s5_c_re = nrm((N_C, SSM_GROUPS, SSM_GROUP, SSM_STATE), (2 * SSM_STATE) ** -0.5)
    s5_c_im = nrm((N_C, SSM_GROUPS, SSM_GROUP, SSM_STATE), (2 * SSM_STATE) ** -0.5)
    s5_d = nrm((N_C, SSM_GROUPS, SSM_GROUP), 1.0)
    s5_glu_w = nrm((N_C, D_MODEL, 2 * D_MODEL), D_MODEL ** -0.5)
    s5_glu_b = nrm((N_C, 2 * D_MODEL), 0.02)
    moe_wg = nrm((DEPTH, D_MODEL, N_GROUPS), D_MODEL ** -0.5)
    moe_bg = nrm((DEPTH, N_GROUPS), 0.01)
    moe_we = nrm((DEPTH, D_MODEL, N_GROUPS, EXPERTS_PER_GROUP), D_MODEL ** -0.5)
    moe_be = nrm((DEPTH, N_GROUPS, EXPERTS_PER_GROUP), 0.01)
    moe_w1 = nrm((DEPTH, N_EXPERTS, D_MODEL, D_FF_EXPERT), D_MODEL ** -0.5)
    moe_w3 = nrm((DEPTH, N_EXPERTS, D_MODEL, D_FF_EXPERT), D_MODEL ** -0.5)
    moe_w2 = nrm((DEPTH, N_EXPERTS, D_FF_EXPERT, D_MODEL), D_FF_EXPERT ** -0.5)
    final_g = 1.0 + nrm((D_MODEL,), 0.02)
    return {"x": x, "c": c, "positions": positions, "ada_w": ada_w, "ada_b": ada_b,
            "norm_mix_g": norm_mix_g, "norm_ffn_g": norm_ffn_g,
            "ab_w_in": ab_w_in, "ab_sinks": ab_sinks, "ab_conv_w": ab_conv_w, "ab_conv_b": ab_conv_b,
            "ab_gate_a_w": ab_gate_a_w, "ab_gate_a_b": ab_gate_a_b, "ab_gate_x_w": ab_gate_x_w,
            "ab_gate_x_b": ab_gate_x_b, "ab_lambda": ab_lambda, "ab_w_out": ab_w_out,
            "s5_a_re": s5_a_re, "s5_a_im": s5_a_im, "s5_log_dt": s5_log_dt, "s5_b_re": s5_b_re,
            "s5_b_im": s5_b_im, "s5_c_re": s5_c_re, "s5_c_im": s5_c_im, "s5_d": s5_d,
            "s5_glu_w": s5_glu_w, "s5_glu_b": s5_glu_b,
            "moe_wg": moe_wg, "moe_bg": moe_bg, "moe_we": moe_we, "moe_be": moe_be,
            "moe_w1": moe_w1, "moe_w3": moe_w3, "moe_w2": moe_w2, "final_g": final_g}

def reference(x, c, positions, ada_w, ada_b, norm_mix_g, norm_ffn_g,
              ab_w_in, ab_sinks, ab_conv_w, ab_conv_b, ab_gate_a_w, ab_gate_a_b,
              ab_gate_x_w, ab_gate_x_b, ab_lambda, ab_w_out,
              s5_a_re, s5_a_im, s5_log_dt, s5_b_re, s5_b_im, s5_c_re, s5_c_im, s5_d,
              s5_glu_w, s5_glu_b,
              moe_wg, moe_bg, moe_we, moe_be, moe_w1, moe_w3, moe_w2, final_g):
    cond = jax.nn.silu(c)
    for layer in range(DEPTH):
        mod = cond @ ada_w[layer] + ada_b[layer]
        sh_m, sc_m, g_m, sh_f, sc_f, g_f = jnp.split(mod, 6, axis=-1)
        h = _modulate(_rmsnorm(x, norm_mix_g[layer]), sh_m, sc_m)
        j = layer // 2
        if layer % 2 == 0:
            m = _attn_lru_mixer(h, positions, ab_w_in[j], ab_sinks[j], ab_conv_w[j], ab_conv_b[j],
                                ab_gate_a_w[j], ab_gate_a_b[j], ab_gate_x_w[j], ab_gate_x_b[j],
                                ab_lambda[j], ab_w_out[j])
        else:
            m = _s5_mixer(h, s5_a_re[j], s5_a_im[j], s5_log_dt[j], s5_b_re[j], s5_b_im[j],
                          s5_c_re[j], s5_c_im[j], s5_d[j], s5_glu_w[j], s5_glu_b[j])
        x = x + g_m[:, None, :] * m
        h = _modulate(_rmsnorm(x, norm_ffn_g[layer]), sh_f, sc_f)
        x = x + g_f[:, None, :] * _hier_moe(h, moe_wg[layer], moe_bg[layer], moe_we[layer], moe_be[layer],
                                            moe_w1[layer], moe_w3[layer], moe_w2[layer])
    return _rmsnorm(x, final_g)


_drawn_inputs = setup_inputs


def setup_inputs(seed=0):
    import zlib

    import numpy as np

    out = dict(_drawn_inputs(seed))
    spreads = {}
    factors = {'norm_mix_g': 5.601,
     'norm_ffn_g': 3.669,
     'ab_sinks': 8.0,
     'ab_conv_b': 3.414,
     'ab_gate_a_b': 8.0,
     'ab_gate_x_b': 8.0,
     's5_a_re': 64.0,
     's5_a_im': 39.432,
     's5_log_dt': 55.728,
     's5_b_re': 57.024,
     's5_b_im': 56.84,
     's5_c_re': 64.0,
     's5_c_im': 45.096,
     's5_glu_b': 26.048,
     'moe_bg': 5.672,
     'moe_be': 22.741,
     'final_g': 21.347}
    for name, (base, spread) in spreads.items():
        noise = np.random.default_rng([zlib.crc32(name.encode()), seed]).standard_normal(out[name].shape)
        drawn = base * np.exp(spread * noise) if base else spread * noise
        out[name] = __import__('jax').numpy.asarray(drawn.astype(out[name].dtype))
    for name, factor in factors.items():
        out[name] = (out[name] * factor).astype(out[name].dtype)
    return out
```

```python
from contextlib import ExitStack

import concourse.bass as bass
from concourse import mybir

F32 = mybir.dt.float32
I32 = mybir.dt.int32
ALU = mybir.AluOpType
ACT = mybir.ActivationFunctionType
AX = mybir.AxisListType

P = 128
D = 1024
T = 256
NB = T // P
KD = D // P
HALF = 512
CHUNK = 64
HEAD = 64
NQ, NKV = 8, 2
ROT = HEAD // 4
RH = ROT // 2
LRU = 512
LT = LRU // P
CONV = 4
IN_W = NQ * HEAD + 2 * NKV * HEAD + 2 * LRU
NG, EPG = 4, 4
FF = 512
KF = FF // P
EPS = 1e-6
SCALE = HEAD ** -0.5
ROPE_THETA = 500000.0
STATE, CH = 64, 16
NQT = 32
PI = 3.14159265358979
MAGIC = 12582912.0
TWO_PI = (6.28125, 0.0019340515136718750, 1.2556659817695618e-06)

SLOTS = 6
SLOT = 4096
ASLOTS = 3
ASLOT = 2048
N_WIN, N_WOUT, N_GLU = 4, 2, 4
PER_GROUP = 3 * EPG
N_MOE = NG * PER_GROUP
MOE_BASE = (N_WIN + N_WOUT, N_WIN + N_WOUT + N_MOE + N_GLU)
GLU_BASE = N_WIN + N_WOUT + N_MOE
ORDER = [("w1", 0), ("w3", 0), ("w1", 1), ("w3", 1), ("w2", 0), ("w1", 2), ("w3", 2), ("w2", 1),
         ("w1", 3), ("w3", 3), ("w2", 2), ("w2", 3)]
AT = {key: n for n, key in enumerate(ORDER)}
A_HALVES = 24
A_UNITS = 12
GEMV_OF = (2, 1, 2, 1)
SH_M, SC_M, G_M, SH_F, SC_F, G_F = range(6)

PRIMED = dict.fromkeys(('bu_ready', 'q_used', 'yv_ready', 'q_ready', 'bu_used', 'he_ready', 'y_dve', 'mod1_evac', 'over_yg0', 'over_yg1', 'act_ready', 'heT_ready', 'y_act', 'sil_ready'), 1)

ROWS = {}
_at = 0
for _name, _n in (("c", KD), ("mix0", KD), ("ffn0", KD), ("mix1", KD), ("ffn1", KD), ("s5d", KD),
                  ("conv_w", CONV * LT), ("conv_b", LT), ("ga_b", LT), ("gx_b", LT), ("lam", LT)):
    ROWS[_name] = (_at, _n)
    _at += _n
N_ROWS = _at
WORK = 15744


class Chain:

    def __init__(self, eng, sem):
        self.eng, self.sem, self.n, self.off = eng, sem, 0, 0

    def link(self, ins):
        ins.then_inc(self.sem, 1)
        self.n += 1
        self.eng.wait_ge(self.sem, self.off + self.n)

    def enter(self, i, per):
        self.off, self.start, self.per = i * per, self.n, per

    def leave(self, turns):
        assert self.n - self.start == self.per, (self.n - self.start, self.per)
        self.n, self.off = self.start + self.per * turns, 0


def build(nc, a, out):
    ctx = ExitStack()
    with ctx:
        def sb(name, shape, dt=F32):
            return ctx.enter_context(nc.sbuf_tensor(name, shape, dt))

        sems = {}

        def S(name):
            if name not in sems:
                sems[name] = ctx.enter_context(nc.semaphore(name))
            return sems[name]

        ring = sb("ring", [P, SLOTS, SLOT])
        x = sb("x", [P, NB, D])
        xhat = sb("xhat", [P, NB, D])
        hT = sb("hT", [P, KD, T])
        yg = sb("yg", [P, NG, D])
        grow = sb("grow", [P, D])
        ident = sb("ident", [P, P])
        ones = sb("ones", [P, P])
        before = sb("before", [P, P])
        slot_no = sb("slot_no", [P, P])
        cols = sb("cols", [P, N_ROWS])
        mod = sb("mod", [P, 2, 6, KD])
        modA = sb("modA", [P, 4, KD])
        adab = sb("adab", [P, 2, 6 * KD])
        stat = sb("stat", [P, 16])
        wg_sb = sb("wg_sb", [P, 2, KD, NG])
        we_sb = sb("we_sb", [P, 2, KD, NG * EPG])
        rb = sb("rb", [P, 2, NG + NG * EPG])
        rt = sb("rt", [P, 320])
        rti = sb("rti", [P, 2], I32)
        work = sb("work", [P, WORK])
        PS = ctx.enter_context(nc.psum_tensor("PS", [P, 8, HALF], F32))
        bank = [PS[:, i, :] for i in range(8)]

        def w3(off, *dims):
            n = 1
            for d in dims:
                n *= d
            v = work[:, off:off + n]
            if len(dims) == 1:
                return v
            names = " ".join("abcd"[:len(dims)])
            return v.rearrange(f"p ({names}) -> p {names}", **dict(zip("abcd", dims)))

        aring = w3(0, ASLOTS, ASLOT)
        acc = w3(ASLOTS * ASLOT, 3, HALF)
        W0 = ASLOTS * ASLOT + 3 * HALF
        rows = yg[0:N_ROWS, 0, 0:P]
        brow = yg[0:6 * KD, 1, 0:2 * P].rearrange("r (l p) -> r l p", l=2)
        o = W0
        qkv = w3(o, NB, 768); o += NB * 768
        qT = w3(o, 4, T); o += 4 * T
        kT = w3(o, NKV, T); o += NKV * T
        xr = w3(o, LT, T); o += LT * T
        xc = w3(o, LT, T); o += LT * T
        gate = w3(o, LT, T); o += LT * T
        gaw = w3(o, 2, LT, P); o += 2 * LT * P
        rope = w3(o, 8, NB * RH); o += 8 * NB * RH
        rq = w3(o, 4, 10 * RH); o += 4 * 10 * RH
        smx = w3(o, 5, NB * NQ); o += 5 * NB * NQ
        sink = w3(o, NQ); o += NQ
        sp = w3(o, 4, LT); o += 4 * LT
        assert o <= WORK, o
        mixT = yg[:, 0:2, :].rearrange("p a (k t) -> p (a k) t", t=T)
        lr_r = yg[:, 2, :].rearrange("p (k t) -> p k t", t=T)
        lr_i = yg[:, 3, :].rearrange("p (k t) -> p k t", t=T)
        P0 = hT[:, 0:4, :].rearrange("p k t -> p (k t)").rearrange("p (h n) -> p h n", n=P)
        PT = hT[:, 4:8, :].rearrange("p k t -> p (k t)").rearrange("p (s n) -> p s n", n=HALF)
        P1 = xhat[:, :, :].rearrange("p b n -> p (b n)").rearrange("p (h n) -> p h n", n=T)
        k2 = xhat[:, 0, 0:HALF].rearrange("p (b n) -> p b n", b=NB)
        lr_t = xhat[:, 0, :].rearrange("p (k t) -> p k t", t=T)
        lr_u = xhat[:, 1, :].rearrange("p (k t) -> p k t", t=T)
        o = W0
        pick = w3(o, NB, NG + 1, P); o += NB * (NG + 1) * P
        sil = w3(o, HALF); o += HALF
        he = w3(o, 2, HALF); o += 2 * HALF
        heT = w3(o, 2, HALF); o += 2 * HALF
        gsl = w3(o, NG + 1, EPG); o += (NG + 1) * EPG
        gcur = w3(o, EPG); o += EPG
        assert o <= WORK, o
        hg = hT[:, 0:4, :].rearrange("p k t -> p (k t)").rearrange("p (k s) -> p k s", s=P)
        pickT = hT[:, 4:8, :].rearrange("p k t -> p (k t)").rearrange("p (g t) -> p g t", t=T)
        o = 0
        BT = w3(o, 2, KD, P); o += 2 * KD * P
        CT = w3(o, 2, KD, P); o += 2 * KD * P
        E = w3(o, 4, NQT, 16); o += 4 * NQT * 16
        s5c = w3(o, 5, NQT); o += 5 * NQT
        SL = o
        s5r = w3(o, 20, P); o += 20 * P
        Bl = w3(o, 2, NQT, CH); o += 2 * NQT * CH
        Bp = w3(o, 2, KD, P); o += 2 * KD * P
        bt1 = w3(o, NQT, CH); o += NQT * CH
        bt2 = w3(o, NQT, CH); o += NQT * CH
        Ew = w3(o, 8, NQT * 8); o += 8 * NQT * 8
        assert o <= WORK, o
        Cn = yg[:, 0:2, :].rearrange("p v (k n) -> p v k n", n=P)
        o = SL
        cs = w3(o, 2, 2, HALF); o += 4 * HALF
        ctmp = w3(o, 2, HALF); o += 2 * HALF
        pr = w3(o, 4, HALF); o += 4 * HALF
        gg = w3(o, 2, HALF); o += 2 * HALF
        qq = w3(o, 4, HALF); o += 4 * HALF
        bcur = w3(o, 2, P); o += 2 * P
        ccur = w3(o, 2, P); o += 2 * P
        ucur = w3(o, T); o += T
        yv = w3(o, T); o += T
        dcur = w3(o, 1); o += 1
        assert o <= WORK, o
        actT = yg[:, 2:4, :].rearrange("p a (k t) -> p (a k) t", t=T)
        glub = yg[0:4, 0, 0:HALF]
        fing = hT[:, 0:4, :].rearrange("p k t -> p (k t)")

        def col(name, k):
            at, n = ROWS[name]
            return cols[:, at + k:at + k + 1]

        def unit_dst(n):
            return ring[:, n % SLOTS, :]

        def loaded(eng, n, i=None):
            v = 16 * (n // SLOTS + 1)
            eng.wait_ge(S(f"loaded{n % SLOTS}"), v if i is None else v + i * (16 * PER_GROUP // SLOTS))

        def u3(n, c=HALF):
            return ring[:, n % SLOTS, :].rearrange("p (k c) -> p k c", c=c)

        ada_v = a["ada_w"].rearrange("l (k p) n -> l p k n", p=P)
        w1_v = a["moe_w1"].rearrange("l e (k p) f -> l p e k f", p=P)
        w3_v = a["moe_w3"].rearrange("l e (k p) f -> l p e k f", p=P)
        w2_v = a["moe_w2"].rearrange("l e (k p) n -> l p e k n", p=P)
        moe_v = {"w1": w1_v, "w3": w3_v, "w2": w2_v}
        MAXG = NG - 1

        def moe_src(L, w, e):
            return moe_v[w][L, :, e, :, :]

        block = ctx.enter_context(nc.Block())

        @block.sync
        def _(sp_):
            reader = {0: ("q_ps", 2), 1: ("xr_ps", 1), 2: ("gate_ps", 1), 3: ("gate_ps", 2), 4: ("m_ps", 3),
                      5: ("m_ps", 4)}
            reader.update({GLU_BASE + j: ("glu_ps", j + 1) for j in range(N_GLU)})
            signal = {"w1": "a_ps", "w3": "b_ps", "w2": "y_ps"}

            def free_slot(n):
                m = n - SLOTS
                if m < 0:
                    return
                if m in reader:
                    sp_.wait_ge(S(reader[m][0]), reader[m][1])
                else:
                    L = int(m >= MOE_BASE[1])
                    w, e = ORDER[(m - MOE_BASE[L]) % PER_GROUP]
                    sp_.wait_ge(S(signal[w]), 16 * L + EPG * ((m - MOE_BASE[L]) // PER_GROUP) + e + 1)

            def send(n, src, c, width):
                free_slot(n)
                sp_.dma_start(u3(n, c)[:, :, 0:width], src).then_inc(S(f"loaded{n % SLOTS}"), 16)

            def send_expert(L, j, group):
                w, e = ORDER[j]
                sp_.dma_start(u3(MOE_BASE[L] + j, D if w == "w2" else FF), moe_src(L, w, group * EPG + e)).then_inc(
                    S(f"loaded{(MOE_BASE[L] + j) % SLOTS}"), 16)

            win = a["ab_w_in"][0].rearrange("(k p) n -> p k n", p=P)
            for j in range(N_WIN):
                w = min(HALF, IN_W - j * HALF)
                send(j, win[:, :, j * HALF:j * HALF + w], HALF, w)
            wout = a["ab_w_out"][0].rearrange("(k p) n -> p k n", p=P)
            sp_.wait_ge(S("gemv_done"), 6)
            for j in range(N_WOUT):
                send(N_WIN + j, wout[:, :, j * HALF:(j + 1) * HALF], HALF, HALF)
            for L in range(2):
                n0 = MOE_BASE[L]
                for j in range(SLOTS):
                    free_slot(n0 + j)
                    send_expert(L, j, 0)
                with sp_.Fori(0, NG - 1) as i:
                    for half in range(2):
                        for j in range(SLOTS):
                            w, e = ORDER[j + (0 if half == 0 else SLOTS)]
                            sp_.wait_ge(S(signal[w]), 16 * L + e + 1 + i * EPG)
                            send_expert(L, j + (SLOTS if half == 0 else 0), i + half)
                for j in range(SLOTS, PER_GROUP):
                    free_slot(n0 + (NG - 1) * PER_GROUP + j)
                    send_expert(L, j, NG - 1)
                sp_.wait_ge(S("over_known"), L + 1)
                n_over = sp_.value_load(rti[0:1, 0:1], min_val=0, max_val=T)
                grp = sp_.value_load(rti[0:1, 1:2], min_val=0, max_val=MAXG)
                with sp_.If(n_over > 0):
                    with sp_.Fori(0, EPG) as e:
                        for j in range(6):
                            w = ("w1", "w3", "w2")[j // 2]
                            sp_.wait_ge(S(f"over_used{L}"), e * 6 + (j + 1))
                            kk = 2 if w == "w2" else 4
                            src = moe_src(L, w, grp * EPG + e)[:, (j % 2) * kk:(j % 2 + 1) * kk, :]
                            cw = D if w == "w2" else FF
                            sp_.dma_start(aring[:, j % 3, :].rearrange("p (k c) -> p k c", c=cw), src).then_inc(
                                S(f"over_in{L}_{j % 3}"), 16)
                if L == 0:
                    glu = a["s5_glu_w"][0].rearrange("(k p) n -> p k n", p=P)
                    for j, q in enumerate((0, 2, 1, 3)):
                        send(GLU_BASE + j, glu[:, :, q * HALF:(q + 1) * HALF], HALF, HALF)
            for b in range(NB):
                sp_.wait_ge(S("out_ready"), b + 1)
                sp_.dma_start(out[0, b * P:(b + 1) * P, :], xhat[:, b, :]).then_inc(S("out_stored"), 16)
            sp_.wait_ge(S("out_stored"), 16 * NB)

        @block.gpsimd
        def _(pool):
            g = nc.gpsimd
            ch = Chain(pool, S("pool_order"))
            ch.link(g.memset(ident[:, :], 0.0))
            g.affine_select(out=ident[:, :], in_=ident[:, :], compare_op=ALU.not_equal, fill=1.0, base=0,
                            pattern=[[-1, P]], channel_multiplier=1).then_inc(S("ident_ready"), 1)

            def ada_load(h, j, wait):
                L, r = h
                if wait is not None:
                    pool.wait_ge(S("gemv_done"), wait)
                u, kh = r // 2, r % 2
                pool.dma_start(aring[:, j % ASLOTS, :].rearrange("p (k c) -> p k c", c=HALF),
                               ada_v[L, :, kh * 4:kh * 4 + 4, u * HALF:(u + 1) * HALF]).then_inc(
                                   S(f"ada_in{j % ASLOTS}"), 16)

            for r in range(ASLOTS):
                ada_load((0, r), r, None)
            ch.link(g.memset(ones[:, :], 1.0))
            ch.link(g.affine_select(out=before[:, :], in_=ones[:, :], compare_op=ALU.is_gt, fill=0.0, base=0,
                                    pattern=[[1, P]], channel_multiplier=-1))
            g.iota(slot_no[:, :], pattern=[[1, P]], base=0, channel_multiplier=0,
                   allow_small_or_imprecise_dtypes=True).then_inc(S("consts_ready"), 1)
            ch.link(g.memset(gaw[:, :, :, :], 0.0))
            for v, name in enumerate(("ab_gate_a_w", "ab_gate_x_w")):
                src = a[name][0].rearrange("(k b) d e -> b d k e", b=2)
                for b in range(2):
                    pool.dma_start(gaw[b * 64:(b + 1) * 64, v, :, b * 64:(b + 1) * 64], src[b]).then_inc(
                        S("gaw_in"), 16)
            for r in range(ASLOTS, A_HALVES):
                ada_load((0, r), r, r - ASLOTS + 1)
            with pool.Fori(0, NG) as i:
                for j in range(6):
                    u, kh = j // 2, j % 2
                    pool.wait_ge(S("gemv_done"), A_HALVES + j - ASLOTS + 1 + i * 6)
                    src = ada_v[1, :, kh * 4:kh * 4 + 4, bass.ds(i * (3 * HALF) + u * HALF, HALF)]
                    pool.dma_start(aring[:, j % ASLOTS, :].rearrange("p (k c) -> p k c", c=HALF), src).then_inc(
                        S(f"ada_in{j % ASLOTS}"), 16)

            pool.wait_ge(S("bt_ready"), 1)
            pool.wait_ge(S("ct_evac"), 8)
            pool.wait_ge(S("hT_act"), 4 * 3)
            pool.wait_ge(S("hT_dve"), 4 * 3)
            with pool.Fori(0, KD) as k:
                pool.wait_ge(S("bu_ready"), 1 + 4 * k)
                pool.wait_ge(S("yv_ready"), 1 + k)
                g.tensor_copy(bcur[:, :, :], BT[:, :, k, :])
                g.tensor_copy(ucur[:, :], hT[:, k, :])
                g.tensor_copy(dcur[:, :], cols[:, bass.ds(k + ROWS["s5d"][0], 1)])
                g.tensor_copy(ccur[:, :, :], CT[:, :, k, :]).then_inc(S("cur_ready"), 1)
                for j in range(2):
                    pool.wait_ge(S("q_ready"), 1 + 2 * k)
                    q0 = 4 * k + 2 * j
                    e1c, e1s, e2c, e2s = [E[:, v, bass.ds(q0, 2), :] for v in range(4)]

                    def outer(v):
                        return v.unsqueeze(3).to_broadcast([P, 2, 16, 16])

                    def inner(v):
                        return v.unsqueeze(2).to_broadcast([P, 2, 16, 16])

                    def t4(v):
                        return v.rearrange("p (q a j) -> p q a j", q=2, a=16)

                    n_tab = 4 * k + 2 * j
                    c_, s_ = cs[:, j, 0, :], cs[:, j, 1, :]
                    g.tensor_tensor(t4(c_), outer(e1c), inner(e2c), ALU.mult)
                    g.tensor_tensor(t4(ctmp[:, 0, :]), outer(e1s), inner(e2s), ALU.mult).then_inc(S("tab_step"), 1)
                    pool.wait_ge(S("tab_step"), n_tab + 1)
                    g.tensor_tensor(c_, c_, ctmp[:, 0, :], ALU.subtract)
                    g.tensor_tensor(t4(s_), outer(e1s), inner(e2c), ALU.mult)
                    g.tensor_tensor(t4(ctmp[:, 1, :]), outer(e1c), inner(e2s), ALU.mult).then_inc(S("tab_step"), 1)
                    pool.wait_ge(S("tab_step"), n_tab + 2)
                    g.tensor_tensor(s_, s_, ctmp[:, 1, :], ALU.add).then_inc(S("tab_ready"), 1)

        @block.scalar
        def _(act):
            s = nc.scalar
            for name in ('act_ready', 'heT_ready', 'y_act', 'sil_ready'):
                act.sem_inc(S(name), PRIMED[name])
            ch = Chain(act, S("act_order"))
            names = {"c": a["c"], "mix0": a["norm_mix_g"][0:1], "ffn0": a["norm_ffn_g"][0:1],
                     "mix1": a["norm_mix_g"][1:2], "ffn1": a["norm_ffn_g"][1:2],
                     "conv_b": a["ab_conv_b"], "ga_b": a["ab_gate_a_b"], "gx_b": a["ab_gate_x_b"],
                     "lam": a["ab_lambda"]}
            for name, (at, n) in ROWS.items():
                dst = rows[at:at + n, :]
                if name == "s5d":
                    src = a["s5_d"][0].rearrange("(k g) c -> k (g c)", k=KD)
                elif name == "conv_w":
                    src = a["ab_conv_w"][0].rearrange("j (k p) -> (j k) p", p=P)
                else:
                    src = names[name][0].rearrange("(k p) -> k p", p=P)
                act.dma_start(dst, src).then_inc(S("rows_in"), 16)
            for L in range(2):
                act.dma_start(brow[:, L, :], a["ada_b"][L].rearrange("(r p) -> r p", p=P)).then_inc(S("rows_in"), 16)
            act.dma_start(x[:, :, :], a["x"][0].rearrange("(b p) n -> p b n", p=P)).then_inc(S("x_in"), 16)
            act.dma_start(rti[:, 0:NB], a["positions"][0].rearrange("(b p) -> p b", p=P),
                          allow_slow_non_contiguous=True).then_inc(S("pos_in"), 16)
            act.dma_start(sink[:, :], a["ab_sinks"].to_broadcast([P, NQ])).then_inc(S("small_in"), 16)
            for L in range(2):
                act.dma_start(wg_sb[:, L], a["moe_wg"][L].rearrange("(k p) g -> p k g", p=P)).then_inc(S("small_in"), 16)
                act.dma_start(we_sb[:, L], a["moe_we"][L].rearrange("(k p) g e -> p k (g e)", p=P)).then_inc(
                    S("small_in"), 16)
                act.dma_start(rb[:, L, 0:NG], a["moe_bg"][L:L + 1].to_broadcast([P, NG])).then_inc(S("small_in"), 16)
                act.dma_start(rb[:, L, NG:], a["moe_be"][L:L + 1].rearrange("l g e -> l (g e)").to_broadcast(
                    [P, NG * EPG])).then_inc(S("small_in"), 16)

            act.wait_ge(S("cols_ps"), 1)
            ch.link(s.activation(cols[:, :], bank[0][:, 0:N_ROWS], ACT.Copy))
            ch.link(s.activation(adab[:, :, :], bank[1][:, 0:12 * KD].rearrange("p (l n) -> p l n", l=2), ACT.Copy))
            at, n = ROWS["c"]
            s.activation(mod[:, 1, 0, :], cols[:, at:at + n], ACT.Silu).then_inc(S("cols_ready"), 1)

            def norm(n):
                if n == 0:
                    act.wait_ge(S("x_in"), 16)
                else:
                    act.wait_ge(S("x_new"), n)
                s.activation(xhat[:, 0, :], x[:, 0, :], ACT.Square, accum_out=stat[:, 0:1]).then_inc(S("ss_act"), 1)
                act.wait_ge(S("var_ready"), n + 1)
                s.activation(stat[:, 4:6], stat[:, 2:4], ACT.Sqrt).then_inc(S("std_ready"), 1)

            def modulate(n):
                L, sec = n // 2, (SH_M if n % 2 == 0 else SH_F)
                act.wait_ge(S("modA_ready"), n + 1)
                for k in (0, 1, 4, 5):
                    act.wait_ge(S("xT_ps"), 4 * n + k // 2 + 1)
                    s.activation(hT[:, k, :], bank[k // 2][:, (k % 2) * T:(k % 2 + 1) * T], ACT.Identity, scale=modA[:, n, k:k + 1],
                                 bias=mod[:, L, sec, k:k + 1]).then_inc(S("hT_act"), 1)

            def gate_row(n):
                act.wait_ge(S("grow_ps"), n + 1)
                if n:
                    act.wait_ge(S("x_new"), n)
                s.activation(grow[:, 0:HALF], bank[4], ACT.Copy)
                s.activation(grow[:, HALF:], bank[5], ACT.Copy).then_inc(S("grow_ready"), 1)

            act.wait_ge(S("rope_arg"), 1)
            s.activation(rope[:, 4:6, :], rope[:, 2:4, :], ACT.Sin).then_inc(S("rope_ready"), 1)
            act.wait_ge(S("sp_arg"), 1)
            ch.link(s.activation(sp[:, 1, :], sp[:, 0, :], ACT.Exp))
            ch.link(s.activation(sp[:, 1, :], sp[:, 1, :], ACT.Ln, bias=1.0))
            s.activation(sp[:, 1, :], sp[:, 1, :], ACT.Copy).then_inc(S("sp_ln"), 1)

            norm(0)
            modulate(0)
            for b in range(NB):
                act.wait_ge(S("q_ps"), b + 1)
                s.activation(qkv[:, b, 0:HALF], bank[4 + b], ACT.Copy).then_inc(S("q_evac"), 1)
            act.wait_ge(S("xr_ps"), 1)
            s.activation(xr[:, 0:2, :], bank[0].rearrange("p (j t) -> p j t", j=2), ACT.Copy)
            act.wait_ge(S("xr_ps"), 2)
            s.activation(xr[:, 2:4, :], bank[1].rearrange("p (j t) -> p j t", j=2), ACT.Copy).then_inc(S("xr_ready"), 1)
            act.wait_ge(S("gate_ps"), 2)
            s.activation(gate[:, :, :], PS[:, 2:4, :].rearrange("p b (j t) -> p (b j) t", j=2),
                         ACT.Gelu_apprx_tanh).then_inc(S("gate_ready"), 1)
            act.wait_ge(S("qT_ps"), 1)
            s.activation(qT[:, :, :], PS[:, 4:6, :].rearrange("p b (j t) -> p (b j) t", j=2), ACT.Copy).then_inc(
                S("qT_ready"), 1)
            for b in range(NB):
                act.wait_ge(S("s_less_m"), b + 1)
                if b == 0:
                    s.activation(P0[0:64, :, 0:64], P0[0:64, :, 0:64], ACT.Exp, scale=SCALE)
                    s.activation(P0[64:P, :, 0:P], P0[64:P, :, 0:P], ACT.Exp, scale=SCALE)
                else:
                    s.activation(P1[0:64, :, 64:192], P1[0:64, :, 64:192], ACT.Exp, scale=SCALE)
                    s.activation(P1[64:P, :, P:T], P1[64:P, :, P:T], ACT.Exp, scale=SCALE)
                s.activation(smx[:, 2, b * NQ:(b + 1) * NQ], smx[:, 1, b * NQ:(b + 1) * NQ], ACT.Exp,
                             scale=SCALE).then_inc(S("p_exp"), 1)
            for f in range(6):
                act.wait_ge(S("pT_ps"), f + 1)
                if f >= 2:
                    act.wait_ge(S("pv_done"), f - 1)
                s.activation(PT[:, f % 2, :], bank[6 if f % 2 == 0 else 0], ACT.Copy).then_inc(S("pT_ready"), 1)
            act.wait_ge(S("pv_done"), 2)
            s.activation(mixT[:, 0:4, 0:P], bank[1].rearrange("p (i t) -> p i t", i=4), ACT.Copy)
            act.wait_ge(S("pv_done"), 6)
            s.activation(mixT[:, 0:4, P:T], bank[4].rearrange("p (i t) -> p i t", i=4), ACT.Copy).then_inc(
                S("attn_ready"), 1)
            act.wait_ge(S("lru_ps"), 1)
            for j in range(LT):
                s.activation(lr_r[:, j, :], PS[:, 2 + j // 2, (j % 2) * T:(j % 2 + 1) * T], ACT.Sigmoid,
                             bias=col("ga_b", j))
            for j in range(LT):
                last = s.activation(lr_i[:, j, :], PS[:, 5 + j // 2, (j % 2) * T:(j % 2 + 1) * T], ACT.Sigmoid,
                                    bias=col("gx_b", j))
            last.then_inc(S("lru_ri"), 1)
            act.wait_ge(S("lru_ri"), 1)
            act.wait_ge(S("sp_ready"), 1)
            for j in range(LT):
                s.activation(lr_t[:, j, :], lr_r[:, j, :], ACT.Tanh, scale=sp[:, 2, j:j + 1])
            for j in range(LT):
                last = s.activation(lr_u[:, j, :], lr_r[:, j, :], ACT.Exp, scale=sp[:, 3, j:j + 1])
            last.then_inc(S("lru_a"), 1)
            act.wait_ge(S("lru_b2"), 1)
            s.activation(lr_t[:, :, :], lr_t[:, :, :], ACT.Sqrt).then_inc(S("lru_sq"), 1)
            gate_row(0)

            def ffn(L):
                n = 2 * L + 1
                norm(n)
                modulate(n)
                act.wait_ge(S("lg_ready"), L + 1)
                s.activation(rt[:, 64:64 + 8], rt[:, 56:56 + 8], ACT.Exp).then_inc(S("eg_ready"), 1)
                act.wait_ge(S("l2_ready"), L + 1)
                s.activation(rt[:, 86:88], rt[:, 84:86], ACT.Exp).then_inc(S("e2_ready"), 1)
                n0 = MOE_BASE[L]

                def hg_evac(i):
                    act.wait_ge(S("gathered"), 10 * L + 1 + 2 * i)
                    for k in range(0, 4):
                        last = s.activation(hg[:, k, :], bank[0][:, k * P:(k + 1) * P], ACT.Identity,
                                            scale=modA[:, n, k:k + 1], bias=mod[:, L, SH_F, k:k + 1])
                    last.then_inc(S("hg_act"), 1)

                hg_evac(0)
                with act.Fori(0, NG) as i:
                    def silu(e):
                        act.wait_ge(S("a_ps"), 16 * L + 4 * i + e + 1)
                        act.wait_ge(S("he_ready"), 1 + 16 * L + 4 * i + e)
                        s.activation(sil[:, :], bank[0 + e % 2], ACT.Silu).then_inc(S("sil_ready"), 1)

                    def he_t(e):
                        act.wait_ge(S("heT_ps"), 16 * L + 4 * i + e + 1)
                        s.activation(heT[:, e % 2, :], bank[6], ACT.Copy).then_inc(S("heT_ready"), 1)

                    silu(0)
                    silu(1)
                    he_t(0)
                    silu(2)
                    he_t(1)
                    silu(3)
                    he_t(2)
                    hg_evac(i + 1)
                    he_t(3)
                    act.wait_ge(S("y_ps"), 16 * L + 4 * i + 4)
                    s.activation(yg[:, bass.ds(i, 1), 0:HALF], bank[4].unsqueeze(1), ACT.Copy).then_inc(
                        S("y_act"), 1)
                gate_row(n)
                act.wait_ge(S("over_known"), L + 1)
                n_over = act.value_load(rti[0:1, 0:1], min_val=0, max_val=T)
                with act.If(n_over > 0):
                    with act.Fori(0, EPG) as e:
                        act.wait_ge(S(f"over_used{L}"), e * 6 + 7)
                        s.activation(sil[:, :], bank[0], ACT.Silu).then_inc(S(f"over_sil{L}"), 1)
                        act.wait_ge(S(f"over_heT{L}"), e + 1)
                        s.activation(heT[:, 0, :], bank[6], ACT.Copy).then_inc(S(f"over_hT{L}"), 1)

            ffn(0)

            act.wait_ge(S("x_new"), 2)
            s.dma_start(s5r[0:NQT, 0, :], a["s5_a_re"][0].rearrange("(q g) p -> q (g p)", g=2)).then_inc(S("s5_in"), 16)
            s.dma_start(s5r[0:NQT, 1, :], a["s5_a_im"][0].rearrange("(q g) p -> q (g p)", g=2)).then_inc(S("s5_in"), 16)
            s.dma_start(s5r[0:NQT, 2, 0:2], a["s5_log_dt"][0].rearrange("(q g) -> q g", g=2)).then_inc(S("s5_in"), 16)
            for v, name in enumerate(("s5_b_re", "s5_b_im")):
                s.dma_start(Bl[:, v, :, :], a[name][0].rearrange("(q g) p c -> (g p) q c", g=2)).then_inc(S("s5_in"), 16)
            for v, name in enumerate(("s5_c_re", "s5_c_im")):
                for u in range(2):
                    s.dma_start(Cn[:, v, :, u * 64:(u + 1) * 64],
                                a[name][0].rearrange("(k g) c p -> (g c) k p", k=KD)).then_inc(S("s5_in"), 16)
            act.wait_ge(S("s5_in"), 16 * 9)
            R = s5r
            ch.link(s.activation(R[0:NQT, 3, 0:2], R[0:NQT, 2, 0:2], ACT.Exp))
            s.activation(R[0:NQT, 4, 0:2], R[0:NQT, 3, 0:2], ACT.Copy).then_inc(S("dt_ready"), 1)
            act.wait_ge(S("s5_th"), 1)
            s.activation(R[0:NQT, 7, :], R[0:NQT, 5, :], ACT.Exp)
            s.activation(R[0:NQT, 8:10, :], R[0:NQT, 10:12, :], ACT.Sin).then_inc(S("s5_trig"), 1)
            for v in range(2):
                for hf in range(2):
                    act.wait_ge(S("bt_ps"), 2 * v + hf + 1)
                    last = s.activation(BT[:, v, hf * 4:hf * 4 + 4, :], bank[5 + hf].rearrange("p (k n) -> p k n", n=P),
                                        ACT.Copy)
                    if (v, hf) == (1, 1):
                        last.then_inc(S("bt_ready"), 1)
                    else:
                        last.then_inc(S("bt_evac"), 1)
            norm(2)
            modulate(2)
            gate_row(2)
            act.wait_ge(S("ct_evac"), 8)
            s.dma_start(glub, a["s5_glu_b"][0].rearrange("(r n) -> r n", r=4)).then_inc(S("glub_in"), 16)
            with act.Fori(0, KD) as k:
                act.wait_ge(S("yv_ready"), 1 + k + 1)
                s.activation(actT[:, bass.ds(k, 1), :], yv[:, :].unsqueeze(1), ACT.Gelu_apprx_tanh).then_inc(
                    S("act_ready"), 1)
            for h in range(2):
                for b in range(NB):
                    act.wait_ge(S("glu_ps"), 2 * h + 2)
                    s.activation(qq[:, 2 * h + b, :], bank[4 * h + 2 + b], ACT.Sigmoid).then_inc(S("glu_sig"), 1)
            ffn(1)
            act.wait_ge(S("x_new"), 4)
            act.dma_start(fing, a["final_g"].rearrange("(o n) -> o n", o=1).to_broadcast([P, D])).then_inc(S("fg_in"), 16)
            norm(4)

        @block.vector
        def _(dve):
            v = nc.vector
            for name in ('yv_ready', 'q_ready', 'bu_used', 'he_ready', 'y_dve', 'mod1_evac', 'over_yg0', 'over_yg1'):
                dve.sem_inc(S(name), PRIMED[name])
            ch = Chain(dve, S("dve_order"))
            link = ch.link

            cond = mod[:, 1, 0, :]

            def gemv(r, j, use, done):
                dve.wait_ge(S(f"ada_in{j % ASLOTS}"), use)
                u, kh = j // 2 % 3, r % 2
                if kh:
                    dve.wait_ge(S("gemv_done"), done)
                w = aring[:, j % ASLOTS, :].rearrange("p (k c) -> p k c", c=HALF)
                for kk in range(4):
                    k = kh * 4 + kk
                    if k == 0:
                        ins = v.tensor_scalar(acc[:, u, :], w[:, kk, :], condc[:, k:k + 1], None, ALU.mult)
                    else:
                        ins = v.scalar_tensor_tensor(acc[:, u, :], w[:, kk, :], condc[:, k:k + 1], acc[:, u, :],
                                                     ALU.mult, ALU.add)
                    if kk < 3:
                        link(ins)
                    else:
                        ins.then_inc(S("gemv_done"), 1)

            condc = stat[:, 8:16]
            dve.wait_ge(S("pos_in"), 16)
            pos = rope[:, 0, 0:NB]
            link(v.tensor_copy(pos, rti[:, 0:NB]))
            ang = rope[:, 1, :].rearrange("p (b i) -> p b i", b=NB)
            for i in range(RH):
                last = v.tensor_scalar(ang[:, :, i], pos, float(ROPE_THETA ** (-2.0 * i / ROT)), None, ALU.mult)
            link(last)

            def reduce_angle(src, turns, lo, hi):
                link(v.tensor_scalar(turns, src, 1.0 / (2 * PI), MAGIC, ALU.mult, ALU.add))
                link(v.tensor_scalar(turns, turns, -MAGIC, None, ALU.add))
                link(v.scalar_tensor_tensor(hi, turns, -TWO_PI[0], src, ALU.mult, ALU.add))
                link(v.scalar_tensor_tensor(hi, turns, -TWO_PI[1], hi, ALU.mult, ALU.add))
                link(v.scalar_tensor_tensor(hi, turns, -TWO_PI[2], hi, ALU.mult, ALU.add))
                link(v.tensor_scalar(hi, hi, 3.1415925, -3.1415925, ALU.min, ALU.max))
                link(v.scalar_tensor_tensor(lo, hi, -1.0, hi, ALU.mult, ALU.max))

            reduce_angle(rope[:, 1, :], rope[:, 6, :], rope[:, 2, :], rope[:, 3, :])
            v.tensor_scalar(rope[:, 2, :], rope[:, 2, :], -1.0, PI / 2, ALU.mult, ALU.add).then_inc(S("rope_arg"), 1)

            dve.wait_ge(S("cols_ready"), 1)
            link(v.tensor_copy(condc, cond))
            at, n = ROWS["lam"]
            lam = cols[:, at:at + n]
            link(v.scalar_tensor_tensor(sp[:, 2, :], lam, -1.0, lam, ALU.mult, ALU.max))
            v.tensor_scalar(sp[:, 0, :], sp[:, 2, :], -1.0, None, ALU.mult).then_inc(S("sp_arg"), 1)
            link(v.tensor_scalar(sp[:, 3, :], lam, -1.0, 0.0, ALU.mult, ALU.max))
            dve.wait_ge(S("sp_ln"), 1)
            link(v.tensor_tensor(sp[:, 1, :], sp[:, 1, :], sp[:, 3, :], ALU.add))
            v.tensor_scalar(sp[:, 2, :], sp[:, 1, :], 8.0, None, ALU.mult)
            v.tensor_scalar(sp[:, 3, :], sp[:, 1, :], -8.0, None, ALU.mult).then_inc(S("sp_ready"), 1)

            def mod_evac(lo, hi):
                dve.wait_ge(S("mod_ps"), hi)
                v.tensor_tensor(mod[:, 0].rearrange("p s k -> p (s k)")[:, 4 * lo:4 * hi],
                                bank[7][:, 4 * lo:4 * hi], adab[:, 0, 4 * lo:4 * hi], ALU.add).then_inc(
                                    S("mod_cols"), 1)
                dve.wait_ge(S("mod_cols"), {0: 1, 4: 2, 6: 3}[lo])

            def mod_scale(n, done=True):
                L, sec = n // 2, (SC_M if n % 2 == 0 else SC_F)
                at = ROWS[("mix0", "ffn0", "mix1", "ffn1")[n]][0]
                v.scalar_tensor_tensor(modA[:, n, :], mod[:, L, sec, :], 1.0, cols[:, at:at + KD],
                                       ALU.add, ALU.mult).then_inc(S("modA_ready"), 1)
                dve.wait_ge(S("modA_ready"), n + 1)

            def gemv0(lo, hi):
                for r in range(lo, hi):
                    if r % 2 == 0 and r // 2 >= 3:
                        dve.wait_ge(S("mod_ps"), r // 2 - 2)
                    gemv(r, r % 6, 16 * (r // ASLOTS + 1), r)

            def norm(n):
                if n == 0:
                    dve.wait_ge(S("x_in"), 16)
                link(v.tensor_tensor_reduce(out=xhat[:, 1, :], in0=x[:, 1, :], in1=x[:, 1, :], scale=1.0, scalar=0.0,
                                            op0=ALU.mult, op1=ALU.add, accum_out=stat[:, 1:2]))
                dve.wait_ge(S("ss_act"), n + 1)
                v.tensor_scalar(stat[:, 2:4], stat[:, 0:2], 1.0 / D, EPS, ALU.mult, ALU.add).then_inc(S("var_ready"), 1)
                dve.wait_ge(S("std_ready"), n + 1)
                link(v.reciprocal(stat[:, 6:8], stat[:, 4:6]))
                for b in range(NB):
                    last = v.tensor_scalar(xhat[:, b, :], x[:, b, :], stat[:, 6 + b:7 + b], None, ALU.mult)
                    if n < 4:
                        last.then_inc(S("xhat_ready"), 1)
                    else:
                        link(last)

            def modulate(n):
                L, sec = n // 2, (SH_M if n % 2 == 0 else SH_F)
                for k in (2, 3, 6, 7):
                    dve.wait_ge(S("xT_ps"), 4 * n + k // 2 + 1)
                    v.tensor_scalar(hT[:, k, :], bank[k // 2][:, (k % 2) * T:(k % 2 + 1) * T], modA[:, n, k:k + 1],
                                    mod[:, L, sec, k:k + 1], ALU.mult, ALU.add).then_inc(S("hT_dve"), 1)

            gemv0(0, 8)
            mod_evac(0, 4)
            mod_scale(0)
            norm(0)
            modulate(0)
            dve.wait_ge(S("kv_ps"), 1)
            link(v.tensor_copy(qkv[:, :, HALF:768], bank[6].rearrange("p (b n) -> p b n", b=NB)))
            dve.wait_ge(S("q_evac"), 2)
            dve.wait_ge(S("rope_ready"), 1)
            for b in range(NB):
                hd = qkv[:, b, 0:640].rearrange("p (h n) -> p h n", n=HEAD)
                x1, x2 = hd[:, :, 0:RH], hd[:, :, RH:ROT]
                cc = rope[:, 4, b * RH:(b + 1) * RH].unsqueeze(1).to_broadcast([P, 10, RH])
                ss = rope[:, 5, b * RH:(b + 1) * RH].unsqueeze(1).to_broadcast([P, 10, RH])
                t = [rq[:, m, :].rearrange("p (h n) -> p h n", n=RH) for m in range(4)]
                v.tensor_tensor(t[0], x1, cc, ALU.mult)
                v.tensor_tensor(t[1], x2, ss, ALU.mult)
                v.tensor_tensor(t[2], x2, cc, ALU.mult)
                link(v.tensor_tensor(t[3], x1, ss, ALU.mult))
                v.tensor_tensor(x1, t[0], t[1], ALU.subtract)
                link(v.tensor_tensor(x2, t[2], t[3], ALU.add))
                kh = qkv[:, b, NQ * HEAD:640].rearrange("p (g n) -> p g n", g=NKV)
                v.tensor_copy(k2[:, b, :].rearrange("p (g u n) -> p g u n", g=NKV, u=2),
                              kh.unsqueeze(2).to_broadcast([P, NKV, 2, HEAD])).then_inc(S("rope_done"), 1)
                dve.wait_ge(S("rope_done"), b + 1)
            dve.wait_ge(S("xr_ready"), 1)
            for j in range(LT):
                link(v.tensor_scalar(xc[:, j, :], xr[:, j, :], col("conv_w", 3 * LT + j), col("conv_b", j),
                                     ALU.mult, ALU.add))
            for s_ in range(1, CONV):
                for j in range(LT):
                    last = v.scalar_tensor_tensor(xc[:, j, s_:], xr[:, j, 0:T - s_], col("conv_w", (3 - s_) * LT + j),
                                                  xc[:, j, s_:], ALU.mult, ALU.add)
                    if s_ < CONV - 1:
                        if j == LT - 1:
                            link(last)
            last.then_inc(S("xc_ready"), 1)
            dve.wait_ge(S("kT_ps"), 1)
            v.tensor_copy(kT[:, :, :], bank[6].rearrange("p (g t) -> p g t", g=NKV)).then_inc(S("kT_ready"), 1)
            dve.wait_ge(S("small_in"), 16 * 9)
            sk = smx[:, 4, 0:NQ]
            link(v.tensor_scalar(sk.rearrange("p (r i) -> p r i", r=2), sink[:, :].rearrange("p (i r) -> p r i", r=2),
                                 1.0 / SCALE, None, ALU.mult))
            for b in range(NB):
                pp = P0 if b == 0 else P1
                n_k = P * (b + 1)
                dve.wait_ge(S("s_ps"), b + 1)
                if b == 0:
                    sc = [PS[:, r, :].rearrange("p (i n) -> p i n", n=P) for r in range(2)]
                    rng = [(0, 64, 0, 64), (64, P, 0, P)]
                    zero = [(0, 64, 64, P)]
                else:
                    sc = [PS[:, w:w + 2, :].rearrange("p b (i n) -> p (b i) n", n=T) for w in (4, 2)]
                    rng = [(0, 64, 64, 192), (64, P, P, T)]
                    zero = [(0, 64, 0, 64), (0, 64, 192, T), (64, P, 0, P)]
                for lo, hi, k0, k1 in zero:
                    v.memset(pp[lo:hi, :, k0:k1], 0.0)
                mx = smx[:, 0, b * NQ:(b + 1) * NQ]
                for lo, hi, k0, k1 in rng:
                    for r in range(2):
                        last = v.tensor_reduce(smx[lo:hi, 0, b * NQ + 4 * r:b * NQ + 4 * r + 4], sc[r][lo:hi, :, k0:k1],
                                               AX.X, ALU.max)
                link(last)
                link(v.tensor_tensor(mx, mx, sk, ALU.max))
                v.tensor_tensor(smx[:, 1, b * NQ:(b + 1) * NQ], sk, mx, ALU.subtract)
                for lo, hi, k0, k1 in rng:
                    for r in range(2):
                        m = smx[lo:hi, 0, b * NQ + 4 * r:b * NQ + 4 * r + 4].unsqueeze(2).to_broadcast(
                            [64, 4, k1 - k0])
                        last = v.tensor_tensor(pp[lo:hi, 4 * r:4 * r + 4, k0:k1], sc[r][lo:hi, :, k0:k1], m,
                                               ALU.subtract)
                last.then_inc(S("s_less_m"), 1)
            for b in range(NB):
                pp = P0 if b == 0 else P1
                n_k = P * (b + 1)
                dve.wait_ge(S("p_exp"), b + 1)
                den = smx[:, 3, b * NQ:(b + 1) * NQ]
                link(v.tensor_reduce(den, pp[:, :, 0:n_k], AX.X, ALU.add))
                link(v.tensor_tensor(den, den, smx[:, 2, b * NQ:(b + 1) * NQ], ALU.add))
                link(v.reciprocal(den, den))
                v.tensor_tensor(pp[:, :, 0:n_k], pp[:, :, 0:n_k], den.unsqueeze(2).to_broadcast([P, NQ, n_k]),
                                ALU.mult).then_inc(S("p_ready"), 1)
            gemv0(8, 12)
            mod_evac(4, 6)
            dve.wait_ge(S("lru_a"), 1)
            link(v.tensor_tensor(lr_i, lr_i, xc[:, :, :], ALU.mult))
            link(v.tensor_tensor(lr_r, lr_u, lr_u, ALU.mult))
            v.scalar_tensor_tensor(lr_t.rearrange("p k t -> p (k t)"), lr_r.rearrange("p k t -> p (k t)"), 1.0,
                                   lr_t.rearrange("p k t -> p (k t)"), ALU.add, ALU.mult).then_inc(S("lru_b2"), 1)
            dve.wait_ge(S("lru_sq"), 1)
            link(v.tensor_tensor(lr_i, lr_i, lr_t, ALU.mult))
            for j in range(LT):
                last = v.tensor_tensor_scan(lr_r[:, j, :], lr_u[:, j, :], lr_i[:, j, :], 0.0, ALU.mult, ALU.add)
            link(last)
            v.tensor_tensor(mixT[:, 4:8, :], lr_r, gate[:, :, :], ALU.mult).then_inc(S("lru_ready"), 1)

            def residual(n, waits, psum):
                dve.wait_ge(S("grow_ready"), n + 1)
                tmp = hT[:, 4:8, :].rearrange("p k t -> p (k t)").rearrange("p (s n) -> p s n", n=HALF)
                for b in range(NB):
                    for h in range(2):
                        dve.wait_ge(S(waits), (2 * b + h + 1) + 4 * (n // 2))
                        gr = grow[:, h * HALF:(h + 1) * HALF]
                        link(v.tensor_tensor(tmp[:, h, :], psum(b, h), gr, ALU.mult))
                        last = v.tensor_tensor(x[:, b, h * HALF:(h + 1) * HALF], x[:, b, h * HALF:(h + 1) * HALF],
                                               tmp[:, h, :], ALU.add)
                return last

            residual(0, "m_ps", lambda b, h: bank[2 * b + h]).then_inc(S("x_new"), 1)
            dve.wait_ge(S("x_new"), 1)
            gemv0(12, 24)
            mod_evac(6, 12)
            mod_scale(1)

            def ffn(L):
                n = 2 * L + 1
                norm(n)
                modulate(n)
                lg = rt[:, 0:40].rearrange("p (b n) -> p b n", b=NB)
                dve.wait_ge(S("router_ps"), L + 1)
                psl = bank[4][:, 0:40].rearrange("p (b n) -> p b n", b=NB)
                link(v.tensor_tensor(lg, psl, rb[:, L:L + 1, :].to_broadcast([P, NB, 20]), ALU.add))
                lg4 = lg[:, :, 0:NG]
                r2 = lambda o: rt[:, o:o + NB]
                r8 = lambda o: rt[:, o:o + 8].rearrange("p (b g) -> p b g", b=NB)
                bc = lambda ap: ap.unsqueeze(2).to_broadcast([P, NB, 4])
                prio = r8(300)
                for g_ in range(4):
                    last = v.memset(prio[:, :, g_], float(4 - g_))
                link(last)

                def first_max(val, mx, oh, key):
                    link(v.tensor_reduce(mx, val, AX.X, ALU.max))
                    link(v.tensor_tensor(oh, val, bc(mx), ALU.is_equal))
                    link(v.tensor_tensor(oh, oh, prio, ALU.mult))
                    link(v.tensor_reduce(key, oh, AX.X, ALU.max))
                    link(v.tensor_tensor(oh, oh, bc(key), ALU.is_equal))

                oh = r8(48)
                first_max(lg4, r2(40), oh, r2(42))
                v.tensor_tensor(r8(56), lg4, bc(r2(40)), ALU.subtract).then_inc(S("lg_ready"), 1)
                le = lg[:, :, NG:].rearrange("p b (g e) -> p b g e", g=NG)
                sel = rt[:, 96:128].rearrange("p (b g e) -> p b g e", b=NB, g=NG)
                link(v.tensor_tensor(sel, le, oh.unsqueeze(3).to_broadcast([P, NB, NG, EPG]), ALU.mult))
                les = r8(128)
                link(v.tensor_reduce(les, sel.rearrange("p b g e -> p b e g"), AX.X, ALU.add))
                oh1, oh2 = r8(136), r8(144)
                first_max(les, r2(80), oh1, r2(42))
                link(v.scalar_tensor_tensor(rt[:, 152:160], rt[:, 136:144], -1e30, rt[:, 128:136], ALU.mult, ALU.add))
                first_max(r8(152), r2(82), oh2, r2(42))
                v.tensor_tensor(r2(84), r2(82), r2(80), ALU.subtract).then_inc(S("l2_ready"), 1)
                dve.wait_ge(S("eg_ready"), L + 1)
                link(v.tensor_reduce(r2(88), r8(64), AX.X, ALU.add))
                dve.wait_ge(S("e2_ready"), L + 1)
                link(v.tensor_scalar(r2(90), r2(86), 1.0, None, ALU.add))
                link(v.tensor_tensor(r2(88), r2(88), r2(90), ALU.mult))
                link(v.reciprocal(r2(88), r2(88)))
                link(v.tensor_tensor(r2(90), r2(88), r2(86), ALU.mult))
                gt = r8(160)
                link(v.tensor_tensor(gt, oh1, bc(r2(88)), ALU.mult))
                link(v.tensor_tensor(oh2, oh2, bc(r2(90)), ALU.mult))
                v.tensor_tensor(gt, gt, oh2, ALU.add).then_inc(S("gates_ready"), 1)
                dve.wait_ge(S("gates_ready"), L + 1)
                dve.wait_ge(S("rank_ps"), L + 1)
                rk = r2(168)
                link(v.tensor_tensor(r8(176), oh, bank[5][:, 0:8].rearrange("p (b g) -> p b g", b=NB), ALU.mult))
                link(v.tensor_reduce(rk, r8(176), AX.X, ALU.add))
                for b in range(NB):
                    for g_ in range(NG):
                        v.tensor_scalar(pick[:, b, g_, :], slot_no[:, :], rt[:, 168 + b:169 + b], oh[:, b, g_:g_ + 1],
                                        ALU.is_equal, ALU.mult)
                link(v.tensor_scalar(r2(170), rk, -float(P), None, ALU.add))
                for b in range(NB):
                    last = v.tensor_scalar(pick[:, b, NG, :], slot_no[:, :], rt[:, 170 + b:171 + b], None, ALU.is_equal)
                last.then_inc(S("pick_ready"), 1)
                ov = rt[:, 192:196].rearrange("p (b n) -> p b n", b=NB)
                link(v.tensor_scalar(ov[:, :, 0], rk, float(P), None, ALU.is_ge))
                link(v.tensor_scalar(ov[:, :, 1], rk, float(P), None, ALU.is_equal))
                for g_ in range(NG):
                    last = v.tensor_scalar(r8(200)[:, :, g_], oh[:, :, g_], float(g_), None, ALU.mult)
                link(last)
                link(v.tensor_reduce(r2(208), r8(200), AX.X, ALU.add))
                v.tensor_tensor(ov[:, :, 1], ov[:, :, 1], r2(208), ALU.mult).then_inc(S("ov_ready"), 1)
                dve.wait_ge(S("gsl_ps"), L + 1)
                link(v.tensor_copy(gsl[:, :, :], bank[5][:, 16:16 + 20].rearrange("p (g e) -> p g e", e=EPG)))
                v.tensor_copy(rti[:, 0:2], bank[5][:, 40:42]).then_inc(S("over_known"), 1)
                dve.wait_ge(S("over_known"), L + 1)

                def hg_evac(i):
                    dve.wait_ge(S("gathered"), 10 * L + 2 + 2 * i)
                    for k in range(4, KD):
                        last = v.tensor_scalar(hg[:, k, :], bank[2][:, (k - 4) * P:(k - 3) * P],
                                               modA[:, n, k:k + 1], mod[:, L, SH_F, k:k + 1], ALU.mult, ALU.add)
                    last.then_inc(S("hg_dve"), 1)

                hg_evac(0)
                n0 = MOE_BASE[L]
                per = 1 + (18 if L == 0 else 0)
                with dve.Fori(0, NG) as i:
                    ch.enter(i, per)
                    link(v.tensor_copy(gcur[:, :], gsl[:, bass.ds(i, 1), :].rearrange("p a e -> p (a e)")))
                    j = 0
                    for e in range(EPG):
                        dve.wait_ge(S("sil_ready"), 1 + 16 * L + 4 * i + e + 1)
                        dve.wait_ge(S("b_ps"), 16 * L + 4 * i + e + 1)
                        v.scalar_tensor_tensor(he[:, e % 2, :], sil[:, :], gcur[:, e:e + 1], bank[2 + e % 2],
                                               ALU.mult, ALU.mult).then_inc(S("he_ready"), 1)
                        if L == 0:
                            for _ in range(GEMV_OF[e]):
                                if j % 2 == 0:
                                    dve.wait_ge(S("mod_ps"), A_UNITS + 3 * i)
                                gemv(j, j, 16 * (j // ASLOTS + 1) + 16 * A_HALVES // ASLOTS + i * 32, A_HALVES + j + 6 * i)
                                j += 1
                    hg_evac(i + 1)
                    dve.wait_ge(S("y_ps"), 16 * L + 4 * i + 4)
                    v.tensor_copy(yg[:, bass.ds(i, 1), HALF:], bank[5].unsqueeze(1)).then_inc(S("y_dve"), 1)
                    if L == 0:
                        dve.wait_ge(S("mod_ps"), A_UNITS + 3 + 3 * i)
                        v.tensor_copy(mod[:, 1].rearrange("p s k -> p (s k)")[:, bass.ds(i * 12, 12)],
                                      bank[7][:, 64:76]).then_inc(S("mod1_evac"), 1)
                ch.leave(NG)
                if L == 0:
                    dve.wait_ge(S("mod1_evac"), 1 + NG)
                    m1 = mod[:, 1].rearrange("p s k -> p (s k)")
                    v.tensor_tensor(m1, m1, adab[:, 1, :], ALU.add).then_inc(S("mod_cols"), 1)
                    dve.wait_ge(S("mod_cols"), 4)
                    mod_scale(2)
                    mod_scale(3)
                dve.wait_ge(S("pickT_ps"), L + 1)
                v.tensor_copy(pickT[:, :, :], PS[:, 0:2, :].rearrange("p c (g t) -> p (c g) t", t=T)).then_inc(
                    S("pickT_ready"), 1)
                dve.wait_ge(S("grow_ready"), n + 1)
                tmp = heT
                for b in range(NB):
                    for h in range(2):
                        dve.wait_ge(S("sc_ps"), 4 * L + 2 * b + h + 1)
                        link(v.tensor_tensor(tmp[:, h, :], bank[(0, 1, 2, 3)[2 * b + h]], grow[:, h * HALF:(h + 1) * HALF],
                                             ALU.mult))
                        last = v.tensor_tensor(x[:, b, h * HALF:(h + 1) * HALF], x[:, b, h * HALF:(h + 1) * HALF],
                                               tmp[:, h, :], ALU.add)
                last.then_inc(S("x_main"), 1)
                dve.wait_ge(S("x_main"), L + 1)
                n_over = dve.value_load(rti[0:1, 0:1], min_val=0, max_val=T)
                with dve.If(n_over > 0):
                    oc = Chain(dve, S(f"over_order{L}"))
                    oc.link(v.memset(yg[:, 0, :], 0.0))
                    with dve.Fori(0, EPG) as e:
                        oc.enter(e, 1)
                        dve.wait_ge(S(f"over_sil{L}"), e + 1)
                        oc.link(v.tensor_copy(gcur[:, 0:1], gsl[:, NG, bass.ds(e, 1)]))
                        v.scalar_tensor_tensor(he[:, 0, :], sil[:, :], gcur[:, 0:1], bank[2], ALU.mult,
                                               ALU.mult).then_inc(S(f"over_he{L}"), 1)
                        dve.wait_ge(S(f"over_used{L}"), e * 6 + 9)
                        v.tensor_tensor(yg[:, 0, :], yg[:, 0, :], PS[:, 4:6, :].rearrange("p b n -> p (b n)"),
                                        ALU.add).then_inc(S(f"over_yg{L}"), 1)
                        dve.wait_ge(S(f"over_yg{L}"), 1 + e + 1)
                    oc.leave(EPG)
                    dve.wait_ge(S(f"over_pT{L}"), 1)
                    v.tensor_copy(pickT[:, 0, :], bank[6][:, 0:T]).then_inc(S(f"over_pick{L}"), 1)
                    dve.wait_ge(S(f"over_sc{L}"), 1)
                    for b in range(NB):
                        for h in range(2):
                            oc.link(v.tensor_tensor(tmp[:, h, :], bank[2 * b + h], grow[:, h * HALF:(h + 1) * HALF],
                                                    ALU.mult))
                            oc.link(v.tensor_tensor(x[:, b, h * HALF:(h + 1) * HALF],
                                                    x[:, b, h * HALF:(h + 1) * HALF], tmp[:, h, :], ALU.add))
                nc.vector.drain().then_inc(S("x_new"), 1)
                dve.wait_ge(S("x_new"), 2 * L + 2)

            ffn(0)

            R = s5r
            q = slice(0, NQT)
            dve.wait_ge(S("dt_ready"), 1)
            dtb = R[q, 4, 0:2].unsqueeze(2).to_broadcast([NQT, 2, STATE])
            h2 = lambda r: R[q, r, :].rearrange("q (g p) -> q g p", g=2)
            link(v.tensor_tensor(h2(5), h2(0), dtb, ALU.mult))
            link(v.tensor_tensor(h2(6), h2(1), dtb, ALU.mult))
            reduce_angle(R[q, 6, :], R[q, 12, :], R[q, 10, :], R[q, 11, :])
            v.tensor_scalar(R[q, 10, :], R[q, 10, :], -1.0, PI / 2, ALU.mult, ALU.add).then_inc(S("s5_th"), 1)
            dve.wait_ge(S("s5_trig"), 1)
            tt = lambda d, s1, s2, op: link(v.tensor_tensor(R[q, d, :], R[q, s1, :], R[q, s2, :], op))
            tt(12, 7, 8, ALU.mult)
            tt(13, 7, 9, ALU.mult)
            link(v.tensor_scalar(R[q, 12, :], R[q, 12, :], -1.0, None, ALU.add))
            tt(14, 0, 0, ALU.mult)
            tt(15, 1, 1, ALU.mult)
            tt(14, 14, 15, ALU.add)
            link(v.reciprocal(R[q, 14, :], R[q, 14, :]))
            tt(15, 12, 0, ALU.mult)
            tt(16, 13, 1, ALU.mult)
            tt(15, 15, 16, ALU.add)
            tt(16, 13, 0, ALU.mult)
            tt(17, 12, 1, ALU.mult)
            tt(16, 16, 17, ALU.subtract)
            tt(10, 15, 14, ALU.mult)
            v.tensor_tensor(R[q, 11, :], R[q, 16, :], R[q, 14, :], ALU.mult).then_inc(S("s5_rows"), 1)
            dve.wait_ge(S("s5_cols_ps"), 1)
            link(v.tensor_copy(s5c[:, :, :], bank[4][:, 0:5 * NQT].rearrange("p (r q) -> p r q", r=5)))
            cb = lambda r: s5c[:, r, :].unsqueeze(2).to_broadcast([P, NQT, CH])
            link(v.memset(Bp[:, :, :, :], 0.0))
            for w, (s1, s2, op) in enumerate(((0, 1, ALU.subtract), (1, 0, ALU.add))):
                link(v.tensor_tensor(bt1[:, :, :], Bl[:, s1, :, :], cb(3), ALU.mult))
                link(v.tensor_tensor(bt2[:, :, :], Bl[:, s2, :, :], cb(4), ALU.mult))
                for u in range(2):
                    pr_ = slice(u * 64, u * 64 + 64)
                    dst = Bp[pr_, w].rearrange("p k (q g c) -> p (k q) g c", g=2, c=CH)[:, :, u, :]
                    v.tensor_tensor(dst, bt1[pr_, :, :], bt2[pr_, :, :], op).then_inc(S("bp_ready"), 1)
                dve.wait_ge(S("bp_ready"), 2 * w + 2)
            link(v.memset(CT[:, :, :, :], 0.0))
            for w in range(2):
                for hf in range(2):
                    dve.wait_ge(S("ct_ps"), 2 * w + hf + 1)
                    for u in range(2):
                        pr_ = slice(u * 64, u * 64 + 64)
                        dst = CT[pr_, w, hf * 4:hf * 4 + 4, :].rearrange("p k (q g c) -> p (k q) g c", g=2, c=CH)[:, :, u, :]
                        src = bank[hf * 2 + 1][pr_, :].rearrange("p (k g c) -> p k g c", g=2, c=CH)[:, :, u, :]
                        v.tensor_scalar(dst, src, -1.0 if w else 1.0, None, ALU.mult).then_inc(S("ct_evac"), 1)
            w32 = lambda m: Ew[:, m, 0:NQT]
            link(v.tensor_copy(w32(0), s5c[:, 1, :]))
            link(v.tensor_copy(w32(1), s5c[:, 2, :]))
            for table in (1, 0):
                Ec, Es = E[:, 2 * table, :, :], E[:, 2 * table + 1, :, :]
                v.memset(Ec[:, :, 0:1], 1.0)
                link(v.memset(Es[:, :, 0:1], 0.0))
                for n_ in (1, 2, 4, 8):
                    c_b = w32(0).unsqueeze(2).to_broadcast([P, NQT, n_])
                    s_b = w32(1).unsqueeze(2).to_broadcast([P, NQT, n_])
                    te = [Ew[:, 2 + m, 0:NQT * n_].rearrange("p (q n) -> p q n", n=n_) for m in range(4)]
                    v.tensor_tensor(te[0], Ec[:, :, 0:n_], c_b, ALU.mult)
                    v.tensor_tensor(te[1], Es[:, :, 0:n_], s_b, ALU.mult)
                    v.tensor_tensor(te[2], Ec[:, :, 0:n_], s_b, ALU.mult)
                    link(v.tensor_tensor(te[3], Es[:, :, 0:n_], c_b, ALU.mult))
                    v.tensor_tensor(Ec[:, :, n_:2 * n_], te[0], te[1], ALU.subtract)
                    link(v.tensor_tensor(Es[:, :, n_:2 * n_], te[2], te[3], ALU.add))
                    v.tensor_tensor(w32(2), w32(0), w32(0), ALU.mult)
                    v.tensor_tensor(w32(3), w32(1), w32(1), ALU.mult)
                    link(v.tensor_tensor(w32(4), w32(0), w32(1), ALU.mult))
                    link(v.tensor_tensor(w32(0), w32(2), w32(3), ALU.subtract))
                    link(v.tensor_scalar(w32(1), w32(4), 2.0, None, ALU.mult))
            norm(2)
            modulate(2)
            f2 = lambda ap: ap.rearrange("p (q t) -> p q t", q=2)
            per = 4
            with dve.Fori(0, KD) as k:
                ch.enter(k, per)
                for j in range(2):
                    bre = PS[:, 2 * j:2 * j + 2, 0:T]
                    bim = PS[:, 2 * j:2 * j + 2, T:2 * T]
                    c_, s_ = f2(cs[:, j, 0, :]), f2(cs[:, j, 1, :])
                    dve.wait_ge(S("bu_ready"), 1 + 4 * k + 2 * j + 2)
                    dve.wait_ge(S("tab_ready"), 2 * k + j + 1)
                    v.tensor_tensor(f2(pr[:, 0, :]), bre, c_, ALU.mult)
                    v.tensor_tensor(f2(pr[:, 1, :]), bim, s_, ALU.mult)
                    v.tensor_tensor(f2(pr[:, 2, :]), bim, c_, ALU.mult)
                    v.tensor_tensor(f2(pr[:, 3, :]), bre, s_, ALU.mult).then_inc(S("bu_used"), 1)
                    dve.wait_ge(S("bu_used"), 1 + 2 * k + j + 1)
                    v.tensor_tensor(pr[:, 0, :], pr[:, 0, :], pr[:, 1, :], ALU.add)
                    link(v.tensor_tensor(pr[:, 2, :], pr[:, 2, :], pr[:, 3, :], ALU.subtract))
                    for q_ in range(2):
                        r_ = s5c[:, 0, bass.ds(4 * k + 2 * j + q_, 1)].to_broadcast([P, T])
                        for m in range(2):
                            last = v.tensor_tensor_scan(gg[:, m, q_ * T:(q_ + 1) * T], r_,
                                                        pr[:, 2 * m, q_ * T:(q_ + 1) * T], 0.0, ALU.mult, ALU.add)
                    link(last)
                    dve.wait_ge(S("q_used"), 1 + 2 * k + j)
                    v.tensor_tensor(qq[:, 0, :], gg[:, 0, :], cs[:, j, 0, :], ALU.mult)
                    v.scalar_tensor_tensor(qq[:, 1, :], gg[:, 1, :], -1.0, cs[:, j, 1, :], ALU.mult, ALU.mult)
                    v.tensor_tensor(qq[:, 2, :], gg[:, 0, :], cs[:, j, 1, :], ALU.mult)
                    v.tensor_tensor(qq[:, 3, :], gg[:, 1, :], cs[:, j, 0, :], ALU.mult).then_inc(S("q_ready"), 1)
                dve.wait_ge(S("q_used"), 1 + 2 * k + 2)
                dve.wait_ge(S("act_ready"), 1 + k)
                v.scalar_tensor_tensor(yv[:, :], ucur[:, :], dcur[:, :], bank[4][:, 0:T], ALU.mult,
                                       ALU.add).then_inc(S("yv_ready"), 1)
            ch.leave(KD)
            dve.wait_ge(S("grow_ready"), 3)
            for h in range(2):
                for b in range(NB):
                    dve.wait_ge(S("glu_sig"), 2 * h + b + 1)
                    link(v.tensor_tensor(qq[:, 2 * h + b, :], qq[:, 2 * h + b, :], bank[4 * h + b], ALU.mult))
                    link(v.tensor_tensor(qq[:, 2 * h + b, :], qq[:, 2 * h + b, :], grow[:, h * HALF:(h + 1) * HALF],
                                         ALU.mult))
                    last = v.tensor_tensor(x[:, b, h * HALF:(h + 1) * HALF], x[:, b, h * HALF:(h + 1) * HALF],
                                           qq[:, 2 * h + b, :], ALU.add)
            last.then_inc(S("x_new"), 1)
            dve.wait_ge(S("x_new"), 3)
            ffn(1)
            norm(4)
            dve.wait_ge(S("fg_in"), 16)
            for b in range(NB):
                v.tensor_tensor(xhat[:, b, :], xhat[:, b, :], fing, ALU.mult).then_inc(S("out_ready"), 1)

        @block.tensor
        def _(pe):
            mm = nc.tensor.matmul
            for name in ('bu_ready', 'q_used'):
                pe.sem_inc(S(name), PRIMED[name])

            def tr(dst, src, n=P):
                return nc.tensor.transpose(dst, src, ident[0:n, 0:n])

            def bcol(ap, n=P):
                return ap.to_broadcast([ap.shape[0], n])

            pe.wait_ge(S("rows_in"), 16 * (len(ROWS) + 2))
            pe.wait_ge(S("ident_ready"), 1)
            tr(bank[0][:, 0:N_ROWS], rows, N_ROWS)
            tr(bank[1][:, 0:6 * KD], brow[:, 0, :], 6 * KD)
            tr(bank[1][:, 6 * KD:12 * KD], brow[:, 1, :], 6 * KD).then_inc(S("cols_ps"), 1)
            pe.wait_ge(S("consts_ready"), 1)
            pe.wait_ge(S("pool_order"), 3)

            def mod_cols(u, at):
                for c4 in range(4):
                    last = mm(bank[7][:, at + c4:at + c4 + 1], acc[:, u % 3, c4 * P:(c4 + 1) * P], ones[:, 0:1],
                              start=True, stop=True)
                last.then_inc(S("mod_ps"), 1)

            def mod0(lo, hi):
                if lo:
                    pe.wait_ge(S("mod_cols"), lo // 4 if lo == 4 else 2)
                for u in range(lo, hi):
                    pe.wait_ge(S("gemv_done"), 2 * u + 2)
                    mod_cols(u, 4 * u)

            def turn_x(n):
                pe.wait_ge(S("xhat_ready"), 2 * n + 2)
                for c in range(4):
                    for kk in range(2):
                        for b in range(NB):
                            last = tr(bank[c][:, kk * T + b * P:kk * T + (b + 1) * P],
                                      xhat[:, b, (2 * c + kk) * P:(2 * c + kk + 1) * P])
                    last.then_inc(S("xT_ps"), 1)

            def hT_ready(n):
                pe.wait_ge(S("hT_act"), 4 * n + 4)
                pe.wait_ge(S("hT_dve"), 4 * n + 4)

            def gate_row(n):
                L, sec = n // 2, (G_M if n % 2 == 0 else G_F)
                pe.wait_ge(S("mod_cols"), (2, 3, 4, 4)[n])
                for k in range(KD):
                    last = mm(bank[4 + k // 4][:, (k % 4) * P:(k % 4 + 1) * P], bcol(mod[:, L, sec, k:k + 1]),
                              ident[:, :], start=True, stop=True)
                last.then_inc(S("grow_ps"), 1)

            mod0(0, 4)
            turn_x(0)
            hT_ready(0)
            loaded(pe, 0)
            for b in range(NB):
                for k in range(KD):
                    last = mm(bank[4 + b], hT[:, k, b * P:(b + 1) * P], u3(0)[:, k, :], start=k == 0, stop=k == KD - 1)
                last.then_inc(S("q_ps"), 1)
            pe.wait_ge(S("q_ps"), 2)
            loaded(pe, 1)
            for b in range(NB):
                for k in range(KD):
                    last = mm(bank[6][:, b * 256:(b + 1) * 256], hT[:, k, b * P:(b + 1) * P], u3(1)[:, k, 0:256],
                              start=k == 0, stop=k == KD - 1)
            last.then_inc(S("kv_ps"), 1)

            def feature_tile(dst, w):
                for k in range(KD):
                    last = mm(dst, w[:, k, :], hT[:, k, :], start=k == 0, stop=k == KD - 1)
                return last

            for j in range(LT):
                at = 768 + j * P
                if j == 2:
                    loaded(pe, 2)
                w = u3(at // HALF)[:, :, at % HALF:at % HALF + P]
                last = feature_tile(bank[j // 2][:, (j % 2) * T:(j % 2 + 1) * T], w)
                if j % 2:
                    last.then_inc(S("xr_ps"), 1)
            for j in range(LT):
                at = 1280 + j * P
                if j == 2:
                    loaded(pe, 3)
                w = u3(at // HALF)[:, :, at % HALF:at % HALF + P]
                last = feature_tile(bank[2 + j // 2][:, (j % 2) * T:(j % 2 + 1) * T], w)
                if j % 2:
                    last.then_inc(S("gate_ps"), 1)
            for b in range(NB):
                pe.wait_ge(S("rope_done"), b + 1)
                for t in range(4):
                    last = tr(bank[4 + t // 2][:, (t % 2) * T + b * P:(t % 2) * T + (b + 1) * P],
                              qkv[:, b, t * P:(t + 1) * P])
                if b == NB - 1:
                    last.then_inc(S("qT_ps"), 1)
                for g in range(NKV):
                    last = tr(bank[6][:, g * T + b * P:g * T + (b + 1) * P], k2[:, b, g * P:(g + 1) * P])
                if b == NB - 1:
                    last.then_inc(S("kT_ps"), 1)
            pe.wait_ge(S("qT_ready"), 1)
            pe.wait_ge(S("kT_ready"), 1)
            pe.wait_ge(S("xr_ready"), 1)
            pe.wait_ge(S("gate_ready"), 1)
            for b in range(NB):
                n_k = P * (b + 1)
                for i in range(4):
                    for r in range(2):
                        h = 2 * i + r
                        if b == 0:
                            dst = PS[:, r, i * P:(i + 1) * P]
                        else:
                            dst = PS[:, (4, 2)[r] + i // 2, (i % 2) * T:(i % 2 + 1) * T]
                        pp = slice(64 * r, 64 * r + 64)
                        last = mm(dst, qT[pp, i, b * P:(b + 1) * P], kT[pp, h // 4, 0:n_k], start=True, stop=True)
                last.then_inc(S("s_ps"), 1)
            mod0(4, 6)
            f = 0
            pieces = [(0, [(hh, 0) for hh in range(0, 4)]), (0, [(hh, 0) for hh in range(4, 8)])]
            pieces += [(1, [(hh, kb) for hh in (2 * m, 2 * m + 1) for kb in range(2)]) for m in range(4)]

            def turn_p(f):
                b, part = pieces[f]
                pe.wait_ge(S("p_ready"), b + 1)
                pe.wait_ge(S("s_less_m"), b + 1)
                if f >= 2:
                    pe.wait_ge(S("pT_ready"), f - 1)
                pp = P0 if b == 0 else P1
                for m, (hh, kb) in enumerate(part):
                    last = tr(bank[6 if f % 2 == 0 else 0][:, m * P:(m + 1) * P], pp[:, hh, kb * P:(kb + 1) * P])
                last.then_inc(S("pT_ps"), 1)

            def weigh(f):
                b, part = pieces[f]
                pe.wait_ge(S("pT_ready"), f + 1)
                for m, (hh, kb) in enumerate(part):
                    r, i = hh // 4, hh % 4
                    h = 2 * i + r
                    at = (NQ + NKV) * HEAD + (h // 4) * HEAD
                    last = mm(bank[(1, 4)[b]][64 * r:64 * r + 64, i * P:(i + 1) * P], qkv[:, kb, at:at + HEAD],
                              PT[:, f % 2, m * P:(m + 1) * P], start=kb == 0, stop=kb == b)
                last.then_inc(S("pv_done"), 1)

            turn_p(0)
            for f in range(6):
                if f < 5:
                    turn_p(f + 1)
                weigh(f)
            pe.wait_ge(S("xc_ready"), 1)
            pe.wait_ge(S("gaw_in"), 64)
            for v_ in range(2):
                for j in range(LT):
                    last = mm(PS[:, (2, 5)[v_] + j // 2, (j % 2) * T:(j % 2 + 1) * T], gaw[:, v_, j, :], xc[:, j, :],
                              start=True, stop=True)
            last.then_inc(S("lru_ps"), 1)
            pe.wait_ge(S("lru_ri"), 1)
            pe.wait_ge(S("attn_ready"), 1)
            gate_row(0)
            pe.wait_ge(S("lru_ready"), 1)
            for h in range(2):
                loaded(pe, N_WIN + h)
            for b in range(NB):
                for h in range(2):
                    for k in range(KD):
                        last = mm(bank[2 * b + h], mixT[:, k, b * P:(b + 1) * P], u3(N_WIN + h)[:, k, :],
                                  start=k == 0, stop=k == KD - 1)
                    last.then_inc(S("m_ps"), 1)
            pe.wait_ge(S("m_ps"), 4)
            mod0(6, 12)

            def ffn(L):
                n = 2 * L + 1
                n0 = MOE_BASE[L]
                turn_x(n)
                hT_ready(n)
                if L == 0:
                    pe.wait_ge(S("small_in"), 16 * 9)
                for b in range(NB):
                    for w, at, wd in ((wg_sb, 0, NG), (we_sb, NG, NG * EPG)):
                        for k in range(KD):
                            last = mm(bank[4][:, b * 20 + at:b * 20 + at + wd], hT[:, k, b * P:(b + 1) * P],
                                      w[:, L, k, :], start=k == 0, stop=k == KD - 1)
                last.then_inc(S("router_ps"), 1)
                pe.wait_ge(S("l2_ready"), L + 1)
                oh = rt[:, 48:56].rearrange("p (b g) -> p b g", b=NB)
                mm(bank[5][:, 0:4], before[:, :], oh[:, 0, :], start=True, stop=True)
                mm(bank[5][:, 4:8], before[:, :], oh[:, 1, :], start=True, stop=False)
                mm(bank[5][:, 4:8], ones[:, :], oh[:, 0, :], start=False, stop=True).then_inc(S("rank_ps"), 1)
                pe.wait_ge(S("pick_ready"), L + 1)
                gt = rt[:, 160:168].rearrange("p (b g) -> p b g", b=NB)
                for g in range(NG + 1):
                    for b in range(NB):
                        last = mm(bank[5][:, 16 + 4 * g:20 + 4 * g], pick[:, b, g, :], gt[:, b, :], start=b == 0,
                                  stop=b == NB - 1)
                pe.wait_ge(S("ov_ready"), L + 1)
                ov = rt[:, 192:196].rearrange("p (b n) -> p b n", b=NB)
                for b in range(NB):
                    last = mm(bank[5][:, 40:42], ones[:, :], ov[:, b, :], start=b == 0, stop=b == NB - 1)
                last.then_inc(S("gsl_ps"), 1)

                def gather(i):
                    for k in range(KD):
                        for b in range(NB):
                            last = mm(bank[2 * (k // 4)][:, (k % 4) * P:(k % 4 + 1) * P],
                                      xhat[:, b, k * P:(k + 1) * P], pick[:, b, i, :], start=b == 0, stop=b == NB - 1)
                        if k in (3, 7):
                            last.then_inc(S("gathered"), 1)

                gather(0)
                with pe.Fori(0, NG) as i:
                    e0 = 16 * L + 4 * i

                    def up(e):
                        if e == 0:
                            pe.wait_ge(S("hg_act"), 5 * L + i + 1)
                            pe.wait_ge(S("hg_dve"), 5 * L + i + 1)
                        for w, sem, last_reader, bk in (("w1", "a_ps", "sil_ready", 0), ("w3", "b_ps", "he_ready", 2)):
                            j = AT[(w, e)]
                            loaded(pe, n0 + j, i)
                            if e >= 1 or L == 1:
                                pe.wait_ge(S(last_reader), e0 + e - 1 + PRIMED.get(last_reader, 0))
                            for k in range(KD):
                                last = mm(bank[bk + e % 2], hg[:, k, :], u3(n0 + j)[:, k, :], start=k == 0,
                                          stop=k == KD - 1)
                            last.then_inc(S(sem), 1)

                    def down(e):
                        pe.wait_ge(S("he_ready"), 1 + e0 + e + 1)
                        pe.wait_ge(S("heT_ready"), 1 + e0 + e)
                        for c4 in range(4):
                            last = tr(bank[6][:, c4 * P:(c4 + 1) * P], he[:, e % 2, c4 * P:(c4 + 1) * P])
                        last.then_inc(S("heT_ps"), 1)
                        j = AT[("w2", e)]
                        loaded(pe, n0 + j, i)
                        pe.wait_ge(S("heT_ready"), 1 + e0 + e + 1)
                        if e == 0:
                            pe.wait_ge(S("y_act"), 1 + NG * L + i)
                            pe.wait_ge(S("y_dve"), 1 + NG * L + i)
                        for h in range(2):
                            for c4 in range(KF):
                                last = mm(bank[4 + h], heT[:, e % 2, c4 * P:(c4 + 1) * P],
                                          u3(n0 + j, D)[:, c4, h * HALF:(h + 1) * HALF],
                                          start=e == 0 and c4 == 0, stop=e == EPG - 1 and c4 == KF - 1)
                        last.then_inc(S("y_ps"), 1)

                    up(0)
                    up(1)
                    down(0)
                    up(2)
                    down(1)
                    up(3)
                    down(2)
                    pe.wait_ge(S("sil_ready"), 1 + e0 + 3)
                    pe.wait_ge(S("he_ready"), 1 + e0 + 3)
                    gather(i + 1)
                    down(3)
                    if L == 0:
                        pe.wait_ge(S("gemv_done"), A_HALVES + 6 + 6 * i)
                        pe.wait_ge(S("mod_cols"), 3)
                        pe.wait_ge(S("mod1_evac"), 1 + i)
                        for u in range(3):
                            mod_cols(u, 64 + 4 * u)
                pe.wait_ge(S("he_ready"), 1 + 16 * L + 16)
                pe.wait_ge(S("sil_ready"), 1 + 16 * L + 16)
                pe.wait_ge(S("hg_act"), 5 * L + 5)
                pe.wait_ge(S("hg_dve"), 5 * L + 5)
                for g in range(NG):
                    for b in range(NB):
                        last = tr(bank[g // 2][:, (g % 2) * T + b * P:(g % 2) * T + (b + 1) * P], pick[:, b, g, :])
                last.then_inc(S("pickT_ps"), 1)
                pe.wait_ge(S("y_act"), 1 + NG * (L + 1))
                pe.wait_ge(S("y_dve"), 1 + NG * (L + 1))
                gate_row(n)
                pe.wait_ge(S("pickT_ready"), L + 1)
                for b in range(NB):
                    for h in range(2):
                        for g in range(NG):
                            last = mm(bank[2 * b + h], pickT[:, g, b * P:(b + 1) * P],
                                      yg[:, g, h * HALF:(h + 1) * HALF], start=g == 0, stop=g == NG - 1)
                        last.then_inc(S("sc_ps"), 1)
                pe.wait_ge(S("over_known"), L + 1)
                n_over = pe.value_load(rti[0:1, 0:1], min_val=0, max_val=T)
                with pe.If(n_over > 0):
                    pe.wait_ge(S("x_main"), L + 1)
                    for _ in range(3):
                        pe.sem_inc(S(f"over_used{L}"), 1)
                    with pe.Fori(0, EPG) as e:
                        for j in range(4):
                            pe.wait_ge(S(f"over_in{L}_{j % 3}"), 32 * e + 16 * (j // 3 + 1))
                            w = aring[:, j % 3, :].rearrange("p (k c) -> p k c", c=FF)
                            for kk in range(4):
                                k = (j % 2) * 4 + kk
                                last = mm(bank[(0, 2)[j // 2]], hg[:, k, :], w[:, kk, :], start=k == 0, stop=k == KD - 1)
                            last.then_inc(S(f"over_used{L}"), 1)
                        pe.wait_ge(S(f"over_he{L}"), e + 1)
                        for c4 in range(4):
                            last = tr(bank[6][:, c4 * P:(c4 + 1) * P], he[:, 0, c4 * P:(c4 + 1) * P])
                        last.then_inc(S(f"over_heT{L}"), 1)
                        pe.wait_ge(S(f"over_hT{L}"), e + 1)
                        pe.wait_ge(S(f"over_yg{L}"), 1 + e)
                        for j in range(4, 6):
                            pe.wait_ge(S(f"over_in{L}_{j % 3}"), 32 * e + 16 * (j // 3 + 1))
                            w = aring[:, j % 3, :].rearrange("p (k c) -> p k c", c=D)
                            for h in range(2):
                                for kk in range(2):
                                    c4 = (j - 4) * 2 + kk
                                    last = mm(bank[4 + h], heT[:, 0, c4 * P:(c4 + 1) * P],
                                              w[:, kk, h * HALF:(h + 1) * HALF], start=c4 == 0, stop=c4 == KF - 1)
                            last.then_inc(S(f"over_used{L}"), 1)
                    pe.wait_ge(S(f"over_yg{L}"), 1 + EPG)
                    for b in range(NB):
                        last = tr(bank[6][:, b * P:(b + 1) * P], pick[:, b, NG, :])
                    last.then_inc(S(f"over_pT{L}"), 1)
                    pe.wait_ge(S(f"over_pick{L}"), 1)
                    for b in range(NB):
                        for h in range(2):
                            last = mm(bank[2 * b + h], pickT[:, 0, b * P:(b + 1) * P],
                                      yg[:, 0, h * HALF:(h + 1) * HALF], start=True, stop=True)
                    last.then_inc(S(f"over_sc{L}"), 1)
                pe.wait_ge(S("x_new"), 2 * L + 2)

            ffn(0)

            pe.wait_ge(S("s5_rows"), 1)
            for m, r in enumerate((7, 8, 9, 10, 11)):
                last = tr(bank[4][:, m * NQT:(m + 1) * NQT], s5r[0:NQT, r, :], NQT)
            last.then_inc(S("s5_cols_ps"), 1)
            pe.wait_ge(S("bp_ready"), 4)
            for v_ in range(2):
                for hf in range(2):
                    if v_:
                        pe.wait_ge(S("bt_evac"), 1 + hf)
                    for kk in range(4):
                        last = tr(bank[5 + hf][:, kk * P:(kk + 1) * P], Bp[:, v_, hf * 4 + kk, :])
                    last.then_inc(S("bt_ps"), 1)
            for v_ in range(2):
                for hf in range(2):
                    if v_:
                        pe.wait_ge(S("ct_evac"), 2 + 2 * hf)
                    for kk in range(4):
                        last = tr(bank[hf * 2 + 1][:, kk * P:(kk + 1) * P], Cn[:, v_, hf * 4 + kk, :])
                    last.then_inc(S("ct_ps"), 1)
            pe.wait_ge(S("bt_ready"), 1)
            pe.wait_ge(S("ct_evac"), 8)
            turn_x(2)
            gate_row(2)
            pe.wait_ge(S("grow_ready"), 3)
            hT_ready(2)
            with pe.Fori(0, KD) as k:
                pe.wait_ge(S("cur_ready"), k + 1)
                for q4 in range(4):
                    if q4 % 2 == 0:
                        pe.wait_ge(S("bu_used"), 1 + 2 * k)
                    pp = slice(32 * q4, 32 * q4 + 32)
                    for m in range(2):
                        last = mm(PS[:, q4, m * T:(m + 1) * T], bcur[pp, m, :], ucur[pp, :], start=True, stop=True)
                    last.then_inc(S("bu_ready"), 1)
                pe.wait_ge(S("yv_ready"), 1 + k)
                for j in range(2):
                    pe.wait_ge(S("q_ready"), 1 + 2 * k + j + 1)
                    for q_ in range(2):
                        q4 = 2 * j + q_
                        for m in range(4):
                            last = mm(bank[4][32 * q4:32 * q4 + 32, 0:T], ccur[:, m // 2, 32 * q4:32 * q4 + 32],
                                      qq[:, m, q_ * T:(q_ + 1) * T], start=m == 0, stop=m == 3)
                    last.then_inc(S("q_used"), 1)
            pe.wait_ge(S("act_ready"), 1 + KD)
            pe.wait_ge(S("glub_in"), 16)
            for h in range(2):
                for part in range(2):
                    n = GLU_BASE + 2 * h + part
                    loaded(pe, n)
                    r = h + 2 * part
                    for b in range(NB):
                        dst = bank[4 * h + 2 * part + b]
                        mm(dst, bcol(ident[0:4, r:r + 1]), glub, start=True, stop=False)
                        for k in range(KD):
                            last = mm(dst, actT[:, k, b * P:(b + 1) * P], u3(n)[:, k, :], start=False, stop=k == KD - 1)
                    last.then_inc(S("glu_ps"), 1)
            pe.wait_ge(S("x_new"), 3)
            ffn(1)


_OUT = (1, T, D)


def kernel(**inputs):
    import numpy as np
    import concourse.bacc as bacc
    from concourse.bass_utils import run_bass_kernel_spmd

    nc = bacc.Bacc("TRN2", target_bir_lowering=False, num_devices=1)
    arrays, a = {}, {}
    for name, value in inputs.items():
        value = np.ascontiguousarray(value)
        arrays[f"in_{name}"] = value
        a[name] = nc.dram_tensor(f"in_{name}", value.shape, mybir.dt.from_np(value.dtype), kind="ExternalInput").ap()
    out = nc.dram_tensor("out", _OUT, F32, kind="ExternalOutput").ap()
    build(nc, a, out)
    r = run_bass_kernel_spmd(nc, [arrays], core_ids=[0])
    return r.results[0]["out"]
```

```python
from contextlib import ExitStack

import concourse.bass as bass
from concourse import mybir

F32 = mybir.dt.float32
I32 = mybir.dt.int32
ALU = mybir.AluOpType
ACT = mybir.ActivationFunctionType
AX = mybir.AxisListType

P = 128
D = 1024
T = 256
NB = T // P
KD = D // P
HALF = 512
CHUNK = 64
HEAD = 64
NQ, NKV = 8, 2
ROT = HEAD // 4
RH = ROT // 2
LRU = 512
LT = LRU // P
CONV = 4
IN_W = NQ * HEAD + 2 * NKV * HEAD + 2 * LRU
NG, EPG = 4, 4
FF = 512
KF = FF // P
EPS = 1e-6
SCALE = HEAD ** -0.5
ROPE_THETA = 500000.0
STATE, CH = 64, 16
NQT = 32
PI = 3.14159265358979
MAGIC = 12582912.0
TWO_PI = (6.28125, 0.0019340515136718750, 1.2556659817695618e-06)

SLOTS = 6
SLOT = 4096
ASLOTS = 2
ASLOT = 2048
N_WIN, N_WOUT, N_GLU = 4, 2, 4
PER_GROUP = 3 * EPG
N_MOE = NG * PER_GROUP
MOE_BASE = (N_WIN + N_WOUT, N_WIN + N_WOUT + N_MOE + N_GLU)
GLU_BASE = N_WIN + N_WOUT + N_MOE
ORDER = [("w1", 0), ("w3", 0), ("w1", 1), ("w3", 1), ("w2", 0), ("w1", 2), ("w3", 2), ("w2", 1),
         ("w1", 3), ("w3", 3), ("w2", 2), ("w2", 3)]
AT = {key: n for n, key in enumerate(ORDER)}
A_HALVES = 24
A_UNITS = 12
RING_ADA = (0, 1, 4, 5)
A_HALF0 = [2 * u + kh for u in range(A_UNITS) if u not in RING_ADA for kh in range(2)]
GEMV_OF = (2, 1, 2, 1)
SH_M, SC_M, G_M, SH_F, SC_F, G_F = range(6)

PRIMED = dict.fromkeys(('bu_ready', 'q_used', 'yv_ready', 'q_ready', 'bu_used', 'he_ready', 'y_dve', 'mod1_evac', 'over_yg0', 'over_yg1', 'act_ready', 'heT_ready', 'y_act', 'sil_ready'), 1)
PRIMED.update(q_used=2, q_ready=2)

ROWS = {}
_at = 0
for _name, _n in (("mix0", KD), ("ffn0", KD), ("mix1", KD), ("ffn1", KD), ("s5d", KD),
                  ("conv_w", CONV * LT), ("conv_b", LT), ("ga_b", LT), ("gx_b", LT), ("lam", LT)):
    ROWS[_name] = (_at, _n)
    _at += _n
N_ROWS = _at
WORK = 15744


class Chain:

    def __init__(self, eng, sem):
        self.eng, self.sem, self.n, self.off = eng, sem, 0, 0

    def link(self, ins):
        ins.then_inc(self.sem, 1)
        self.n += 1
        self.eng.wait_ge(self.sem, self.off + self.n)

    def enter(self, i, per):
        self.off, self.start, self.per = i * per, self.n, per

    def leave(self, turns):
        assert self.n - self.start == self.per, (self.n - self.start, self.per)
        self.n, self.off = self.start + self.per * turns, 0


def build(nc, a, out):
    ctx = ExitStack()
    with ctx:
        def sb(name, shape, dt=F32):
            return ctx.enter_context(nc.sbuf_tensor(name, shape, dt))

        sems = {}

        def S(name):
            if name not in sems:
                sems[name] = ctx.enter_context(nc.semaphore(name))
            return sems[name]

        ring = sb("ring", [P, SLOTS, SLOT])
        x = sb("x", [P, NB, D])
        xhat = sb("xhat", [P, NB, D])
        hT = sb("hT", [P, KD, T])
        yg = sb("yg", [P, NG, D])
        grow = sb("grow", [P, D])
        ident = sb("ident", [P, P])
        ones = sb("ones", [P, P])
        before = sb("before", [P, P])
        slot_no = sb("slot_no", [P, P])
        cols = sb("cols", [P, N_ROWS])
        mod = sb("mod", [P, 2, 6, KD])
        modA = sb("modA", [P, 4, KD])
        adab = sb("adab", [P, 2, 6 * KD])
        stat = sb("stat", [P, 8])
        condc = sb("condc", [P, KD])
        wr_sb = sb("wr_sb", [P, 2, KD, NG + NG * EPG])
        rb = sb("rb", [P, 2, NG + NG * EPG])
        rt = sb("rt", [P, 320])
        rti = sb("rti", [P, 2], I32)
        work = sb("work", [P, WORK])
        PS = ctx.enter_context(nc.psum_tensor("PS", [P, 8, HALF], F32))
        bank = [PS[:, i, :] for i in range(8)]

        def w3(off, *dims):
            n = 1
            for d in dims:
                n *= d
            v = work[:, off:off + n]
            if len(dims) == 1:
                return v
            names = " ".join("abcd"[:len(dims)])
            return v.rearrange(f"p ({names}) -> p {names}", **dict(zip("abcd", dims)))

        aring = w3(0, ASLOTS, ASLOT)
        acc = w3(ASLOTS * ASLOT, 3, HALF)
        W0 = ASLOTS * ASLOT + 3 * HALF
        T0 = WORK - 3 * 2 * KD * P - 5 * NQT
        rows = yg[0:N_ROWS, 0, 0:P]
        crow = yg[0:KD, 0, P:2 * P]
        brow = yg[0:6 * KD, 1, 0:2 * P].rearrange("r (l p) -> r l p", l=2)
        o = W0
        qkv = w3(o, NB, 768); o += NB * 768
        qT = w3(o, 4, T); o += 4 * T
        kT = w3(o, NKV, T); o += NKV * T
        xr = w3(o, LT, T); o += LT * T
        xc = w3(o, LT, T); o += LT * T
        gate = w3(o, LT, T); o += LT * T
        gaw = w3(o, 2, LT, P); o += 2 * LT * P
        rope = w3(o, 8, NB * RH); o += 8 * NB * RH
        rq = w3(o, 4, 10 * RH); o += 4 * 10 * RH
        smx = w3(o, 5, NB * NQ); o += 5 * NB * NQ
        sink = w3(o, NQ); o += NQ
        sp = w3(o, 4, LT); o += 4 * LT
        assert o <= WORK - 4 * NQT * 16, o
        mixT = yg[:, 0:2, :].rearrange("p a (k t) -> p (a k) t", t=T)
        lr_r = yg[:, 2, :].rearrange("p (k t) -> p k t", t=T)
        lr_i = yg[:, 3, :].rearrange("p (k t) -> p k t", t=T)
        P0 = hT[:, 0:4, :].rearrange("p k t -> p (k t)").rearrange("p (h n) -> p h n", n=P)
        PT = hT[:, 4:8, :].rearrange("p k t -> p (k t)").rearrange("p (s n) -> p s n", n=HALF)
        P1 = xhat[:, :, :].rearrange("p b n -> p (b n)").rearrange("p (h n) -> p h n", n=T)
        k2 = xhat[:, 0, 0:HALF].rearrange("p (b n) -> p b n", b=NB)
        lr_t = xhat[:, 0, :].rearrange("p (k t) -> p k t", t=T)
        lr_u = xhat[:, 1, :].rearrange("p (k t) -> p k t", t=T)
        o = W0
        pick = w3(o, NB, NG + 1, P); o += NB * (NG + 1) * P
        sil = w3(o, HALF); o += HALF
        he = w3(o, HALF); o += HALF
        heT = w3(o, HALF); o += HALF
        gsl = w3(o, NG + 1, EPG); o += (NG + 1) * EPG
        gcur = w3(o, EPG); o += EPG
        assert o <= T0, o
        hg = hT[:, 0:4, :].rearrange("p k t -> p (k t)").rearrange("p (k s) -> p k s", s=P)
        pickT = hT[:, 4:8, :].rearrange("p k t -> p (k t)").rearrange("p (g t) -> p g t", t=T)
        o = T0
        BT = w3(o, 2, KD, P); o += 2 * KD * P
        CT = w3(o, 2, KD, P); o += 2 * KD * P
        s5c = w3(o, 5, NQT); o += 5 * NQT
        E = w3(o, 4, NQT, 16)
        Bl = w3(o, 2, NQT, CH)
        s5i = w3(o + 2 * NQT * CH, 3, P)
        o += 4 * NQT * 16
        assert o == WORK
        o = W0
        s5r = w3(o, 20, P); o += 20 * P
        bt1 = w3(o, NQT, CH); o += NQT * CH
        bt2 = w3(o, NQT, CH); o += NQT * CH
        Ew = w3(o, 5, NQT); o += 5 * NQT
        assert o <= T0, o
        Bp = hT[:, :, :].rearrange("p k t -> p (k t)").rearrange("p (v k n) -> p v k n", v=2, n=P)
        Et = xhat[:, 1, :].rearrange("p (v n) -> p v n", v=4)
        Cn = yg[:, 2:4, :].rearrange("p v (k n) -> p v k n", n=P)
        o = 0
        cs = w3(o, 2, 2, HALF); o += 4 * HALF
        pr = w3(o, 4, HALF); o += 4 * HALF
        gg = w3(o, 2, HALF); o += 2 * HALF
        q_a = w3(o, 4, HALF); o += 4 * HALF
        bcur = w3(o, 2, 2, P); o += 4 * P
        ccur = w3(o, 2, 2, P); o += 4 * P
        ucur = w3(o, 2, T); o += 2 * T
        yv = w3(o, T); o += T
        dcur = w3(o, 2); o += 2
        assert o <= T0, o
        qq = [q_a, xhat[:, :, :].rearrange("p b (h n) -> p (b h) n", n=HALF)]
        ctmp = yg[:, 1, :].rearrange("p (v n) -> p v n", v=2)
        actT = yg[:, 2:4, :].rearrange("p a (k t) -> p (a k) t", t=T)
        glub = yg[0:4, 0, 0:HALF]
        fing = hT[:, 0:4, :].rearrange("p k t -> p (k t)")

        def col(name, k):
            at, n = ROWS[name]
            return cols[:, at + k:at + k + 1]

        def unit_dst(n):
            return ring[:, n % SLOTS, :]

        def loaded(eng, n, i=None):
            v = 16 * (n // SLOTS + 1)
            eng.wait_ge(S(f"loaded{n % SLOTS}"), v if i is None else v + i * (16 * PER_GROUP // SLOTS))

        def u3(n, c=HALF):
            return ring[:, n % SLOTS, :].rearrange("p (k c) -> p k c", c=c)

        ada_v = a["ada_w"].rearrange("l (k p) n -> l p k n", p=P)
        w1_v = a["moe_w1"].rearrange("l e (k p) f -> l p e k f", p=P)
        w3_v = a["moe_w3"].rearrange("l e (k p) f -> l p e k f", p=P)
        w2_v = a["moe_w2"].rearrange("l e (k p) n -> l p e k n", p=P)
        moe_v = {"w1": w1_v, "w3": w3_v, "w2": w2_v}
        MAXG = NG - 1

        def moe_src(L, w, e):
            return moe_v[w][L, :, e, :, :]

        block = ctx.enter_context(nc.Block())

        @block.sync
        def _(sp_):
            reader = {0: ("q_ps", 2), 1: ("xr_ps", 1), 2: ("gate_ps", 1), 3: ("gate_ps", 2), 4: ("m_ps", 3),
                      5: ("m_ps", 4)}
            reader.update({GLU_BASE + j: ("glu_ps", j + 1) for j in range(N_GLU)})
            signal = {"w1": "a_ps", "w3": "b_ps", "w2": "y_ps"}

            def free_slot(n):
                m = n - SLOTS
                if m < 0:
                    return
                if m in reader:
                    sp_.wait_ge(S(reader[m][0]), reader[m][1])
                else:
                    L = int(m >= MOE_BASE[1])
                    w, e = ORDER[(m - MOE_BASE[L]) % PER_GROUP]
                    sp_.wait_ge(S(signal[w]), 16 * L + EPG * ((m - MOE_BASE[L]) // PER_GROUP) + e + 1)

            def send(n, src, c, width):
                free_slot(n)
                sp_.dma_start(u3(n, c)[:, :, 0:width], src).then_inc(S(f"loaded{n % SLOTS}"), 16)

            def send_expert(L, j, group):
                w, e = ORDER[j]
                sp_.dma_start(u3(MOE_BASE[L] + j, D if w == "w2" else FF), moe_src(L, w, group * EPG + e)).then_inc(
                    S(f"loaded{(MOE_BASE[L] + j) % SLOTS}"), 16)

            def send_ada(u):
                sp_.dma_start(u3(N_WIN + u % 2), ada_v[0, :, :, u * HALF:(u + 1) * HALF]).then_inc(
                    S(f"ada_ring{u % 2}"), 16)

            win = a["ab_w_in"][0].rearrange("(k p) n -> p k n", p=P)
            for u in RING_ADA[0:2]:
                send_ada(u)
            for j in range(N_WIN):
                w = min(HALF, IN_W - j * HALF)
                send(j, win[:, :, j * HALF:j * HALF + w], HALF, w)
                if j in (1, 2):
                    sp_.wait_ge(S("gemv_done"), 2 * j)
                    send_ada(RING_ADA[1 + j])
            wout = a["ab_w_out"][0].rearrange("(k p) n -> p k n", p=P)
            for j in range(N_WOUT):
                sp_.wait_ge(S("gemv_done"), 2 * RING_ADA[2 + j] + 2)
                send(N_WIN + j, wout[:, :, j * HALF:(j + 1) * HALF], HALF, HALF)
            for L in range(2):
                n0 = MOE_BASE[L]
                for j in range(SLOTS):
                    free_slot(n0 + j)
                    send_expert(L, j, 0)
                with sp_.Fori(0, NG - 1) as i:
                    for half in range(2):
                        for j in range(SLOTS):
                            w, e = ORDER[j + (0 if half == 0 else SLOTS)]
                            sp_.wait_ge(S(signal[w]), 16 * L + e + 1 + i * EPG)
                            send_expert(L, j + (SLOTS if half == 0 else 0), i + half)
                for j in range(SLOTS, PER_GROUP):
                    free_slot(n0 + (NG - 1) * PER_GROUP + j)
                    send_expert(L, j, NG - 1)
                sp_.wait_ge(S("over_known"), L + 1)
                n_over = sp_.value_load(rti[0:1, 0:1], min_val=0, max_val=T)
                grp = sp_.value_load(rti[0:1, 1:2], min_val=0, max_val=MAXG)
                with sp_.If(n_over > 0):
                    with sp_.Fori(0, EPG) as e:
                        for j, w in enumerate(("w1", "w3", "w2")):
                            sp_.wait_ge(S(f"over_used{L}"), e * 3 + (j + 1))
                            cw = D if w == "w2" else FF
                            sp_.dma_start(u3(j, cw), moe_src(L, w, grp * EPG + e)).then_inc(S(f"over_in{L}_{j}"), 16)
                if L == 0:
                    glu = a["s5_glu_w"][0].rearrange("(k p) n -> p k n", p=P)
                    for j, q in enumerate((0, 2, 1, 3)):
                        send(GLU_BASE + j, glu[:, :, q * HALF:(q + 1) * HALF], HALF, HALF)
            for b in range(NB):
                sp_.wait_ge(S("out_ready"), b + 1)
                sp_.dma_start(out[0, b * P:(b + 1) * P, :], xhat[:, b, :]).then_inc(S("out_stored"), 16)
            sp_.wait_ge(S("out_stored"), 16 * NB)

        @block.gpsimd
        def _(pool):
            g = nc.gpsimd
            ch = Chain(pool, S("pool_order"))
            ch.link(g.memset(ident[:, :], 0.0))
            g.affine_select(out=ident[:, :], in_=ident[:, :], compare_op=ALU.not_equal, fill=1.0, base=0,
                            pattern=[[-1, P]], channel_multiplier=1).then_inc(S("ident_ready"), 1)

            def ada_load(h, j, wait):
                L, r = h
                if wait is not None:
                    pool.wait_ge(S("gemv_done"), wait)
                u, kh = r // 2, r % 2
                pool.dma_start(aring[:, j % ASLOTS, :].rearrange("p (k c) -> p k c", c=HALF),
                               ada_v[L, :, kh * 4:kh * 4 + 4, u * HALF:(u + 1) * HALF]).then_inc(
                                   S(f"ada_in{j % ASLOTS}"), 16)

            for j, r in enumerate(A_HALF0[:ASLOTS]):
                ada_load((0, r), j, None)
            ch.link(g.memset(ones[:, :], 1.0))
            ch.link(g.affine_select(out=before[:, :], in_=ones[:, :], compare_op=ALU.is_gt, fill=0.0, base=0,
                                    pattern=[[1, P]], channel_multiplier=-1))
            g.iota(slot_no[:, :], pattern=[[1, P]], base=0, channel_multiplier=0,
                   allow_small_or_imprecise_dtypes=True).then_inc(S("consts_ready"), 1)
            ch.link(g.memset(gaw[:, :, :, :], 0.0))
            for v, name in enumerate(("ab_gate_a_w", "ab_gate_x_w")):
                src = a[name][0].rearrange("(k b) d e -> b d k e", b=2)
                for b in range(2):
                    pool.dma_start(gaw[b * 64:(b + 1) * 64, v, :, b * 64:(b + 1) * 64], src[b]).then_inc(
                        S("gaw_in"), 16)
            for j, r in enumerate(A_HALF0):
                if j >= ASLOTS:
                    ada_load((0, r), j, A_HALF0[j - ASLOTS] + 1)
            with pool.Fori(0, NG) as i:
                for j in range(6):
                    u, kh = j // 2, j % 2
                    pool.wait_ge(S("gemv_done"), A_HALVES + j - ASLOTS + 1 + i * 6)
                    src = ada_v[1, :, kh * 4:kh * 4 + 4, bass.ds(i * (3 * HALF) + u * HALF, HALF)]
                    pool.dma_start(aring[:, j % ASLOTS, :].rearrange("p (k c) -> p k c", c=HALF), src).then_inc(
                        S(f"ada_in{j % ASLOTS}"), 16)

            pool.wait_ge(S("x_new"), 2)
            with pool.Fori(0, KD) as k:
                for j in range(2):
                    if j == 0:
                        pool.wait_ge(S("q_ready"), 1 + 2 * k)
                    else:
                        pool.wait_ge(S("q_ready"), 2 + 2 * k)
                    q0 = 4 * k + 2 * j
                    e1c, e1s, e2c, e2s = [E[:, v, bass.ds(q0, 2), :] for v in range(4)]

                    def outer(v):
                        return v.unsqueeze(3).to_broadcast([P, 2, 16, 16])

                    def inner(v):
                        return v.unsqueeze(2).to_broadcast([P, 2, 16, 16])

                    def t4(v):
                        return v.rearrange("p (q a j) -> p q a j", q=2, a=16)

                    n_tab = 4 * k + 2 * j
                    c_, s_ = cs[:, j, 0, :], cs[:, j, 1, :]
                    g.tensor_tensor(t4(c_), outer(e1c), inner(e2c), ALU.mult)
                    g.tensor_tensor(t4(ctmp[:, 0, :]), outer(e1s), inner(e2s), ALU.mult).then_inc(S("tab_step"), 1)
                    pool.wait_ge(S("tab_step"), n_tab + 1)
                    g.tensor_tensor(c_, c_, ctmp[:, 0, :], ALU.subtract)
                    g.tensor_tensor(t4(s_), outer(e1s), inner(e2c), ALU.mult)
                    g.tensor_tensor(t4(ctmp[:, 1, :]), outer(e1c), inner(e2s), ALU.mult).then_inc(S("tab_step"), 1)
                    pool.wait_ge(S("tab_step"), n_tab + 2)
                    g.tensor_tensor(s_, s_, ctmp[:, 1, :], ALU.add).then_inc(S("tab_ready"), 1)

        @block.scalar
        def _(act):
            s = nc.scalar
            for name in ('act_ready', 'heT_ready', 'y_act', 'sil_ready'):
                act.sem_inc(S(name), PRIMED[name])
            ch = Chain(act, S("act_order"))
            act.dma_start(crow, a["c"][0].rearrange("(k p) -> k p", p=P)).then_inc(S("c_in"), 16)
            act.dma_start(x[:, :, :], a["x"][0].rearrange("(b p) n -> p b n", p=P)).then_inc(S("x_in"), 16)
            names = {"mix0": a["norm_mix_g"][0:1], "ffn0": a["norm_ffn_g"][0:1],
                     "mix1": a["norm_mix_g"][1:2], "ffn1": a["norm_ffn_g"][1:2],
                     "conv_b": a["ab_conv_b"], "ga_b": a["ab_gate_a_b"], "gx_b": a["ab_gate_x_b"],
                     "lam": a["ab_lambda"]}
            for name, (at, n) in ROWS.items():
                dst = rows[at:at + n, :]
                if name == "s5d":
                    src = a["s5_d"][0].rearrange("(k g) c -> k (g c)", k=KD)
                elif name == "conv_w":
                    src = a["ab_conv_w"][0].rearrange("j (k p) -> (j k) p", p=P)
                else:
                    src = names[name][0].rearrange("(k p) -> k p", p=P)
                act.dma_start(dst, src).then_inc(S("rows_in"), 16)
            for L in range(2):
                act.dma_start(brow[:, L, :], a["ada_b"][L].rearrange("(r p) -> r p", p=P)).then_inc(S("rows_in"), 16)
            act.dma_start(rti[:, 0:NB], a["positions"][0].rearrange("(b p) -> p b", p=P),
                          allow_slow_non_contiguous=True).then_inc(S("pos_in"), 16)
            act.dma_start(sink[:, :], a["ab_sinks"].to_broadcast([P, NQ])).then_inc(S("small_in"), 16)
            for L in range(2):
                act.dma_start(wr_sb[:, L, :, 0:NG], a["moe_wg"][L].rearrange("(k p) g -> p k g", p=P)).then_inc(S("small_in"), 16)
                act.dma_start(wr_sb[:, L, :, NG:], a["moe_we"][L].rearrange("(k p) g e -> p k (g e)", p=P)).then_inc(
                    S("small_in"), 16)
                act.dma_start(rb[:, L, 0:NG], a["moe_bg"][L:L + 1].to_broadcast([P, NG])).then_inc(S("small_in"), 16)
                act.dma_start(rb[:, L, NG:], a["moe_be"][L:L + 1].rearrange("l g e -> l (g e)").to_broadcast(
                    [P, NG * EPG])).then_inc(S("small_in"), 16)

            s5_rows = a["s5_a_re"][0].rearrange("(q g) p -> q (g p)", g=2)
            s.dma_start(s5i[0:NQT, 0, :], s5_rows).then_inc(S("s5_in"), 16)
            s.dma_start(s5i[0:NQT, 1, :], a["s5_a_im"][0].rearrange("(q g) p -> q (g p)", g=2)).then_inc(S("s5_in"), 16)
            s.dma_start(s5i[0:NQT, 2, 0:2], a["s5_log_dt"][0].rearrange("(q g) -> q g", g=2)).then_inc(S("s5_in"), 16)
            for v, name in enumerate(("s5_b_re", "s5_b_im")):
                s.dma_start(Bl[:, v, :, :], a[name][0].rearrange("(q g) p c -> (g p) q c", g=2)).then_inc(S("s5_in"), 16)
            act.wait_ge(S("c_ps"), 1)
            s.activation(condc[:, :], bank[2][:, 0:KD], ACT.Silu).then_inc(S("cond_ready"), 1)
            act.wait_ge(S("cols_ps"), 1)
            ch.link(s.activation(cols[:, :], bank[0][:, 0:N_ROWS], ACT.Copy))
            s.activation(adab[:, :, :], bank[1][:, 0:12 * KD].rearrange("p (l n) -> p l n", l=2), ACT.Copy).then_inc(
                S("cols_ready"), 1)

            def norm(n):
                if n == 0:
                    act.wait_ge(S("x_in"), 16)
                else:
                    act.wait_ge(S("x_new"), n)
                s.activation(xhat[:, 0, :], x[:, 0, :], ACT.Square, accum_out=stat[:, 0:1]).then_inc(S("ss_act"), 1)
                act.wait_ge(S("var_ready"), n + 1)
                s.activation(stat[:, 4:6], stat[:, 2:4], ACT.Sqrt).then_inc(S("std_ready"), 1)

            def modulate(n):
                L, sec = n // 2, (SH_M if n % 2 == 0 else SH_F)
                act.wait_ge(S("modA_ready"), n + 1)
                for k in (0, 1, 4, 5):
                    act.wait_ge(S("xT_ps"), 4 * n + k // 2 + 1)
                    s.activation(hT[:, k, :], bank[k // 2][:, (k % 2) * T:(k % 2 + 1) * T], ACT.Identity, scale=modA[:, n, k:k + 1],
                                 bias=mod[:, L, sec, k:k + 1]).then_inc(S("hT_act"), 1)

            def gate_row(n):
                act.wait_ge(S("grow_ps"), n + 1)
                if n:
                    act.wait_ge(S("x_new"), n)
                s.activation(grow[:, 0:HALF], bank[4], ACT.Copy)
                s.activation(grow[:, HALF:], bank[5], ACT.Copy).then_inc(S("grow_ready"), 1)

            act.wait_ge(S("rope_arg"), 1)
            s.activation(rope[:, 4:6, :], rope[:, 2:4, :], ACT.Sin).then_inc(S("rope_ready"), 1)
            act.wait_ge(S("sp_arg"), 1)
            ch.link(s.activation(sp[:, 1, :], sp[:, 0, :], ACT.Exp))
            ch.link(s.activation(sp[:, 1, :], sp[:, 1, :], ACT.Ln, bias=1.0))
            s.activation(sp[:, 1, :], sp[:, 1, :], ACT.Copy).then_inc(S("sp_ln"), 1)

            norm(0)
            modulate(0)
            for b in range(NB):
                act.wait_ge(S("q_ps"), b + 1)
                s.activation(qkv[:, b, 0:HALF], bank[4 + b], ACT.Copy).then_inc(S("q_evac"), 1)
            act.wait_ge(S("xr_ps"), 1)
            s.activation(xr[:, 0:2, :], bank[0].rearrange("p (j t) -> p j t", j=2), ACT.Copy)
            act.wait_ge(S("xr_ps"), 2)
            s.activation(xr[:, 2:4, :], bank[1].rearrange("p (j t) -> p j t", j=2), ACT.Copy).then_inc(S("xr_ready"), 1)
            act.wait_ge(S("gate_ps"), 2)
            s.activation(gate[:, :, :], PS[:, 2:4, :].rearrange("p b (j t) -> p (b j) t", j=2),
                         ACT.Gelu_apprx_tanh).then_inc(S("gate_ready"), 1)
            act.wait_ge(S("qT_ps"), 1)
            s.activation(qT[:, :, :], PS[:, 4:6, :].rearrange("p b (j t) -> p (b j) t", j=2), ACT.Copy).then_inc(
                S("qT_ready"), 1)
            for b in range(NB):
                act.wait_ge(S("s_less_m"), b + 1)
                if b == 0:
                    s.activation(P0[0:64, :, 0:64], P0[0:64, :, 0:64], ACT.Exp, scale=SCALE)
                    s.activation(P0[64:P, :, 0:P], P0[64:P, :, 0:P], ACT.Exp, scale=SCALE)
                else:
                    s.activation(P1[0:64, :, 64:192], P1[0:64, :, 64:192], ACT.Exp, scale=SCALE)
                    s.activation(P1[64:P, :, P:T], P1[64:P, :, P:T], ACT.Exp, scale=SCALE)
                s.activation(smx[:, 2, b * NQ:(b + 1) * NQ], smx[:, 1, b * NQ:(b + 1) * NQ], ACT.Exp,
                             scale=SCALE).then_inc(S("p_exp"), 1)
            for f in range(6):
                act.wait_ge(S("pT_ps"), f + 1)
                if f >= 2:
                    act.wait_ge(S("pv_done"), f - 1)
                s.activation(PT[:, f % 2, :], bank[6 if f % 2 == 0 else 0], ACT.Copy).then_inc(S("pT_ready"), 1)
            act.wait_ge(S("pv_done"), 2)
            s.activation(mixT[:, 0:4, 0:P], bank[1].rearrange("p (i t) -> p i t", i=4), ACT.Copy)
            act.wait_ge(S("pv_done"), 6)
            s.activation(mixT[:, 0:4, P:T], bank[4].rearrange("p (i t) -> p i t", i=4), ACT.Copy).then_inc(
                S("attn_ready"), 1)
            act.wait_ge(S("lru_ps"), 1)
            for j in range(LT):
                s.activation(lr_r[:, j, :], PS[:, 2 + j // 2, (j % 2) * T:(j % 2 + 1) * T], ACT.Sigmoid,
                             bias=col("ga_b", j))
            for j in range(LT):
                last = s.activation(lr_i[:, j, :], PS[:, 5 + j // 2, (j % 2) * T:(j % 2 + 1) * T], ACT.Sigmoid,
                                    bias=col("gx_b", j))
            last.then_inc(S("lru_ri"), 1)
            act.wait_ge(S("lru_ri"), 1)
            act.wait_ge(S("sp_ready"), 1)
            for j in range(LT):
                s.activation(lr_t[:, j, :], lr_r[:, j, :], ACT.Tanh, scale=sp[:, 2, j:j + 1])
            for j in range(LT):
                last = s.activation(lr_u[:, j, :], lr_r[:, j, :], ACT.Exp, scale=sp[:, 3, j:j + 1])
            last.then_inc(S("lru_a"), 1)
            act.wait_ge(S("lru_b2"), 1)
            s.activation(lr_t[:, :, :], lr_t[:, :, :], ACT.Sqrt).then_inc(S("lru_sq"), 1)
            gate_row(0)

            act.wait_ge(S("lru_ready"), 1)
            for v, name in enumerate(("s5_c_re", "s5_c_im")):
                for u in range(2):
                    s.dma_start(Cn[:, v, :, u * 64:(u + 1) * 64],
                                a[name][0].rearrange("(k g) c p -> (g c) k p", k=KD)).then_inc(S("cn_in"), 16)
            act.wait_ge(S("s5_in"), 16 * 5)
            act.wait_ge(S("pv_done"), 6)
            R = s5r
            s.activation(R[0:NQT, 4, 0:2], s5i[0:NQT, 2, 0:2], ACT.Exp).then_inc(S("dt_ready"), 1)
            act.wait_ge(S("s5_th"), 1)
            s.activation(R[0:NQT, 7, :], R[0:NQT, 5, :], ACT.Exp)
            s.activation(R[0:NQT, 8:10, :], R[0:NQT, 10:12, :], ACT.Sin).then_inc(S("s5_trig"), 1)
            for v in range(2):
                for hf in range(2):
                    act.wait_ge(S("bt_ps"), 2 * v + hf + 1)
                    s.activation(BT[:, v, hf * 4:hf * 4 + 4, :], bank[4 + hf].rearrange("p (k n) -> p k n", n=P),
                                 ACT.Copy).then_inc(S("bt_evac"), 1)

            def ffn(L):
                n = 2 * L + 1
                norm(n)
                modulate(n)
                act.wait_ge(S("lg_ready"), L + 1)
                s.activation(rt[:, 64:64 + 8], rt[:, 56:56 + 8], ACT.Exp).then_inc(S("eg_ready"), 1)
                act.wait_ge(S("l2_ready"), L + 1)
                s.activation(rt[:, 86:88], rt[:, 84:86], ACT.Exp).then_inc(S("e2_ready"), 1)
                n0 = MOE_BASE[L]

                def hg_evac(i):
                    act.wait_ge(S("gathered"), 10 * L + 1 + 2 * i)
                    for k in range(0, 4):
                        last = s.activation(hg[:, k, :], bank[0][:, k * P:(k + 1) * P], ACT.Identity,
                                            scale=modA[:, n, k:k + 1], bias=mod[:, L, SH_F, k:k + 1])
                    last.then_inc(S("hg_act"), 1)

                hg_evac(0)
                with act.Fori(0, NG) as i:
                    def silu(e):
                        act.wait_ge(S("a_ps"), 16 * L + 4 * i + e + 1)
                        act.wait_ge(S("he_ready"), 1 + 16 * L + 4 * i + e)
                        s.activation(sil[:, :], bank[0 + e % 2], ACT.Silu).then_inc(S("sil_ready"), 1)

                    def he_t(e):
                        act.wait_ge(S("heT_ps"), 16 * L + 4 * i + e + 1)
                        s.activation(heT[:, :], bank[6], ACT.Copy).then_inc(S("heT_ready"), 1)

                    silu(0)
                    silu(1)
                    he_t(0)
                    silu(2)
                    he_t(1)
                    silu(3)
                    he_t(2)
                    hg_evac(i + 1)
                    he_t(3)
                    act.wait_ge(S("y_ps"), 16 * L + 4 * i + 4)
                    s.activation(yg[:, bass.ds(i, 1), 0:HALF], bank[4].unsqueeze(1), ACT.Copy).then_inc(
                        S("y_act"), 1)
                gate_row(n)
                act.wait_ge(S("over_known"), L + 1)
                n_over = act.value_load(rti[0:1, 0:1], min_val=0, max_val=T)
                with act.If(n_over > 0):
                    with act.Fori(0, EPG) as e:
                        act.wait_ge(S(f"over_used{L}"), e * 3 + 5)
                        s.activation(sil[:, :], bank[0], ACT.Silu).then_inc(S(f"over_sil{L}"), 1)
                        act.wait_ge(S(f"over_heT{L}"), e + 1)
                        s.activation(heT[:, :], bank[6], ACT.Copy).then_inc(S(f"over_hT{L}"), 1)

            ffn(0)

            norm(2)
            modulate(2)
            gate_row(2)
            s.dma_start(glub, a["s5_glu_b"][0].rearrange("(r n) -> r n", r=4)).then_inc(S("glub_in"), 16)

            def cur(k, m):
                s.activation(ucur[:, m, :].unsqueeze(1), hT[:, bass.ds(k, 1), :], ACT.Copy)
                s.activation(bcur[:, m, :, :].unsqueeze(2), BT[:, :, bass.ds(k, 1), :], ACT.Copy)
                s.activation(ccur[:, m, :, :].unsqueeze(2), CT[:, :, bass.ds(k, 1), :], ACT.Copy)
                s.activation(dcur[:, m:m + 1], cols[:, bass.ds(k + ROWS["s5d"][0], 1)], ACT.Copy).then_inc(
                    S("cur_ready"), 1)

            act.wait_ge(S("hT_dve"), 4 * 3)
            act.wait_ge(S("hT_act"), 4 * 3)
            cur(0, 0)
            with act.Fori(0, KD // 2) as kk:
                for m in range(2):
                    act.wait_ge(S("yv_ready"), 2 * kk + m + 1)
                    if m == 0:
                        cur(2 * kk + 1, 1)
                    else:
                        cur((2 * kk + 2) % KD, 0)
                    act.wait_ge(S("yv_ready"), 2 * kk + m + 2)
                    s.activation(actT[:, bass.ds(2 * kk + m, 1), :], yv[:, :].unsqueeze(1),
                                 ACT.Gelu_apprx_tanh).then_inc(S("act_ready"), 1)
            for h in range(2):
                for b in range(NB):
                    act.wait_ge(S("glu_ps"), 2 * h + 2)
                    s.activation(q_a[:, 2 * h + b, :], bank[4 * h + 2 + b], ACT.Sigmoid).then_inc(S("glu_sig"), 1)
            ffn(1)
            act.wait_ge(S("x_new"), 4)
            act.dma_start(fing, a["final_g"].rearrange("(o n) -> o n", o=1).to_broadcast([P, D])).then_inc(S("fg_in"), 16)
            norm(4)

        @block.vector
        def _(dve):
            v = nc.vector
            for name in ('yv_ready', 'q_ready', 'bu_used', 'he_ready', 'y_dve', 'mod1_evac', 'over_yg0', 'over_yg1'):
                dve.sem_inc(S(name), PRIMED[name])
            ch = Chain(dve, S("dve_order"))
            link = ch.link

            def gemv(r, j, use, done):
                dve.wait_ge(S(f"ada_in{j % ASLOTS}"), use)
                fold(r, aring[:, j % ASLOTS, :].rearrange("p (k c) -> p k c", c=HALF), done)

            def fold(r, w, done):
                u, kh = r // 2 % 3, r % 2
                if kh:
                    dve.wait_ge(S("gemv_done"), done)
                for kk in range(4):
                    k = kh * 4 + kk
                    if k == 0:
                        ins = v.tensor_scalar(acc[:, u, :], w[:, kk, :], condc[:, k:k + 1], None, ALU.mult)
                    else:
                        ins = v.scalar_tensor_tensor(acc[:, u, :], w[:, kk, :], condc[:, k:k + 1], acc[:, u, :],
                                                     ALU.mult, ALU.add)
                    if kk < 3:
                        link(ins)
                    else:
                        ins.then_inc(S("gemv_done"), 1)

            def gemv0(lo, hi):
                for r in range(lo, hi):
                    if r % 2 == 0 and r // 2 >= 3:
                        dve.wait_ge(S("mod_ps"), r // 2 - 2)
                    if r // 2 in RING_ADA:
                        at = RING_ADA.index(r // 2)
                        dve.wait_ge(S(f"ada_ring{at % 2}"), 16 * (at // 2 + 1))
                        fold(r, u3(N_WIN + at % 2)[:, 4 * (r % 2):4 * (r % 2) + 4, :], r)
                    else:
                        j = A_HALF0.index(r)
                        gemv(r, j, 16 * (j // ASLOTS + 1), r)

            def reduce_angle(src, turns, lo, hi):
                link(v.tensor_scalar(turns, src, 1.0 / (2 * PI), MAGIC, ALU.mult, ALU.add))
                link(v.tensor_scalar(turns, turns, -MAGIC, None, ALU.add))
                link(v.scalar_tensor_tensor(hi, turns, -TWO_PI[0], src, ALU.mult, ALU.add))
                link(v.scalar_tensor_tensor(hi, turns, -TWO_PI[1], hi, ALU.mult, ALU.add))
                link(v.scalar_tensor_tensor(hi, turns, -TWO_PI[2], hi, ALU.mult, ALU.add))
                link(v.tensor_scalar(hi, hi, 3.1415925, -3.1415925, ALU.min, ALU.max))
                link(v.scalar_tensor_tensor(lo, hi, -1.0, hi, ALU.mult, ALU.max))

            dve.wait_ge(S("cond_ready"), 1)
            gemv0(0, 4)
            def norm(n):
                if n == 0:
                    dve.wait_ge(S("x_in"), 16)
                link(v.tensor_tensor_reduce(out=xhat[:, 1, :], in0=x[:, 1, :], in1=x[:, 1, :], scale=1.0, scalar=0.0,
                                            op0=ALU.mult, op1=ALU.add, accum_out=stat[:, 1:2]))
                dve.wait_ge(S("ss_act"), n + 1)
                v.tensor_scalar(stat[:, 2:4], stat[:, 0:2], 1.0 / D, EPS, ALU.mult, ALU.add).then_inc(S("var_ready"), 1)
                dve.wait_ge(S("std_ready"), n + 1)
                link(v.reciprocal(stat[:, 6:8], stat[:, 4:6]))
                for b in range(NB):
                    last = v.tensor_scalar(xhat[:, b, :], x[:, b, :], stat[:, 6 + b:7 + b], None, ALU.mult)
                    if n < 4:
                        last.then_inc(S("xhat_ready"), 1)
                    else:
                        link(last)

            dve.wait_ge(S("pos_in"), 16)
            pos = rope[:, 0, 0:NB]
            link(v.tensor_copy(pos, rti[:, 0:NB]))
            ang = rope[:, 1, :].rearrange("p (b i) -> p b i", b=NB)
            for i in range(RH):
                last = v.tensor_scalar(ang[:, :, i], pos, float(ROPE_THETA ** (-2.0 * i / ROT)), None, ALU.mult)
            link(last)

            reduce_angle(rope[:, 1, :], rope[:, 6, :], rope[:, 2, :], rope[:, 3, :])
            v.tensor_scalar(rope[:, 2, :], rope[:, 2, :], -1.0, PI / 2, ALU.mult, ALU.add).then_inc(S("rope_arg"), 1)

            dve.wait_ge(S("cols_ready"), 1)
            at, n = ROWS["lam"]
            lam = cols[:, at:at + n]
            link(v.scalar_tensor_tensor(sp[:, 2, :], lam, -1.0, lam, ALU.mult, ALU.max))
            v.tensor_scalar(sp[:, 0, :], sp[:, 2, :], -1.0, None, ALU.mult).then_inc(S("sp_arg"), 1)
            link(v.tensor_scalar(sp[:, 3, :], lam, -1.0, 0.0, ALU.mult, ALU.max))
            dve.wait_ge(S("sp_ln"), 1)
            link(v.tensor_tensor(sp[:, 1, :], sp[:, 1, :], sp[:, 3, :], ALU.add))
            v.tensor_scalar(sp[:, 2, :], sp[:, 1, :], 8.0, None, ALU.mult)
            v.tensor_scalar(sp[:, 3, :], sp[:, 1, :], -8.0, None, ALU.mult).then_inc(S("sp_ready"), 1)
            norm(0)
            gemv0(4, 8)

            def mod_evac(lo, hi):
                dve.wait_ge(S("mod_ps"), hi)
                v.tensor_tensor(mod[:, 0].rearrange("p s k -> p (s k)")[:, 4 * lo:4 * hi],
                                bank[7][:, 4 * lo:4 * hi], adab[:, 0, 4 * lo:4 * hi], ALU.add).then_inc(
                                    S("mod_cols"), 1)
                dve.wait_ge(S("mod_cols"), 1 if lo == 0 else 2)

            def mod_scale(n, done=True):
                L, sec = n // 2, (SC_M if n % 2 == 0 else SC_F)
                at = ROWS[("mix0", "ffn0", "mix1", "ffn1")[n]][0]
                v.scalar_tensor_tensor(modA[:, n, :], mod[:, L, sec, :], 1.0, cols[:, at:at + KD],
                                       ALU.add, ALU.mult).then_inc(S("modA_ready"), 1)
                dve.wait_ge(S("modA_ready"), n + 1)

            def modulate(n):
                L, sec = n // 2, (SH_M if n % 2 == 0 else SH_F)
                for k in (2, 3, 6, 7):
                    dve.wait_ge(S("xT_ps"), 4 * n + k // 2 + 1)
                    v.tensor_scalar(hT[:, k, :], bank[k // 2][:, (k % 2) * T:(k % 2 + 1) * T], modA[:, n, k:k + 1],
                                    mod[:, L, sec, k:k + 1], ALU.mult, ALU.add).then_inc(S("hT_dve"), 1)

            mod_evac(0, 4)
            mod_scale(0)
            modulate(0)
            gemv0(8, 16)
            dve.wait_ge(S("kv_ps"), 1)
            link(v.tensor_copy(qkv[:, :, HALF:768], bank[6].rearrange("p (b n) -> p b n", b=NB)))
            dve.wait_ge(S("q_evac"), 2)
            dve.wait_ge(S("rope_ready"), 1)
            for b in range(NB):
                hd = qkv[:, b, 0:640].rearrange("p (h n) -> p h n", n=HEAD)
                x1, x2 = hd[:, :, 0:RH], hd[:, :, RH:ROT]
                cc = rope[:, 4, b * RH:(b + 1) * RH].unsqueeze(1).to_broadcast([P, 10, RH])
                ss = rope[:, 5, b * RH:(b + 1) * RH].unsqueeze(1).to_broadcast([P, 10, RH])
                t = [rq[:, m, :].rearrange("p (h n) -> p h n", n=RH) for m in range(4)]
                v.tensor_tensor(t[0], x1, cc, ALU.mult)
                v.tensor_tensor(t[1], x2, ss, ALU.mult)
                v.tensor_tensor(t[2], x2, cc, ALU.mult)
                link(v.tensor_tensor(t[3], x1, ss, ALU.mult))
                v.tensor_tensor(x1, t[0], t[1], ALU.subtract)
                link(v.tensor_tensor(x2, t[2], t[3], ALU.add))
                kh = qkv[:, b, NQ * HEAD:640].rearrange("p (g n) -> p g n", g=NKV)
                v.tensor_copy(k2[:, b, :].rearrange("p (g u n) -> p g u n", g=NKV, u=2),
                              kh.unsqueeze(2).to_broadcast([P, NKV, 2, HEAD])).then_inc(S("rope_done"), 1)
                dve.wait_ge(S("rope_done"), b + 1)
            gemv0(16, 20)
            dve.wait_ge(S("xr_ready"), 1)
            for j in range(LT):
                link(v.tensor_scalar(xc[:, j, :], xr[:, j, :], col("conv_w", 3 * LT + j), col("conv_b", j),
                                     ALU.mult, ALU.add))
            for s_ in range(1, CONV):
                for j in range(LT):
                    last = v.scalar_tensor_tensor(xc[:, j, s_:], xr[:, j, 0:T - s_], col("conv_w", (3 - s_) * LT + j),
                                                  xc[:, j, s_:], ALU.mult, ALU.add)
                    if s_ < CONV - 1:
                        if j == LT - 1:
                            link(last)
            last.then_inc(S("xc_ready"), 1)
            dve.wait_ge(S("kT_ps"), 1)
            v.tensor_copy(kT[:, :, :], bank[6].rearrange("p (g t) -> p g t", g=NKV)).then_inc(S("kT_ready"), 1)
            dve.wait_ge(S("small_in"), 16 * 9)
            sk = smx[:, 4, 0:NQ]
            link(v.tensor_scalar(sk.rearrange("p (r i) -> p r i", r=2), sink[:, :].rearrange("p (i r) -> p r i", r=2),
                                 1.0 / SCALE, None, ALU.mult))
            for b in range(NB):
                pp = P0 if b == 0 else P1
                n_k = P * (b + 1)
                dve.wait_ge(S("s_ps"), b + 1)
                if b == 0:
                    sc = [PS[:, r, :].rearrange("p (i n) -> p i n", n=P) for r in range(2)]
                    rng = [(0, 64, 0, 64), (64, P, 0, P)]
                    zero = [(0, 64, 64, P)]
                else:
                    sc = [PS[:, w:w + 2, :].rearrange("p b (i n) -> p (b i) n", n=T) for w in (4, 2)]
                    rng = [(0, 64, 64, 192), (64, P, P, T)]
                    zero = [(0, 64, 0, 64), (0, 64, 192, T), (64, P, 0, P)]
                for lo, hi, k0, k1 in zero:
                    v.memset(pp[lo:hi, :, k0:k1], 0.0)
                mx = smx[:, 0, b * NQ:(b + 1) * NQ]
                for lo, hi, k0, k1 in rng:
                    for r in range(2):
                        last = v.tensor_reduce(smx[lo:hi, 0, b * NQ + 4 * r:b * NQ + 4 * r + 4], sc[r][lo:hi, :, k0:k1],
                                               AX.X, ALU.max)
                link(last)
                link(v.tensor_tensor(mx, mx, sk, ALU.max))
                v.tensor_tensor(smx[:, 1, b * NQ:(b + 1) * NQ], sk, mx, ALU.subtract)
                for lo, hi, k0, k1 in rng:
                    for r in range(2):
                        m = smx[lo:hi, 0, b * NQ + 4 * r:b * NQ + 4 * r + 4].unsqueeze(2).to_broadcast(
                            [64, 4, k1 - k0])
                        last = v.tensor_tensor(pp[lo:hi, 4 * r:4 * r + 4, k0:k1], sc[r][lo:hi, :, k0:k1], m,
                                               ALU.subtract)
                last.then_inc(S("s_less_m"), 1)
            for b in range(NB):
                pp = P0 if b == 0 else P1
                n_k = P * (b + 1)
                dve.wait_ge(S("p_exp"), b + 1)
                den = smx[:, 3, b * NQ:(b + 1) * NQ]
                link(v.tensor_reduce(den, pp[:, :, 0:n_k], AX.X, ALU.add))
                link(v.tensor_tensor(den, den, smx[:, 2, b * NQ:(b + 1) * NQ], ALU.add))
                link(v.reciprocal(den, den))
                v.tensor_tensor(pp[:, :, 0:n_k], pp[:, :, 0:n_k], den.unsqueeze(2).to_broadcast([P, NQ, n_k]),
                                ALU.mult).then_inc(S("p_ready"), 1)
            gemv0(20, 24)
            mod_evac(4, 12)
            mod_scale(1)
            dve.wait_ge(S("lru_a"), 1)
            link(v.tensor_tensor(lr_i, lr_i, xc[:, :, :], ALU.mult))
            link(v.tensor_tensor(lr_r, lr_u, lr_u, ALU.mult))
            v.scalar_tensor_tensor(lr_t.rearrange("p k t -> p (k t)"), lr_r.rearrange("p k t -> p (k t)"), 1.0,
                                   lr_t.rearrange("p k t -> p (k t)"), ALU.add, ALU.mult).then_inc(S("lru_b2"), 1)
            dve.wait_ge(S("lru_sq"), 1)
            link(v.tensor_tensor(lr_i, lr_i, lr_t, ALU.mult))
            for j in range(LT):
                last = v.tensor_tensor_scan(lr_r[:, j, :], lr_u[:, j, :], lr_i[:, j, :], 0.0, ALU.mult, ALU.add)
            link(last)
            v.tensor_tensor(mixT[:, 4:8, :], lr_r, gate[:, :, :], ALU.mult).then_inc(S("lru_ready"), 1)

            def residual(n, waits, psum):
                dve.wait_ge(S("grow_ready"), n + 1)
                tmp = acc
                for b in range(NB):
                    for h in range(2):
                        dve.wait_ge(S(waits), (2 * b + h + 1) + 4 * (n // 2))
                        gr = grow[:, h * HALF:(h + 1) * HALF]
                        link(v.tensor_tensor(tmp[:, h, :], psum(b, h), gr, ALU.mult))
                        last = v.tensor_tensor(x[:, b, h * HALF:(h + 1) * HALF], x[:, b, h * HALF:(h + 1) * HALF],
                                               tmp[:, h, :], ALU.add)
                return last

            R = s5r
            q = slice(0, NQT)
            dve.wait_ge(S("dt_ready"), 1)
            dtb = R[q, 4, 0:2].unsqueeze(2).to_broadcast([NQT, 2, STATE])
            h2 = lambda r: R[q, r, :].rearrange("q (g p) -> q g p", g=2)
            link(v.tensor_copy(R[q, 0:2, :], s5i[q, 0:2, :]))
            link(v.tensor_tensor(h2(5), h2(0), dtb, ALU.mult))
            link(v.tensor_tensor(h2(6), h2(1), dtb, ALU.mult))
            reduce_angle(R[q, 6, :], R[q, 12, :], R[q, 10, :], R[q, 11, :])
            v.tensor_scalar(R[q, 10, :], R[q, 10, :], -1.0, PI / 2, ALU.mult, ALU.add).then_inc(S("s5_th"), 1)
            dve.wait_ge(S("s5_trig"), 1)
            tt = lambda d, s1, s2, op: link(v.tensor_tensor(R[q, d, :], R[q, s1, :], R[q, s2, :], op))
            tt(12, 7, 8, ALU.mult)
            tt(13, 7, 9, ALU.mult)
            link(v.tensor_scalar(R[q, 12, :], R[q, 12, :], -1.0, None, ALU.add))
            tt(14, 0, 0, ALU.mult)
            tt(15, 1, 1, ALU.mult)
            tt(14, 14, 15, ALU.add)
            link(v.reciprocal(R[q, 14, :], R[q, 14, :]))
            tt(15, 12, 0, ALU.mult)
            tt(16, 13, 1, ALU.mult)
            tt(15, 15, 16, ALU.add)
            tt(16, 13, 0, ALU.mult)
            tt(17, 12, 1, ALU.mult)
            tt(16, 16, 17, ALU.subtract)
            tt(10, 15, 14, ALU.mult)
            v.tensor_tensor(R[q, 11, :], R[q, 16, :], R[q, 14, :], ALU.mult).then_inc(S("s5_rows"), 1)
            dve.wait_ge(S("s5_cols_ps"), 1)
            link(v.tensor_copy(s5c[:, :, :], bank[6][:, 0:5 * NQT].rearrange("p (r q) -> p r q", r=5)))
            cb = lambda r: s5c[:, r, :].unsqueeze(2).to_broadcast([P, NQT, CH])
            link(v.memset(Bp[:, :, :, :], 0.0))
            for w, (s1, s2, op) in enumerate(((0, 1, ALU.subtract), (1, 0, ALU.add))):
                link(v.tensor_tensor(bt1[:, :, :], Bl[:, s1, :, :], cb(3), ALU.mult))
                link(v.tensor_tensor(bt2[:, :, :], Bl[:, s2, :, :], cb(4), ALU.mult))
                for u in range(2):
                    pr_ = slice(u * 64, u * 64 + 64)
                    dst = Bp[pr_, w].rearrange("p k (q g c) -> p (k q) g c", g=2, c=CH)[:, :, u, :]
                    v.tensor_tensor(dst, bt1[pr_, :, :], bt2[pr_, :, :], op).then_inc(S("bp_ready"), 1)
                dve.wait_ge(S("bp_ready"), 2 * w + 2)
            link(v.memset(CT[:, :, :, :], 0.0))
            for w in range(2):
                for hf in range(2):
                    dve.wait_ge(S("ct_ps"), 2 * w + hf + 1)
                    for u in range(2):
                        pr_ = slice(u * 64, u * 64 + 64)
                        dst = CT[pr_, w, hf * 4:hf * 4 + 4, :].rearrange("p k (q g c) -> p (k q) g c", g=2, c=CH)[:, :, u, :]
                        src = bank[6][pr_, :].rearrange("p (k g c) -> p k g c", g=2, c=CH)[:, :, u, :]
                        v.tensor_scalar(dst, src, -1.0 if w else 1.0, None, ALU.mult).then_inc(S("ct_evac"), 1)
            w32 = lambda m: Ew[:, m, :]
            link(v.tensor_copy(w32(0), s5c[:, 1, :]))
            link(v.tensor_copy(w32(1), s5c[:, 2, :]))
            for table in (1, 0):
                Ec, Es = E[:, 2 * table, :, :], E[:, 2 * table + 1, :, :]
                v.memset(Ec[:, :, 0:1], 1.0)
                link(v.memset(Es[:, :, 0:1], 0.0))
                for n_ in (1, 2, 4, 8):
                    c_b = w32(0).unsqueeze(2).to_broadcast([P, NQT, n_])
                    s_b = w32(1).unsqueeze(2).to_broadcast([P, NQT, n_])
                    te = [Et[:, m, 0:NQT * n_].rearrange("p (q n) -> p q n", n=n_) for m in range(4)]
                    v.tensor_tensor(te[0], Ec[:, :, 0:n_], c_b, ALU.mult)
                    v.tensor_tensor(te[1], Es[:, :, 0:n_], s_b, ALU.mult)
                    v.tensor_tensor(te[2], Ec[:, :, 0:n_], s_b, ALU.mult)
                    link(v.tensor_tensor(te[3], Es[:, :, 0:n_], c_b, ALU.mult))
                    v.tensor_tensor(Ec[:, :, n_:2 * n_], te[0], te[1], ALU.subtract)
                    link(v.tensor_tensor(Es[:, :, n_:2 * n_], te[2], te[3], ALU.add))
                    v.tensor_tensor(w32(2), w32(0), w32(0), ALU.mult)
                    v.tensor_tensor(w32(3), w32(1), w32(1), ALU.mult)
                    link(v.tensor_tensor(w32(4), w32(0), w32(1), ALU.mult))
                    link(v.tensor_tensor(w32(0), w32(2), w32(3), ALU.subtract))
                    link(v.tensor_scalar(w32(1), w32(4), 2.0, None, ALU.mult))
            residual(0, "m_ps", lambda b, h: bank[2 * b + h]).then_inc(S("x_new"), 1)
            dve.wait_ge(S("x_new"), 1)

            def ffn(L):
                n = 2 * L + 1
                norm(n)
                modulate(n)
                lg = rt[:, 0:40].rearrange("p (b n) -> p b n", b=NB)
                dve.wait_ge(S("router_ps"), L + 1)
                psl = bank[4][:, 0:40].rearrange("p (b n) -> p b n", b=NB)
                link(v.tensor_tensor(lg, psl, rb[:, L:L + 1, :].to_broadcast([P, NB, 20]), ALU.add))
                lg4 = lg[:, :, 0:NG]
                r2 = lambda o: rt[:, o:o + NB]
                r8 = lambda o: rt[:, o:o + 8].rearrange("p (b g) -> p b g", b=NB)
                bc = lambda ap: ap.unsqueeze(2).to_broadcast([P, NB, 4])
                prio = r8(300)
                for g_ in range(4):
                    last = v.memset(prio[:, :, g_], float(4 - g_))
                link(last)

                def first_max(val, mx, oh, key):
                    link(v.tensor_reduce(mx, val, AX.X, ALU.max))
                    link(v.tensor_tensor(oh, val, bc(mx), ALU.is_equal))
                    link(v.tensor_tensor(oh, oh, prio, ALU.mult))
                    link(v.tensor_reduce(key, oh, AX.X, ALU.max))
                    link(v.tensor_tensor(oh, oh, bc(key), ALU.is_equal))

                oh = r8(48)
                first_max(lg4, r2(40), oh, r2(42))
                v.tensor_tensor(r8(56), lg4, bc(r2(40)), ALU.subtract).then_inc(S("lg_ready"), 1)
                le = lg[:, :, NG:].rearrange("p b (g e) -> p b g e", g=NG)
                sel = rt[:, 96:128].rearrange("p (b g e) -> p b g e", b=NB, g=NG)
                link(v.tensor_tensor(sel, le, oh.unsqueeze(3).to_broadcast([P, NB, NG, EPG]), ALU.mult))
                les = r8(128)
                link(v.tensor_reduce(les, sel.rearrange("p b g e -> p b e g"), AX.X, ALU.add))
                oh1, oh2 = r8(136), r8(144)
                first_max(les, r2(80), oh1, r2(42))
                link(v.scalar_tensor_tensor(rt[:, 152:160], rt[:, 136:144], -1e30, rt[:, 128:136], ALU.mult, ALU.add))
                first_max(r8(152), r2(82), oh2, r2(42))
                v.tensor_tensor(r2(84), r2(82), r2(80), ALU.subtract).then_inc(S("l2_ready"), 1)
                dve.wait_ge(S("eg_ready"), L + 1)
                link(v.tensor_reduce(r2(88), r8(64), AX.X, ALU.add))
                dve.wait_ge(S("e2_ready"), L + 1)
                link(v.tensor_scalar(r2(90), r2(86), 1.0, None, ALU.add))
                link(v.tensor_tensor(r2(88), r2(88), r2(90), ALU.mult))
                link(v.reciprocal(r2(88), r2(88)))
                link(v.tensor_tensor(r2(90), r2(88), r2(86), ALU.mult))
                gt = r8(160)
                link(v.tensor_tensor(gt, oh1, bc(r2(88)), ALU.mult))
                link(v.tensor_tensor(oh2, oh2, bc(r2(90)), ALU.mult))
                v.tensor_tensor(gt, gt, oh2, ALU.add).then_inc(S("gates_ready"), 1)
                dve.wait_ge(S("gates_ready"), L + 1)
                dve.wait_ge(S("rank_ps"), L + 1)
                rk = r2(168)
                link(v.tensor_tensor(r8(176), oh, bank[5][:, 0:8].rearrange("p (b g) -> p b g", b=NB), ALU.mult))
                link(v.tensor_reduce(rk, r8(176), AX.X, ALU.add))
                for b in range(NB):
                    for g_ in range(NG):
                        v.tensor_scalar(pick[:, b, g_, :], slot_no[:, :], rt[:, 168 + b:169 + b], oh[:, b, g_:g_ + 1],
                                        ALU.is_equal, ALU.mult)
                link(v.tensor_scalar(r2(170), rk, -float(P), None, ALU.add))
                for b in range(NB):
                    last = v.tensor_scalar(pick[:, b, NG, :], slot_no[:, :], rt[:, 170 + b:171 + b], None, ALU.is_equal)
                last.then_inc(S("pick_ready"), 1)
                ov = rt[:, 192:196].rearrange("p (b n) -> p b n", b=NB)
                link(v.tensor_scalar(ov[:, :, 0], rk, float(P), None, ALU.is_ge))
                link(v.tensor_scalar(ov[:, :, 1], rk, float(P), None, ALU.is_equal))
                for g_ in range(NG):
                    last = v.tensor_scalar(r8(200)[:, :, g_], oh[:, :, g_], float(g_), None, ALU.mult)
                link(last)
                link(v.tensor_reduce(r2(208), r8(200), AX.X, ALU.add))
                v.tensor_tensor(ov[:, :, 1], ov[:, :, 1], r2(208), ALU.mult).then_inc(S("ov_ready"), 1)
                dve.wait_ge(S("gsl_ps"), L + 1)
                link(v.tensor_copy(gsl[:, :, :], bank[5][:, 16:16 + 20].rearrange("p (g e) -> p g e", e=EPG)))
                v.tensor_copy(rti[:, 0:2], bank[5][:, 40:42]).then_inc(S("over_known"), 1)
                dve.wait_ge(S("over_known"), L + 1)

                def hg_evac(i):
                    dve.wait_ge(S("gathered"), 10 * L + 2 + 2 * i)
                    for k in range(4, KD):
                        last = v.tensor_scalar(hg[:, k, :], bank[2][:, (k - 4) * P:(k - 3) * P],
                                               modA[:, n, k:k + 1], mod[:, L, SH_F, k:k + 1], ALU.mult, ALU.add)
                    last.then_inc(S("hg_dve"), 1)

                hg_evac(0)
                n0 = MOE_BASE[L]
                per = 1 + (18 if L == 0 else 0)
                with dve.Fori(0, NG) as i:
                    ch.enter(i, per)
                    link(v.tensor_copy(gcur[:, :], gsl[:, bass.ds(i, 1), :].rearrange("p a e -> p (a e)")))
                    j = 0
                    for e in range(EPG):
                        dve.wait_ge(S("sil_ready"), 1 + 16 * L + 4 * i + e + 1)
                        dve.wait_ge(S("b_ps"), 16 * L + 4 * i + e + 1)
                        if e or L:
                            dve.wait_ge(S("heT_ps"), 16 * L + 4 * i + e)
                        v.scalar_tensor_tensor(he[:, :], sil[:, :], gcur[:, e:e + 1], bank[2 + e % 2],
                                               ALU.mult, ALU.mult).then_inc(S("he_ready"), 1)
                        if L == 0:
                            for _ in range(GEMV_OF[e]):
                                if j % 2 == 0:
                                    dve.wait_ge(S("mod_ps"), A_UNITS + 3 * i)
                                gemv(j, j, 16 * (j // ASLOTS + 1) + 16 * len(A_HALF0) // ASLOTS + i * (16 * 6 // ASLOTS), A_HALVES + j + 6 * i)
                                j += 1
                    hg_evac(i + 1)
                    dve.wait_ge(S("y_ps"), 16 * L + 4 * i + 4)
                    v.tensor_copy(yg[:, bass.ds(i, 1), HALF:], bank[5].unsqueeze(1)).then_inc(S("y_dve"), 1)
                    if L == 0:
                        dve.wait_ge(S("mod_ps"), A_UNITS + 3 + 3 * i)
                        v.tensor_copy(mod[:, 1].rearrange("p s k -> p (s k)")[:, bass.ds(i * 12, 12)],
                                      bank[7][:, 64:76]).then_inc(S("mod1_evac"), 1)
                ch.leave(NG)
                if L == 0:
                    dve.wait_ge(S("mod1_evac"), 1 + NG)
                    m1 = mod[:, 1].rearrange("p s k -> p (s k)")
                    v.tensor_tensor(m1, m1, adab[:, 1, :], ALU.add).then_inc(S("mod_cols"), 1)
                    dve.wait_ge(S("mod_cols"), 3)
                    mod_scale(2)
                    mod_scale(3)
                dve.wait_ge(S("pickT_ps"), L + 1)
                v.tensor_copy(pickT[:, :, :], PS[:, 0:2, :].rearrange("p c (g t) -> p (c g) t", t=T)).then_inc(
                    S("pickT_ready"), 1)
                dve.wait_ge(S("grow_ready"), n + 1)
                tmp = w3(W0 + NB * (NG + 1) * P, 2, HALF)
                for b in range(NB):
                    for h in range(2):
                        dve.wait_ge(S("sc_ps"), 4 * L + 2 * b + h + 1)
                        link(v.tensor_tensor(tmp[:, h, :], bank[(0, 1, 2, 3)[2 * b + h]], grow[:, h * HALF:(h + 1) * HALF],
                                             ALU.mult))
                        last = v.tensor_tensor(x[:, b, h * HALF:(h + 1) * HALF], x[:, b, h * HALF:(h + 1) * HALF],
                                               tmp[:, h, :], ALU.add)
                last.then_inc(S("x_main"), 1)
                dve.wait_ge(S("x_main"), L + 1)
                n_over = dve.value_load(rti[0:1, 0:1], min_val=0, max_val=T)
                with dve.If(n_over > 0):
                    oc = Chain(dve, S(f"over_order{L}"))
                    oc.link(v.memset(yg[:, 0, :], 0.0))
                    with dve.Fori(0, EPG) as e:
                        oc.enter(e, 1)
                        dve.wait_ge(S(f"over_sil{L}"), e + 1)
                        oc.link(v.tensor_copy(gcur[:, 0:1], gsl[:, NG, bass.ds(e, 1)]))
                        v.scalar_tensor_tensor(he[:, :], sil[:, :], gcur[:, 0:1], bank[2], ALU.mult,
                                               ALU.mult).then_inc(S(f"over_he{L}"), 1)
                        dve.wait_ge(S(f"over_used{L}"), e * 3 + 6)
                        v.tensor_tensor(yg[:, 0, :], yg[:, 0, :], PS[:, 4:6, :].rearrange("p b n -> p (b n)"),
                                        ALU.add).then_inc(S(f"over_yg{L}"), 1)
                        dve.wait_ge(S(f"over_yg{L}"), 1 + e + 1)
                    oc.leave(EPG)
                    dve.wait_ge(S(f"over_pT{L}"), 1)
                    v.tensor_copy(pickT[:, 0, :], bank[6][:, 0:T]).then_inc(S(f"over_pick{L}"), 1)
                    dve.wait_ge(S(f"over_sc{L}"), 1)
                    for b in range(NB):
                        for h in range(2):
                            oc.link(v.tensor_tensor(tmp[:, h, :], bank[2 * b + h], grow[:, h * HALF:(h + 1) * HALF],
                                                    ALU.mult))
                            oc.link(v.tensor_tensor(x[:, b, h * HALF:(h + 1) * HALF],
                                                    x[:, b, h * HALF:(h + 1) * HALF], tmp[:, h, :], ALU.add))
                nc.vector.drain().then_inc(S("x_new"), 1)
                dve.wait_ge(S("x_new"), 2 * L + 2)

            ffn(0)

            norm(2)
            modulate(2)
            f2 = lambda ap: ap.rearrange("p (q t) -> p q t", q=2)
            per = 4 * 2
            with dve.Fori(0, KD // 2) as kk:
                ch.enter(kk, per)
                for m, j in ((0, 0), (0, 1), (1, 0), (1, 1)):
                    n = 4 * kk + 2 * m + j
                    bre = PS[:, 2 * j:2 * j + 2, 0:T]
                    bim = PS[:, 2 * j:2 * j + 2, T:2 * T]
                    c_, s_ = f2(cs[:, j, 0, :]), f2(cs[:, j, 1, :])
                    dve.wait_ge(S("bu_ready"), 1 + 2 * n + 2)
                    dve.wait_ge(S("tab_ready"), n + 1)
                    v.tensor_tensor(f2(pr[:, 0, :]), bre, c_, ALU.mult)
                    v.tensor_tensor(f2(pr[:, 1, :]), bim, s_, ALU.mult)
                    v.tensor_tensor(f2(pr[:, 2, :]), bim, c_, ALU.mult)
                    v.tensor_tensor(f2(pr[:, 3, :]), bre, s_, ALU.mult).then_inc(S("bu_used"), 1)
                    dve.wait_ge(S("bu_used"), 1 + n + 1)
                    v.tensor_tensor(pr[:, 0, :], pr[:, 0, :], pr[:, 1, :], ALU.add)
                    link(v.tensor_tensor(pr[:, 2, :], pr[:, 2, :], pr[:, 3, :], ALU.subtract))
                    for q_ in range(2):
                        r_ = s5c[:, 0, bass.ds(2 * n + q_, 1)].to_broadcast([P, T])
                        for w in range(2):
                            last = v.tensor_tensor_scan(gg[:, w, q_ * T:(q_ + 1) * T], r_,
                                                        pr[:, 2 * w, q_ * T:(q_ + 1) * T], 0.0, ALU.mult, ALU.add)
                    link(last)
                    dve.wait_ge(S("q_used"), 2 + n - 1)
                    v.tensor_tensor(qq[j][:, 0, :], gg[:, 0, :], cs[:, j, 0, :], ALU.mult)
                    v.scalar_tensor_tensor(qq[j][:, 1, :], gg[:, 1, :], -1.0, cs[:, j, 1, :], ALU.mult, ALU.mult)
                    v.tensor_tensor(qq[j][:, 2, :], gg[:, 0, :], cs[:, j, 1, :], ALU.mult)
                    v.tensor_tensor(qq[j][:, 3, :], gg[:, 1, :], cs[:, j, 0, :], ALU.mult).then_inc(S("q_ready"), 1)
                    if j == 1:
                        dve.wait_ge(S("q_used"), 2 + n + 1)
                        dve.wait_ge(S("act_ready"), 1 + 2 * kk + m)
                        v.scalar_tensor_tensor(yv[:, :], ucur[:, m, :], dcur[:, m:m + 1], bank[4][:, 0:T], ALU.mult,
                                               ALU.add).then_inc(S("yv_ready"), 1)
            ch.leave(KD // 2)
            dve.wait_ge(S("grow_ready"), 3)
            for h in range(2):
                for b in range(NB):
                    dve.wait_ge(S("glu_sig"), 2 * h + b + 1)
                    link(v.tensor_tensor(q_a[:, 2 * h + b, :], q_a[:, 2 * h + b, :], bank[4 * h + b], ALU.mult))
                    link(v.tensor_tensor(q_a[:, 2 * h + b, :], q_a[:, 2 * h + b, :], grow[:, h * HALF:(h + 1) * HALF],
                                         ALU.mult))
                    last = v.tensor_tensor(x[:, b, h * HALF:(h + 1) * HALF], x[:, b, h * HALF:(h + 1) * HALF],
                                           q_a[:, 2 * h + b, :], ALU.add)
            last.then_inc(S("x_new"), 1)
            dve.wait_ge(S("x_new"), 3)
            ffn(1)
            norm(4)
            dve.wait_ge(S("fg_in"), 16)
            for b in range(NB):
                v.tensor_tensor(xhat[:, b, :], xhat[:, b, :], fing, ALU.mult).then_inc(S("out_ready"), 1)

        @block.tensor
        def _(pe):
            mm = nc.tensor.matmul
            for name in ('bu_ready', 'q_used'):
                pe.sem_inc(S(name), PRIMED[name])

            def tr(dst, src, n=P):
                return nc.tensor.transpose(dst, src, ident[0:n, 0:n])

            def bcol(ap, n=P):
                return ap.to_broadcast([ap.shape[0], n])

            pe.wait_ge(S("c_in"), 16)
            pe.wait_ge(S("ident_ready"), 1)
            tr(bank[2][:, 0:KD], crow, KD).then_inc(S("c_ps"), 1)
            pe.wait_ge(S("rows_in"), 16 * (len(ROWS) + 2))
            tr(bank[0][:, 0:N_ROWS], rows, N_ROWS)
            tr(bank[1][:, 0:6 * KD], brow[:, 0, :], 6 * KD)
            tr(bank[1][:, 6 * KD:12 * KD], brow[:, 1, :], 6 * KD).then_inc(S("cols_ps"), 1)
            pe.wait_ge(S("consts_ready"), 1)
            pe.wait_ge(S("pool_order"), 3)

            def mod_cols(u, at):
                for c4 in range(4):
                    last = mm(bank[7][:, at + c4:at + c4 + 1], acc[:, u % 3, c4 * P:(c4 + 1) * P], ones[:, 0:1],
                              start=True, stop=True)
                last.then_inc(S("mod_ps"), 1)

            def mod0(lo, hi):
                if lo:
                    pe.wait_ge(S("mod_cols"), 1)
                for u in range(lo, hi):
                    pe.wait_ge(S("gemv_done"), 2 * u + 2)
                    mod_cols(u, 4 * u)

            def turn_x(n):
                pe.wait_ge(S("xhat_ready"), 2 * n + 2)
                for c in range(4):
                    for kk in range(2):
                        for b in range(NB):
                            last = tr(bank[c][:, kk * T + b * P:kk * T + (b + 1) * P],
                                      xhat[:, b, (2 * c + kk) * P:(2 * c + kk + 1) * P])
                    last.then_inc(S("xT_ps"), 1)

            def hT_ready(n):
                pe.wait_ge(S("hT_act"), 4 * n + 4)
                pe.wait_ge(S("hT_dve"), 4 * n + 4)

            def gate_row(n):
                L, sec = n // 2, (G_M if n % 2 == 0 else G_F)
                pe.wait_ge(S("mod_cols"), (2, 2, 3, 3)[n])
                for k in range(KD):
                    last = mm(bank[4 + k // 4][:, (k % 4) * P:(k % 4 + 1) * P], bcol(mod[:, L, sec, k:k + 1]),
                              ident[:, :], start=True, stop=True)
                last.then_inc(S("grow_ps"), 1)

            turn_x(0)
            mod0(0, 4)
            hT_ready(0)
            loaded(pe, 0)
            for b in range(NB):
                for k in range(KD):
                    last = mm(bank[4 + b], hT[:, k, b * P:(b + 1) * P], u3(0)[:, k, :], start=k == 0, stop=k == KD - 1)
                last.then_inc(S("q_ps"), 1)
            loaded(pe, 1)
            for b in range(NB):
                for k in range(KD):
                    last = mm(bank[6][:, b * 256:(b + 1) * 256], hT[:, k, b * P:(b + 1) * P], u3(1)[:, k, 0:256],
                              start=k == 0, stop=k == KD - 1)
            last.then_inc(S("kv_ps"), 1)

            def feature_tile(dst, w):
                for k in range(KD):
                    last = mm(dst, w[:, k, :], hT[:, k, :], start=k == 0, stop=k == KD - 1)
                return last

            for j in range(LT):
                at = 768 + j * P
                if j == 2:
                    mod0(4, 6)
                    loaded(pe, 2)
                w = u3(at // HALF)[:, :, at % HALF:at % HALF + P]
                last = feature_tile(bank[j // 2][:, (j % 2) * T:(j % 2 + 1) * T], w)
                if j % 2:
                    last.then_inc(S("xr_ps"), 1)
            for j in range(LT):
                at = 1280 + j * P
                if j < 2:
                    mod0(6 + j, 7 + j)
                if j == 2:
                    loaded(pe, 3)
                w = u3(at // HALF)[:, :, at % HALF:at % HALF + P]
                last = feature_tile(bank[2 + j // 2][:, (j % 2) * T:(j % 2 + 1) * T], w)
                if j % 2:
                    last.then_inc(S("gate_ps"), 1)
            for b in range(NB):
                pe.wait_ge(S("rope_done"), b + 1)
                for t in range(4):
                    last = tr(bank[4 + t // 2][:, (t % 2) * T + b * P:(t % 2) * T + (b + 1) * P],
                              qkv[:, b, t * P:(t + 1) * P])
                if b == NB - 1:
                    last.then_inc(S("qT_ps"), 1)
                for g in range(NKV):
                    last = tr(bank[6][:, g * T + b * P:g * T + (b + 1) * P], k2[:, b, g * P:(g + 1) * P])
                if b == NB - 1:
                    last.then_inc(S("kT_ps"), 1)
            mod0(8, 10)
            pe.wait_ge(S("qT_ready"), 1)
            pe.wait_ge(S("kT_ready"), 1)
            pe.wait_ge(S("xr_ready"), 1)
            pe.wait_ge(S("gate_ready"), 1)
            for b in range(NB):
                n_k = P * (b + 1)
                for i in range(4):
                    for r in range(2):
                        h = 2 * i + r
                        if b == 0:
                            dst = PS[:, r, i * P:(i + 1) * P]
                        else:
                            dst = PS[:, (4, 2)[r] + i // 2, (i % 2) * T:(i % 2 + 1) * T]
                        pp = slice(64 * r, 64 * r + 64)
                        last = mm(dst, qT[pp, i, b * P:(b + 1) * P], kT[pp, h // 4, 0:n_k], start=True, stop=True)
                last.then_inc(S("s_ps"), 1)
            f = 0
            pieces = [(0, [(hh, 0) for hh in range(0, 4)]), (0, [(hh, 0) for hh in range(4, 8)])]
            pieces += [(1, [(hh, kb) for hh in (2 * m, 2 * m + 1) for kb in range(2)]) for m in range(4)]

            def turn_p(f):
                b, part = pieces[f]
                pe.wait_ge(S("p_ready"), b + 1)
                pe.wait_ge(S("s_less_m"), b + 1)
                if f >= 2:
                    pe.wait_ge(S("pT_ready"), f - 1)
                pp = P0 if b == 0 else P1
                for m, (hh, kb) in enumerate(part):
                    last = tr(bank[6 if f % 2 == 0 else 0][:, m * P:(m + 1) * P], pp[:, hh, kb * P:(kb + 1) * P])
                last.then_inc(S("pT_ps"), 1)

            def weigh(f):
                b, part = pieces[f]
                pe.wait_ge(S("pT_ready"), f + 1)
                for m, (hh, kb) in enumerate(part):
                    r, i = hh // 4, hh % 4
                    h = 2 * i + r
                    at = (NQ + NKV) * HEAD + (h // 4) * HEAD
                    last = mm(bank[(1, 4)[b]][64 * r:64 * r + 64, i * P:(i + 1) * P], qkv[:, kb, at:at + HEAD],
                              PT[:, f % 2, m * P:(m + 1) * P], start=kb == 0, stop=kb == b)
                last.then_inc(S("pv_done"), 1)

            turn_p(0)
            for f in range(6):
                if f < 5:
                    turn_p(f + 1)
                weigh(f)
            pe.wait_ge(S("xc_ready"), 1)
            pe.wait_ge(S("gaw_in"), 64)
            for v_ in range(2):
                for j in range(LT):
                    last = mm(PS[:, (2, 5)[v_] + j // 2, (j % 2) * T:(j % 2 + 1) * T], gaw[:, v_, j, :], xc[:, j, :],
                              start=True, stop=True)
            last.then_inc(S("lru_ps"), 1)
            mod0(10, 12)
            pe.wait_ge(S("lru_ri"), 1)
            pe.wait_ge(S("attn_ready"), 1)
            gate_row(0)
            pe.wait_ge(S("lru_ready"), 1)
            for h in range(2):
                loaded(pe, N_WIN + h)
            pe.wait_ge(S("grow_ready"), 1)
            for b in range(NB):
                for h in range(2):
                    for k in range(KD):
                        last = mm(bank[2 * b + h], mixT[:, k, b * P:(b + 1) * P], u3(N_WIN + h)[:, k, :],
                                  start=k == 0, stop=k == KD - 1)
                    last.then_inc(S("m_ps"), 1)
                    if (b, h) == (0, 0):
                        pe.wait_ge(S("s5_rows"), 1)
                        for m, r in enumerate((7, 8, 9, 10, 11)):
                            last = tr(bank[6][:, m * NQT:(m + 1) * NQT], s5r[0:NQT, r, :], NQT)
                        last.then_inc(S("s5_cols_ps"), 1)
                    if (b, h) == (0, 1):
                        pe.wait_ge(S("bp_ready"), 4)
                        for v_ in range(2):
                            for hf in range(2):
                                if v_:
                                    pe.wait_ge(S("bt_evac"), 1 + hf)
                                for kk in range(4):
                                    last = tr(bank[4 + hf][:, kk * P:(kk + 1) * P], Bp[:, v_, hf * 4 + kk, :])
                                last.then_inc(S("bt_ps"), 1)
            pe.wait_ge(S("cn_in"), 64)
            for v_ in range(2):
                for hf in range(2):
                    if v_ or hf:
                        pe.wait_ge(S("ct_evac"), 2 * (2 * v_ + hf))
                    for kk in range(4):
                        last = tr(bank[6][:, kk * P:(kk + 1) * P], Cn[:, v_, hf * 4 + kk, :])
                    last.then_inc(S("ct_ps"), 1)
            pe.wait_ge(S("bt_evac"), 4)
            pe.wait_ge(S("ct_evac"), 8)
            pe.wait_ge(S("x_new"), 1)

            def ffn(L):
                n = 2 * L + 1
                n0 = MOE_BASE[L]
                turn_x(n)
                hT_ready(n)
                if L == 0:
                    pe.wait_ge(S("small_in"), 16 * 9)
                for b in range(NB):
                    for k in range(KD):
                        last = mm(bank[4][:, b * 20:b * 20 + 20], hT[:, k, b * P:(b + 1) * P], wr_sb[:, L, k, :],
                                  start=k == 0, stop=k == KD - 1)
                last.then_inc(S("router_ps"), 1)
                pe.wait_ge(S("l2_ready"), L + 1)
                oh = rt[:, 48:56].rearrange("p (b g) -> p b g", b=NB)
                mm(bank[5][:, 0:4], before[:, :], oh[:, 0, :], start=True, stop=True)
                mm(bank[5][:, 4:8], before[:, :], oh[:, 1, :], start=True, stop=False)
                mm(bank[5][:, 4:8], ones[:, :], oh[:, 0, :], start=False, stop=True).then_inc(S("rank_ps"), 1)
                pe.wait_ge(S("pick_ready"), L + 1)
                gt = rt[:, 160:168].rearrange("p (b g) -> p b g", b=NB)
                for g in range(NG + 1):
                    for b in range(NB):
                        last = mm(bank[5][:, 16 + 4 * g:20 + 4 * g], pick[:, b, g, :], gt[:, b, :], start=b == 0,
                                  stop=b == NB - 1)
                pe.wait_ge(S("ov_ready"), L + 1)
                ov = rt[:, 192:196].rearrange("p (b n) -> p b n", b=NB)
                for b in range(NB):
                    last = mm(bank[5][:, 40:42], ones[:, :], ov[:, b, :], start=b == 0, stop=b == NB - 1)
                last.then_inc(S("gsl_ps"), 1)

                def gather(i):
                    for k in range(KD):
                        for b in range(NB):
                            last = mm(bank[2 * (k // 4)][:, (k % 4) * P:(k % 4 + 1) * P],
                                      xhat[:, b, k * P:(k + 1) * P], pick[:, b, i, :], start=b == 0, stop=b == NB - 1)
                        if k in (3, 7):
                            last.then_inc(S("gathered"), 1)

                gather(0)
                with pe.Fori(0, NG) as i:
                    e0 = 16 * L + 4 * i

                    def up(e):
                        if e == 0:
                            pe.wait_ge(S("hg_act"), 5 * L + i + 1)
                            pe.wait_ge(S("hg_dve"), 5 * L + i + 1)
                        for w, sem, last_reader, bk in (("w1", "a_ps", "sil_ready", 0), ("w3", "b_ps", "he_ready", 2)):
                            j = AT[(w, e)]
                            loaded(pe, n0 + j, i)
                            if e >= 1 or L == 1:
                                pe.wait_ge(S(last_reader), e0 + e - 1 + PRIMED.get(last_reader, 0))
                            for k in range(KD):
                                last = mm(bank[bk + e % 2], hg[:, k, :], u3(n0 + j)[:, k, :], start=k == 0,
                                          stop=k == KD - 1)
                            last.then_inc(S(sem), 1)

                    def down(e):
                        pe.wait_ge(S("he_ready"), 1 + e0 + e + 1)
                        pe.wait_ge(S("heT_ready"), 1 + e0 + e)
                        for c4 in range(4):
                            last = tr(bank[6][:, c4 * P:(c4 + 1) * P], he[:, c4 * P:(c4 + 1) * P])
                        last.then_inc(S("heT_ps"), 1)
                        j = AT[("w2", e)]
                        loaded(pe, n0 + j, i)
                        pe.wait_ge(S("heT_ready"), 1 + e0 + e + 1)
                        if e == 0:
                            pe.wait_ge(S("y_act"), 1 + NG * L + i)
                            pe.wait_ge(S("y_dve"), 1 + NG * L + i)
                        for h in range(2):
                            for c4 in range(KF):
                                last = mm(bank[4 + h], heT[:, c4 * P:(c4 + 1) * P],
                                          u3(n0 + j, D)[:, c4, h * HALF:(h + 1) * HALF],
                                          start=e == 0 and c4 == 0, stop=e == EPG - 1 and c4 == KF - 1)
                        last.then_inc(S("y_ps"), 1)

                    up(0)
                    up(1)
                    down(0)
                    up(2)
                    down(1)
                    up(3)
                    down(2)
                    pe.wait_ge(S("sil_ready"), 1 + e0 + 3)
                    pe.wait_ge(S("he_ready"), 1 + e0 + 3)
                    gather(i + 1)
                    down(3)
                    if L == 0:
                        pe.wait_ge(S("gemv_done"), A_HALVES + 6 + 6 * i)
                        pe.wait_ge(S("mod_cols"), 2)
                        pe.wait_ge(S("mod1_evac"), 1 + i)
                        for u in range(3):
                            mod_cols(u, 64 + 4 * u)
                pe.wait_ge(S("he_ready"), 1 + 16 * L + 16)
                pe.wait_ge(S("sil_ready"), 1 + 16 * L + 16)
                pe.wait_ge(S("hg_act"), 5 * L + 5)
                pe.wait_ge(S("hg_dve"), 5 * L + 5)
                for g in range(NG):
                    for b in range(NB):
                        last = tr(bank[g // 2][:, (g % 2) * T + b * P:(g % 2) * T + (b + 1) * P], pick[:, b, g, :])
                last.then_inc(S("pickT_ps"), 1)
                pe.wait_ge(S("y_act"), 1 + NG * (L + 1))
                pe.wait_ge(S("y_dve"), 1 + NG * (L + 1))
                gate_row(n)
                pe.wait_ge(S("pickT_ready"), L + 1)
                for b in range(NB):
                    for h in range(2):
                        for g in range(NG):
                            last = mm(bank[2 * b + h], pickT[:, g, b * P:(b + 1) * P],
                                      yg[:, g, h * HALF:(h + 1) * HALF], start=g == 0, stop=g == NG - 1)
                        last.then_inc(S("sc_ps"), 1)
                pe.wait_ge(S("over_known"), L + 1)
                n_over = pe.value_load(rti[0:1, 0:1], min_val=0, max_val=T)
                with pe.If(n_over > 0):
                    pe.wait_ge(S("x_main"), L + 1)
                    for _ in range(3):
                        pe.sem_inc(S(f"over_used{L}"), 1)
                    with pe.Fori(0, EPG) as e:
                        for j in range(2):
                            pe.wait_ge(S(f"over_in{L}_{j}"), 16 * (e + 1))
                            for k in range(KD):
                                last = mm(bank[2 * j], hg[:, k, :], u3(j)[:, k, :], start=k == 0, stop=k == KD - 1)
                            last.then_inc(S(f"over_used{L}"), 1)
                        pe.wait_ge(S(f"over_he{L}"), e + 1)
                        for c4 in range(4):
                            last = tr(bank[6][:, c4 * P:(c4 + 1) * P], he[:, c4 * P:(c4 + 1) * P])
                        last.then_inc(S(f"over_heT{L}"), 1)
                        pe.wait_ge(S(f"over_hT{L}"), e + 1)
                        pe.wait_ge(S(f"over_yg{L}"), 1 + e)
                        pe.wait_ge(S(f"over_in{L}_2"), 16 * (e + 1))
                        for h in range(2):
                            for c4 in range(KF):
                                last = mm(bank[4 + h], heT[:, c4 * P:(c4 + 1) * P],
                                          u3(2, D)[:, c4, h * HALF:(h + 1) * HALF], start=c4 == 0, stop=c4 == KF - 1)
                        last.then_inc(S(f"over_used{L}"), 1)
                    pe.wait_ge(S(f"over_yg{L}"), 1 + EPG)
                    for b in range(NB):
                        last = tr(bank[6][:, b * P:(b + 1) * P], pick[:, b, NG, :])
                    last.then_inc(S(f"over_pT{L}"), 1)
                    pe.wait_ge(S(f"over_pick{L}"), 1)
                    for b in range(NB):
                        for h in range(2):
                            last = mm(bank[2 * b + h], pickT[:, 0, b * P:(b + 1) * P],
                                      yg[:, 0, h * HALF:(h + 1) * HALF], start=True, stop=True)
                    last.then_inc(S(f"over_sc{L}"), 1)
                pe.wait_ge(S("x_new"), 2 * L + 2)

            ffn(0)

            turn_x(2)
            gate_row(2)
            pe.wait_ge(S("grow_ready"), 3)
            hT_ready(2)

            def bu(k, m, j):
                if j == 0:
                    pe.wait_ge(S("cur_ready"), k + 1)
                for q4 in (2 * j, 2 * j + 1):
                    pp = slice(32 * q4, 32 * q4 + 32)
                    for w in range(2):
                        last = mm(PS[:, q4, w * T:(w + 1) * T], bcur[pp, m, w, :], ucur[pp, m, :], start=True, stop=True)
                    last.then_inc(S("bu_ready"), 1)

            bu(0, 0, 0)
            bu(0, 0, 1)
            with pe.Fori(0, KD // 2) as kk:
                for m, j in ((0, 0), (0, 1), (1, 0), (1, 1)):
                    n = 4 * kk + 2 * m + j
                    pe.wait_ge(S("bu_used"), 1 + n + 1)
                    bu(2 * kk + m + 1, 1 - m, j)
                    if j == 0:
                        pe.wait_ge(S("yv_ready"), 1 + 2 * kk + m)
                    pe.wait_ge(S("q_ready"), 2 + n + 1)
                    for q_ in range(2):
                        q4 = 2 * j + q_
                        for w in range(4):
                            last = mm(bank[4][32 * q4:32 * q4 + 32, 0:T], ccur[:, m, w // 2, 32 * q4:32 * q4 + 32],
                                      qq[j][:, w, q_ * T:(q_ + 1) * T], start=w == 0, stop=w == 3)
                    last.then_inc(S("q_used"), 1)
            pe.wait_ge(S("act_ready"), 1 + KD)
            pe.wait_ge(S("glub_in"), 16)
            for h in range(2):
                for part in range(2):
                    n = GLU_BASE + 2 * h + part
                    loaded(pe, n)
                    r = h + 2 * part
                    for b in range(NB):
                        dst = bank[4 * h + 2 * part + b]
                        mm(dst, bcol(ident[0:4, r:r + 1]), glub, start=True, stop=False)
                        for k in range(KD):
                            last = mm(dst, actT[:, k, b * P:(b + 1) * P], u3(n)[:, k, :], start=False, stop=k == KD - 1)
                    last.then_inc(S("glu_ps"), 1)
            pe.wait_ge(S("x_new"), 3)
            ffn(1)


_OUT = (1, T, D)


def kernel(**inputs):
    import numpy as np
    import concourse.bacc as bacc
    from concourse.bass_utils import run_bass_kernel_spmd

    nc = bacc.Bacc("TRN2", target_bir_lowering=False, num_devices=1)
    arrays, a = {}, {}
    for name, value in inputs.items():
        value = np.ascontiguousarray(value)
        arrays[f"in_{name}"] = value
        a[name] = nc.dram_tensor(f"in_{name}", value.shape, mybir.dt.from_np(value.dtype), kind="ExternalInput").ap()
    out = nc.dram_tensor("out", _OUT, F32, kind="ExternalOutput").ap()
    build(nc, a, out)
    r = run_bass_kernel_spmd(nc, [arrays], core_ids=[0])
    return r.results[0]["out"]
```

```python
from contextlib import ExitStack

import concourse.bass as bass
from concourse import mybir

F32 = mybir.dt.float32
I32 = mybir.dt.int32
ALU = mybir.AluOpType
ACT = mybir.ActivationFunctionType
AX = mybir.AxisListType

P = 128
D = 1024
T = 256
NB = T // P
KD = D // P
HALF = 512
CHUNK = 64
HEAD = 64
NQ, NKV = 8, 2
ROT = HEAD // 4
RH = ROT // 2
LRU = 512
LT = LRU // P
CONV = 4
IN_W = NQ * HEAD + 2 * NKV * HEAD + 2 * LRU
NG, EPG = 4, 4
FF = 512
KF = FF // P
EPS = 1e-6
SCALE = HEAD ** -0.5
ROPE_THETA = 500000.0
STATE, CH = 64, 16
NQT = 32
PI = 3.14159265358979
MAGIC = 12582912.0
TWO_PI = (6.28125, 0.0019340515136718750, 1.2556659817695618e-06)

SLOTS = 6
SLOT = 4096
ASLOTS = 2
ASLOT = 2048
N_WIN, N_WOUT, N_GLU = 4, 2, 4
PER_GROUP = 3 * EPG
N_MOE = NG * PER_GROUP
ADA_BASE = N_WIN + N_WOUT + N_MOE
GLU_BASE = ADA_BASE + 2
MOE_BASE = (N_WIN + N_WOUT, GLU_BASE + N_GLU)
ORDER = [("w1", 0), ("w3", 0), ("w1", 1), ("w3", 1), ("w2", 0), ("w1", 2), ("w3", 2), ("w2", 1),
         ("w1", 3), ("w3", 3), ("w2", 2), ("w2", 3)]
AT = {key: n for n, key in enumerate(ORDER)}
A_HALVES = 24
A_UNITS = 12
RING_ADA = {0: (4, 0), 1: (5, 0), 2: (3, 0), 4: (4, 1), 5: (5, 1)}
A_HALF0 = [2 * u + kh for u in range(A_UNITS) if u not in RING_ADA for kh in range(2)]
A_MOE = 4
SH_M, SC_M, G_M, SH_F, SC_F, G_F = range(6)

PRIMED = dict.fromkeys(('bu_ready', 'q_used', 'yv_ready', 'q_ready', 'bu_used', 'he_ready', 'y_dve', 'mod1_evac', 'over_yg0', 'over_yg1', 'act_ready', 'heT_ready', 'y_act', 'sil_ready'), 1)
PRIMED.update(q_used=2, q_ready=2)

ROWS = {}
_at = 0
for _name, _n in (("mix0", KD), ("ffn0", KD), ("mix1", KD), ("ffn1", KD), ("s5d", KD),
                  ("conv_w", CONV * LT), ("conv_b", LT), ("ga_b", LT), ("gx_b", LT), ("lam", LT)):
    ROWS[_name] = (_at, _n)
    _at += _n
N_ROWS = _at
WORK = 15712


class Chain:

    def __init__(self, eng, sem):
        self.eng, self.sem, self.n, self.off = eng, sem, 0, 0

    def link(self, ins):
        ins.then_inc(self.sem, 1)
        self.n += 1
        self.eng.wait_ge(self.sem, self.off + self.n)

    def enter(self, i, per):
        self.off, self.start, self.per = i * per, self.n, per

    def leave(self, turns):
        assert self.n - self.start == self.per, (self.n - self.start, self.per)
        self.n, self.off = self.start + self.per * turns, 0


def build(nc, a, out):
    ctx = ExitStack()
    with ctx:
        def sb(name, shape, dt=F32):
            return ctx.enter_context(nc.sbuf_tensor(name, shape, dt))

        sems = {}

        def S(name):
            if name not in sems:
                sems[name] = ctx.enter_context(nc.semaphore(name))
            return sems[name]

        ring = sb("ring", [P, SLOTS, SLOT])
        x = sb("x", [P, NB, D])
        xhat = sb("xhat", [P, NB, D])
        hT = sb("hT", [P, KD, T])
        yg = sb("yg", [P, NG, D])
        grow = sb("grow", [P, D])
        ident = sb("ident", [P, P])
        ones = sb("ones", [P, P])
        before = sb("before", [P, P])
        slot_no = sb("slot_no", [P, P])
        cols = sb("cols", [P, N_ROWS])
        mod = sb("mod", [P, 2, 6, KD])
        modA = sb("modA", [P, 4, KD])
        adab = sb("adab", [P, 2, 6 * KD])
        stat = sb("stat", [P, 8])
        condc = sb("condc", [P, KD])
        wr_sb = sb("wr_sb", [P, 2, KD, NG + NG * EPG])
        rb = sb("rb", [P, 2, NG + NG * EPG])
        rt = sb("rt", [P, 320])
        rti = sb("rti", [P, 2 + NG], I32)
        slot_hi = sb("slot_hi", [P, P])
        half_of = sb("half_of", [P, 2])
        work = sb("work", [P, WORK])
        PS = ctx.enter_context(nc.psum_tensor("PS", [P, 8, HALF], F32))
        bank = [PS[:, i, :] for i in range(8)]

        def w3(off, *dims):
            n = 1
            for d in dims:
                n *= d
            v = work[:, off:off + n]
            if len(dims) == 1:
                return v
            names = " ".join("abcd"[:len(dims)])
            return v.rearrange(f"p ({names}) -> p {names}", **dict(zip("abcd", dims)))

        aring = w3(0, ASLOTS, ASLOT)
        acc = w3(ASLOTS * ASLOT, 3, HALF)
        W0 = ASLOTS * ASLOT + 3 * HALF
        T0 = WORK - 3 * 2 * KD * P - 5 * NQT
        rows = yg[0:N_ROWS, 0, 0:P]
        crow = yg[0:KD, 0, P:2 * P]
        brow = yg[0:6 * KD, 1, 0:2 * P].rearrange("r (l p) -> r l p", l=2)
        o = W0
        qkv = w3(o, NB, 768); o += NB * 768
        qT = w3(o, 4, T); o += 4 * T
        kT = w3(o, NKV, T); o += NKV * T
        xr = w3(o, LT, T); o += LT * T
        xc = w3(o, LT, T); o += LT * T
        gate = w3(o, LT, T); o += LT * T
        gaw = w3(o, 2, LT, P); o += 2 * LT * P
        rope = w3(o, 8, NB * RH); o += 8 * NB * RH
        rq = w3(o, 4, 10 * RH); o += 4 * 10 * RH
        smx = w3(o, 5, NB * NQ); o += 5 * NB * NQ
        sink = w3(o, NQ); o += NQ
        sp = w3(o, 4, LT); o += 4 * LT
        assert o <= WORK - 4 * NQT * 16, o
        mixT = yg[:, 0:2, :].rearrange("p a (k t) -> p (a k) t", t=T)
        lr_r = yg[:, 2, :].rearrange("p (k t) -> p k t", t=T)
        lr_i = yg[:, 3, :].rearrange("p (k t) -> p k t", t=T)
        P0 = hT[:, 0:4, :].rearrange("p k t -> p (k t)").rearrange("p (h n) -> p h n", n=P)
        PT = hT[:, 4:8, :].rearrange("p k t -> p (k t)").rearrange("p (s n) -> p s n", n=HALF)
        P1 = xhat[:, :, :].rearrange("p b n -> p (b n)").rearrange("p (h n) -> p h n", n=T)
        k2 = xhat[:, 0, 0:HALF].rearrange("p (b n) -> p b n", b=NB)
        lr_t = xhat[:, 0, :].rearrange("p (k t) -> p k t", t=T)
        lr_u = xhat[:, 1, :].rearrange("p (k t) -> p k t", t=T)
        o = W0
        pick = w3(o, NB, NG + 1, P); o += NB * (NG + 1) * P
        sil = w3(o, HALF); o += HALF
        he = w3(o, HALF); o += HALF
        heT = w3(o, HALF); o += HALF
        gsl = w3(o, NG + 1, EPG + 2); o += (NG + 1) * (EPG + 2)
        gcur = w3(o, EPG + 2); o += EPG + 2
        slotv = [heT[:, g * P:(g + 1) * P] for g in range(NG)] + [he[:, 0:P]]
        Et = w3(o, 2, NQT * 8); o += 2 * NQT * 8
        Ew = w3(o, 5, NQT); o += 5 * NQT
        assert o <= T0, o
        hg = hT[:, 0:4, :].rearrange("p k t -> p (k t)").rearrange("p (k s) -> p k s", s=P)
        pickT = hT[:, 4:8, :].rearrange("p k t -> p (k t)").rearrange("p (g t) -> p g t", t=T)
        o = T0
        BT = w3(o, 2, KD, P); o += 2 * KD * P
        CT = w3(o, 2, KD, P); o += 2 * KD * P
        s5c = w3(o, 5, NQT); o += 5 * NQT
        E = w3(o, 4, NQT, 16)
        Bl = w3(o, 2, NQT, CH)
        s5i = w3(o + 2 * NQT * CH, 3, P)
        o += 4 * NQT * 16
        assert o == WORK
        o = W0
        s5r = w3(o, 20, P); o += 20 * P
        bt1 = w3(o, NQT, CH); o += NQT * CH
        bt2 = w3(o, NQT, CH); o += NQT * CH
        assert o <= T0, o
        Bp = hT[:, :, :].rearrange("p k t -> p (k t)").rearrange("p (v k n) -> p v k n", v=2, n=P)
        Cn = yg[:, 2:4, :].rearrange("p v (k n) -> p v k n", n=P)
        o = 0
        cs = w3(o, 2, 2, HALF); o += 4 * HALF
        pr = w3(o, 4, HALF); o += 4 * HALF
        gg = w3(o, 2, HALF); o += 2 * HALF
        q_a = w3(o, 4, HALF); o += 4 * HALF
        bcur = w3(o, 2, 2, P); o += 4 * P
        ccur = w3(o, 2, 2, P); o += 4 * P
        ucur = w3(o, 2, T); o += 2 * T
        yv = w3(o, T); o += T
        dcur = w3(o, 2); o += 2
        assert o <= T0, o
        qq = [q_a, xhat[:, :, :].rearrange("p b (h n) -> p (b h) n", n=HALF)]
        ctmp = yg[:, 1, :].rearrange("p (v n) -> p v n", v=2)
        actT = yg[:, 2:4, :].rearrange("p a (k t) -> p (a k) t", t=T)
        glub = yg[0:4, 0, 0:HALF]
        arow = yg[0:1, 0, HALF:]
        fing = hT[:, 0:4, :].rearrange("p k t -> p (k t)")

        def col(name, k):
            at, n = ROWS[name]
            return cols[:, at + k:at + k + 1]

        def unit_dst(n):
            return ring[:, n % SLOTS, :]

        def loaded(eng, n, i=None):
            v = 16 * (n // SLOTS + 1)
            if n >= MOE_BASE[1] and (n - ADA_BASE) % SLOTS < 2:
                v -= 16
            eng.wait_ge(S(f"loaded{n % SLOTS}"), v if i is None else v + i * (16 * PER_GROUP // SLOTS))

        def u3(n, c=HALF):
            return ring[:, n % SLOTS, :].rearrange("p (k c) -> p k c", c=c)

        ada_v = a["ada_w"].rearrange("l (k p) n -> l p k n", p=P)
        w1_v = a["moe_w1"].rearrange("l e (k p) f -> l p e k f", p=P)
        w3_v = a["moe_w3"].rearrange("l e (k p) f -> l p e k f", p=P)
        w2_v = a["moe_w2"].rearrange("l e (k p) n -> l p e k n", p=P)
        moe_v = {"w1": w1_v, "w3": w3_v, "w2": w2_v}
        MAXG = NG - 1

        def moe_src(L, w, e):
            return moe_v[w][L, :, e, :, :]

        block = ctx.enter_context(nc.Block())

        @block.sync
        def _(sp_):
            reader = {0: ("q_ps", 2), 1: ("xr_ps", 1), 2: ("gate_ps", 1), 3: ("gate_ps", 2), 4: ("m_ps", 3),
                      5: ("m_ps", 4)}
            reader.update({ADA_BASE + j: ("mod_ps", A_UNITS + A_MOE + 2 * (6 + j) + 1) for j in range(2)})
            reader.update({GLU_BASE + j: ("glu_ps", j + 1) for j in range(N_GLU)})
            signal = {"w1": "a_ps", "w3": "b_ps", "w2": "y_ps"}

            def free_slot(n):
                m = n - SLOTS
                if m < 0:
                    return
                if m in reader:
                    sp_.wait_ge(S(reader[m][0]), reader[m][1])
                else:
                    L = int(m >= MOE_BASE[1])
                    w, e = ORDER[(m - MOE_BASE[L]) % PER_GROUP]
                    sp_.wait_ge(S(signal[w]), 16 * L + EPG * ((m - MOE_BASE[L]) // PER_GROUP) + e + 1)

            def send(n, src, c, width):
                free_slot(n)
                sp_.dma_start(u3(n, c)[:, :, 0:width], src).then_inc(S(f"loaded{n % SLOTS}"), 16)

            def send_expert(L, j, group):
                w, e = ORDER[j]
                sp_.dma_start(u3(MOE_BASE[L] + j, D if w == "w2" else FF), moe_src(L, w, group * EPG + e)).then_inc(
                    S(f"loaded{(MOE_BASE[L] + j) % SLOTS}"), 16)

            def send_ada(u):
                slot = RING_ADA[u][0]
                sp_.dma_start(u3(slot), ada_v[0, :, :, u * HALF:(u + 1) * HALF]).then_inc(S(f"ada_ring{slot}"), 16)

            win = a["ab_w_in"][0].rearrange("(k p) n -> p k n", p=P)
            for u in (0, 1, 2):
                send_ada(u)
            sp_.wait_ge(S("rows_in"), 16 * (len(ROWS) + 2))
            for j in range(N_WIN):
                w = min(HALF, IN_W - j * HALF)
                if j == 3:
                    sp_.wait_ge(S("gemv_done"), 2)
                    send_ada(4)
                    sp_.wait_ge(S("gemv_done"), 6)
                send(j, win[:, :, j * HALF:j * HALF + w], HALF, w)
            send_ada(5)
            wout = a["ab_w_out"][0].rearrange("(k p) n -> p k n", p=P)
            for j in range(N_WOUT):
                sp_.wait_ge(S("gemv_done"), 2 * (4 + j) + 2)
                send(N_WIN + j, wout[:, :, j * HALF:(j + 1) * HALF], HALF, HALF)
            for L in range(2):
                n0 = MOE_BASE[L]
                for j in range(SLOTS):
                    free_slot(n0 + j)
                    send_expert(L, j, 0)
                with sp_.Fori(0, NG - 1) as i:
                    for half in range(2):
                        for j in range(SLOTS):
                            w, e = ORDER[j + (0 if half == 0 else SLOTS)]
                            sp_.wait_ge(S(signal[w]), 16 * L + e + 1 + i * EPG)
                            send_expert(L, j + (SLOTS if half == 0 else 0), i + half)
                for j in range(SLOTS, PER_GROUP):
                    free_slot(n0 + (NG - 1) * PER_GROUP + j)
                    send_expert(L, j, NG - 1)
                sp_.wait_ge(S("over_known"), L + 1)
                n_over = sp_.value_load(rti[0:1, 0:1], min_val=0, max_val=T)
                grp = sp_.value_load(rti[0:1, 1:2], min_val=0, max_val=MAXG)
                with sp_.If(n_over > 0):
                    with sp_.Fori(0, EPG // 2) as ee:
                        for j in range(SLOTS):
                            w = ("w1", "w3", "w2")[j % 3]
                            sp_.wait_ge(S(f"over_used{L}"), ee * SLOTS + (j + 1))
                            cw = D if w == "w2" else FF
                            sp_.dma_start(u3(j, cw), moe_src(L, w, grp * EPG + ee * 2 + j // 3)).then_inc(
                                S(f"over_in{L}_{j}"), 16)
                    sp_.wait_ge(S(f"over_used{L}"), SLOTS + 3 * EPG)
                if L == 0:
                    glu = a["s5_glu_w"][0].rearrange("(k p) n -> p k n", p=P)
                    for j in range(A_UNITS - A_MOE):
                        if j == 2:
                            for jj, q in enumerate((0, 2, 1, 3)):
                                send(GLU_BASE + jj, glu[:, :, q * HALF:(q + 1) * HALF], HALF, HALF)
                        if j < 2:
                            free_slot(ADA_BASE + j)
                        else:
                            sp_.wait_ge(S("mod_ps"), A_UNITS + A_MOE + 2 * (j - 2) + 1)
                        sp_.dma_start(u3(ADA_BASE + j % 2), ada_v[1, :, :, (A_MOE + j) * HALF:(A_MOE + j + 1) * HALF]
                                      ).then_inc(S(f"ada_ring{4 + j % 2}"), 16)
            for b in range(NB):
                sp_.wait_ge(S("out_ready"), b + 1)
                sp_.dma_start(out[0, b * P:(b + 1) * P, :], xhat[:, b, :]).then_inc(S("out_stored"), 16)
            sp_.wait_ge(S("out_stored"), 16 * NB)

        @block.gpsimd
        def _(pool):
            g = nc.gpsimd
            ch = Chain(pool, S("pool_order"))
            ch.link(g.memset(ident[:, :], 0.0))
            g.affine_select(out=ident[:, :], in_=ident[:, :], compare_op=ALU.not_equal, fill=1.0, base=0,
                            pattern=[[-1, P]], channel_multiplier=1).then_inc(S("ident_ready"), 1)

            def ada_load(h, j, wait):
                L, r = h
                if wait is not None:
                    pool.wait_ge(S("gemv_done"), wait)
                u, kh = r // 2, r % 2
                pool.dma_start(aring[:, j % ASLOTS, :].rearrange("p (k c) -> p k c", c=HALF),
                               ada_v[L, :, kh * 4:kh * 4 + 4, u * HALF:(u + 1) * HALF]).then_inc(
                                   S(f"ada_in{j % ASLOTS}"), 16)

            for j, r in enumerate(A_HALF0[:ASLOTS]):
                ada_load((0, r), j, None)
            ch.link(g.memset(ones[:, :], 1.0))
            ch.link(g.affine_select(out=before[:, :], in_=ones[:, :], compare_op=ALU.is_gt, fill=0.0, base=0,
                                    pattern=[[1, P]], channel_multiplier=-1))
            g.iota(slot_no[:, :], pattern=[[1, P]], base=0, channel_multiplier=0,
                   allow_small_or_imprecise_dtypes=True).then_inc(S("consts_ready"), 1)
            ch.link(g.memset(slot_hi[:, 0:64], 0.0))
            ch.link(g.memset(slot_hi[:, 64:P], 64.0))
            ch.link(g.memset(half_of[0:64, 0:1], 0.0))
            ch.link(g.memset(half_of[64:P, 0:1], -1.0))
            ch.link(g.memset(half_of[0:64, 1:2], -1.0))
            g.memset(half_of[64:P, 1:2], 0.0).then_inc(S("consts_ready"), 1)
            pool.wait_ge(S("consts_ready"), 2)
            ch.link(g.memset(gaw[:, :, :, :], 0.0))
            for v, name in enumerate(("ab_gate_a_w", "ab_gate_x_w")):
                src = a[name][0].rearrange("(k b) d e -> b d k e", b=2)
                for b in range(2):
                    pool.dma_start(gaw[b * 64:(b + 1) * 64, v, :, b * 64:(b + 1) * 64], src[b]).then_inc(
                        S("gaw_in"), 16)
            for j, r in enumerate(A_HALF0):
                if j >= ASLOTS:
                    ada_load((0, r), j, A_HALF0[j - ASLOTS] + 1)
            pool.wait_ge(S("lru_ready"), 1)
            pool.wait_ge(S("pv_done"), 6)
            g.memset(Bp[:, :, :, :], 0.0).then_inc(S("tables_zero"), 1)
            g.memset(CT[:, :, :, :], 0.0).then_inc(S("tables_zero"), 1)
            pool.wait_ge(S("bp_ready"), 4)
            w32 = lambda m: Ew[:, m, :]
            ch.link(g.tensor_copy(w32(0), s5c[:, 1, :]))
            ch.link(g.tensor_copy(w32(1), s5c[:, 2, :]))
            for table in (1, 0):
                Ec, Es = E[:, 2 * table, :, :], E[:, 2 * table + 1, :, :]
                g.memset(Ec[:, :, 0:1], 1.0)
                ch.link(g.memset(Es[:, :, 0:1], 0.0))
                for n_ in (1, 2, 4, 8):
                    c_b = w32(0).unsqueeze(2).to_broadcast([P, NQT, n_])
                    s_b = w32(1).unsqueeze(2).to_broadcast([P, NQT, n_])
                    te = [Et[:, m, 0:NQT * n_].rearrange("p (q n) -> p q n", n=n_) for m in range(2)]
                    g.tensor_tensor(te[0], Ec[:, :, 0:n_], c_b, ALU.mult)
                    ch.link(g.tensor_tensor(te[1], Es[:, :, 0:n_], s_b, ALU.mult))
                    ch.link(g.tensor_tensor(Ec[:, :, n_:2 * n_], te[0], te[1], ALU.subtract))
                    g.tensor_tensor(te[0], Ec[:, :, 0:n_], s_b, ALU.mult)
                    ch.link(g.tensor_tensor(te[1], Es[:, :, 0:n_], c_b, ALU.mult))
                    ch.link(g.tensor_tensor(Es[:, :, n_:2 * n_], te[0], te[1], ALU.add))
                    g.tensor_tensor(w32(2), w32(0), w32(0), ALU.mult)
                    g.tensor_tensor(w32(3), w32(1), w32(1), ALU.mult)
                    ch.link(g.tensor_tensor(w32(4), w32(0), w32(1), ALU.mult))
                    ch.link(g.tensor_tensor(w32(0), w32(2), w32(3), ALU.subtract))
                    ch.link(g.tensor_scalar(w32(1), w32(4), 2.0, None, ALU.mult))
            with pool.Fori(0, NG) as i:
                for j in range(2):
                    pool.wait_ge(S("gemv_done"), A_HALVES + j - ASLOTS + 1 + i * 2)
                    src = ada_v[1, :, j * 4:j * 4 + 4, bass.ds(i * HALF, HALF)]
                    pool.dma_start(aring[:, j % ASLOTS, :].rearrange("p (k c) -> p k c", c=HALF), src).then_inc(
                        S(f"ada_in{j % ASLOTS}"), 16)

            pool.wait_ge(S("x_new"), 2)
            with pool.Fori(0, KD) as k:
                for j in range(2):
                    if j == 0:
                        pool.wait_ge(S("q_ready"), 1 + 2 * k)
                    else:
                        pool.wait_ge(S("q_ready"), 2 + 2 * k)
                    q0 = 4 * k + 2 * j
                    e1c, e1s, e2c, e2s = [E[:, v, bass.ds(q0, 2), :] for v in range(4)]

                    def outer(v):
                        return v.unsqueeze(3).to_broadcast([P, 2, 16, 16])

                    def inner(v):
                        return v.unsqueeze(2).to_broadcast([P, 2, 16, 16])

                    def t4(v):
                        return v.rearrange("p (q a j) -> p q a j", q=2, a=16)

                    n_tab = 4 * k + 2 * j
                    c_, s_ = cs[:, j, 0, :], cs[:, j, 1, :]
                    g.tensor_tensor(t4(c_), outer(e1c), inner(e2c), ALU.mult)
                    g.tensor_tensor(t4(ctmp[:, 0, :]), outer(e1s), inner(e2s), ALU.mult).then_inc(S("tab_step"), 1)
                    pool.wait_ge(S("tab_step"), n_tab + 1)
                    g.tensor_tensor(c_, c_, ctmp[:, 0, :], ALU.subtract)
                    g.tensor_tensor(t4(s_), outer(e1s), inner(e2c), ALU.mult)
                    g.tensor_tensor(t4(ctmp[:, 1, :]), outer(e1c), inner(e2s), ALU.mult).then_inc(S("tab_step"), 1)
                    pool.wait_ge(S("tab_step"), n_tab + 2)
                    g.tensor_tensor(s_, s_, ctmp[:, 1, :], ALU.add).then_inc(S("tab_ready"), 1)

        @block.scalar
        def _(act):
            s = nc.scalar
            for name in ('act_ready', 'heT_ready', 'y_act', 'sil_ready'):
                act.sem_inc(S(name), PRIMED[name])
            ch = Chain(act, S("act_order"))
            act.dma_start(crow, a["c"][0].rearrange("(k p) -> k p", p=P)).then_inc(S("c_in"), 16)
            act.dma_start(x[:, :, :], a["x"][0].rearrange("(b p) n -> p b n", p=P)).then_inc(S("x_in"), 16)
            names = {"mix0": a["norm_mix_g"][0:1], "ffn0": a["norm_ffn_g"][0:1],
                     "mix1": a["norm_mix_g"][1:2], "ffn1": a["norm_ffn_g"][1:2],
                     "conv_b": a["ab_conv_b"], "ga_b": a["ab_gate_a_b"], "gx_b": a["ab_gate_x_b"],
                     "lam": a["ab_lambda"]}
            for name, (at, n) in ROWS.items():
                dst = rows[at:at + n, :]
                if name == "s5d":
                    src = a["s5_d"][0].rearrange("(k g) c -> k (g c)", k=KD)
                elif name == "conv_w":
                    src = a["ab_conv_w"][0].rearrange("j (k p) -> (j k) p", p=P)
                else:
                    src = names[name][0].rearrange("(k p) -> k p", p=P)
                act.dma_start(dst, src).then_inc(S("rows_in"), 16)
            for L in range(2):
                act.dma_start(brow[:, L, :], a["ada_b"][L].rearrange("(r p) -> r p", p=P)).then_inc(S("rows_in"), 16)
            act.dma_start(rti[:, 0:NB], a["positions"][0].rearrange("(b p) -> p b", p=P),
                          allow_slow_non_contiguous=True).then_inc(S("pos_in"), 16)
            act.dma_start(sink[:, :], a["ab_sinks"].to_broadcast([P, NQ])).then_inc(S("small_in"), 16)
            for L in range(2):
                act.dma_start(wr_sb[:, L, :, 0:NG], a["moe_wg"][L].rearrange("(k p) g -> p k g", p=P)).then_inc(S("small_in"), 16)
                act.dma_start(wr_sb[:, L, :, NG:], a["moe_we"][L].rearrange("(k p) g e -> p k (g e)", p=P)).then_inc(
                    S("small_in"), 16)
                act.dma_start(rb[:, L, 0:NG], a["moe_bg"][L:L + 1].to_broadcast([P, NG])).then_inc(S("small_in"), 16)
                act.dma_start(rb[:, L, NG:], a["moe_be"][L:L + 1].rearrange("l g e -> l (g e)").to_broadcast(
                    [P, NG * EPG])).then_inc(S("small_in"), 16)

            s5_rows = a["s5_a_re"][0].rearrange("(q g) p -> q (g p)", g=2)
            s.dma_start(s5i[0:NQT, 0, :], s5_rows).then_inc(S("s5_in"), 16)
            s.dma_start(s5i[0:NQT, 1, :], a["s5_a_im"][0].rearrange("(q g) p -> q (g p)", g=2)).then_inc(S("s5_in"), 16)
            s.dma_start(s5i[0:NQT, 2, 0:2], a["s5_log_dt"][0].rearrange("(q g) -> q g", g=2)).then_inc(S("s5_in"), 16)
            for v, name in enumerate(("s5_b_re", "s5_b_im")):
                s.dma_start(Bl[:, v, :, :], a[name][0].rearrange("(q g) p c -> (g p) q c", g=2)).then_inc(S("s5_in"), 16)
            act.wait_ge(S("c_ps"), 1)
            s.activation(condc[:, :], bank[2][:, 0:KD], ACT.Silu).then_inc(S("cond_ready"), 1)
            def norm(n):
                if n == 0:
                    act.wait_ge(S("x_in"), 16)
                else:
                    act.wait_ge(S("x_new"), n)
                s.activation(xhat[:, 0, :], x[:, 0, :], ACT.Square, accum_out=stat[:, 0:1]).then_inc(S("ss_act"), 1)
                act.wait_ge(S("var_ready"), n + 1)
                s.activation(stat[:, 4:6], stat[:, 2:4], ACT.Sqrt).then_inc(S("std_ready"), 1)

            def modulate(n):
                L, sec = n // 2, (SH_M if n % 2 == 0 else SH_F)
                act.wait_ge(S("modA_ready"), n + 1)
                for k in (0, 1, 4, 5):
                    act.wait_ge(S("xT_ps"), 4 * n + k // 2 + 1)
                    s.activation(hT[:, k, :], bank[k // 2][:, (k % 2) * T:(k % 2 + 1) * T], ACT.Identity, scale=modA[:, n, k:k + 1],
                                 bias=mod[:, L, sec, k:k + 1]).then_inc(S("hT_act"), 1)

            def gate_row(n):
                act.wait_ge(S("grow_ps"), n + 1)
                if n:
                    act.wait_ge(S("x_new"), n)
                s.activation(grow[:, 0:HALF], bank[4], ACT.Copy)
                s.activation(grow[:, HALF:], bank[5], ACT.Copy).then_inc(S("grow_ready"), 1)

            norm(0)
            act.wait_ge(S("cols_ps"), 1)
            ch.link(s.activation(cols[:, :], bank[0][:, 0:N_ROWS], ACT.Copy))
            s.activation(adab[:, :, :], bank[1][:, 0:12 * KD].rearrange("p (l n) -> p l n", l=2), ACT.Copy).then_inc(
                S("cols_ready"), 1)

            modulate(0)
            act.wait_ge(S("rope_arg"), 1)
            s.activation(rope[:, 4:6, :], rope[:, 2:4, :], ACT.Sin).then_inc(S("rope_ready"), 1)
            act.wait_ge(S("sp_arg"), 1)
            ch.link(s.activation(sp[:, 1, :], sp[:, 0, :], ACT.Exp))
            ch.link(s.activation(sp[:, 1, :], sp[:, 1, :], ACT.Ln, bias=1.0))
            s.activation(sp[:, 1, :], sp[:, 1, :], ACT.Copy).then_inc(S("sp_ln"), 1)

            for b in range(NB):
                act.wait_ge(S("q_ps"), b + 1)
                s.activation(qkv[:, b, 0:HALF], bank[4 + b], ACT.Copy).then_inc(S("q_evac"), 1)
            act.wait_ge(S("xr_ps"), 1)
            s.activation(xr[:, 0:2, :], bank[0].rearrange("p (j t) -> p j t", j=2), ACT.Copy)
            act.wait_ge(S("xr_ps"), 2)
            s.activation(xr[:, 2:4, :], bank[1].rearrange("p (j t) -> p j t", j=2), ACT.Copy).then_inc(S("xr_ready"), 1)
            act.wait_ge(S("gate_ps"), 2)
            s.activation(gate[:, :, :], PS[:, 2:4, :].rearrange("p b (j t) -> p (b j) t", j=2),
                         ACT.Gelu_apprx_tanh).then_inc(S("gate_ready"), 1)
            act.wait_ge(S("qT_ps"), 1)
            s.activation(qT[:, :, :], PS[:, 4:6, :].rearrange("p b (j t) -> p (b j) t", j=2), ACT.Copy).then_inc(
                S("qT_ready"), 1)
            for b in range(NB):
                act.wait_ge(S("s_less_m"), b + 1)
                if b == 0:
                    s.activation(P0[0:64, :, 0:64], P0[0:64, :, 0:64], ACT.Exp, scale=SCALE)
                    s.activation(P0[64:P, :, 0:P], P0[64:P, :, 0:P], ACT.Exp, scale=SCALE)
                else:
                    s.activation(P1[0:64, :, 64:192], P1[0:64, :, 64:192], ACT.Exp, scale=SCALE)
                    s.activation(P1[64:P, :, P:T], P1[64:P, :, P:T], ACT.Exp, scale=SCALE)
                s.activation(smx[:, 2, b * NQ:(b + 1) * NQ], smx[:, 1, b * NQ:(b + 1) * NQ], ACT.Exp,
                             scale=SCALE).then_inc(S("p_exp"), 1)
            for f in range(6):
                act.wait_ge(S("pT_ps"), f + 1)
                if f >= 2:
                    act.wait_ge(S("pv_done"), f - 1)
                s.activation(PT[:, f % 2, :], bank[6 if f % 2 == 0 else 0], ACT.Copy).then_inc(S("pT_ready"), 1)
            act.wait_ge(S("pv_done"), 2)
            s.activation(mixT[:, 0:4, 0:P], bank[1].rearrange("p (i t) -> p i t", i=4), ACT.Copy)
            act.wait_ge(S("pv_done"), 6)
            s.activation(mixT[:, 0:4, P:T], bank[4].rearrange("p (i t) -> p i t", i=4), ACT.Copy).then_inc(
                S("attn_ready"), 1)
            act.wait_ge(S("lru_ps"), 1)
            for j in range(LT):
                s.activation(lr_r[:, j, :], PS[:, 2 + j // 2, (j % 2) * T:(j % 2 + 1) * T], ACT.Sigmoid,
                             bias=col("ga_b", j))
            for j in range(LT):
                last = s.activation(lr_i[:, j, :], PS[:, 5 + j // 2, (j % 2) * T:(j % 2 + 1) * T], ACT.Sigmoid,
                                    bias=col("gx_b", j))
            last.then_inc(S("lru_ri"), 1)
            act.wait_ge(S("lru_ri"), 1)
            act.wait_ge(S("sp_ready"), 1)
            for j in range(LT):
                s.activation(lr_t[:, j, :], lr_r[:, j, :], ACT.Tanh, scale=sp[:, 2, j:j + 1])
            for j in range(LT):
                last = s.activation(lr_u[:, j, :], lr_r[:, j, :], ACT.Exp, scale=sp[:, 3, j:j + 1])
            last.then_inc(S("lru_a"), 1)
            act.wait_ge(S("lru_b2"), 1)
            s.activation(lr_t[:, :, :], lr_t[:, :, :], ACT.Sqrt).then_inc(S("lru_sq"), 1)
            gate_row(0)

            act.wait_ge(S("lru_ready"), 1)
            for v, name in enumerate(("s5_c_re", "s5_c_im")):
                for u in range(2):
                    s.dma_start(Cn[:, v, :, u * 64:(u + 1) * 64],
                                a[name][0].rearrange("(k g) c p -> (g c) k p", k=KD)).then_inc(S("cn_in"), 16)
            act.wait_ge(S("s5_in"), 16 * 5)
            act.wait_ge(S("pv_done"), 6)
            R = s5r
            s.activation(R[0:NQT, 4, 0:2], s5i[0:NQT, 2, 0:2], ACT.Exp).then_inc(S("s5_act"), 1)
            act.wait_ge(S("s5_th"), 1)
            s.activation(R[0:NQT, 7, :], R[0:NQT, 5, :], ACT.Exp)
            s.activation(R[0:NQT, 8:10, :], R[0:NQT, 10:12, :], ACT.Sin).then_inc(S("s5_act"), 1)
            for v in range(2):
                for hf in range(2):
                    act.wait_ge(S("bt_ps"), 2 * v + hf + 1)
                    s.activation(BT[:, v, hf * 4:hf * 4 + 4, :], bank[4 + hf].rearrange("p (k n) -> p k n", n=P),
                                 ACT.Copy).then_inc(S("bt_evac"), 1)
            for w in range(2):
                for hf in range(2):
                    act.wait_ge(S("ct_ps"), 2 * w + hf + 1)
                    for u in range(2):
                        pr_ = slice(u * 64, u * 64 + 64)
                        dst = CT[pr_, w, hf * 4:hf * 4 + 4, :].rearrange("p k (q g c) -> p (k q) g c", g=2, c=CH)[:, :, u, :]
                        src = bank[6][pr_, :].rearrange("p (k g c) -> p k g c", g=2, c=CH)[:, :, u, :]
                        s.activation(dst, src, ACT.Copy, scale=-1.0 if w else 1.0).then_inc(S("ct_evac"), 1)

            def ffn(L):
                n = 2 * L + 1
                norm(n)
                modulate(n)
                act.wait_ge(S("lg_ready"), L + 1)
                s.activation(rt[:, 64:64 + 8], rt[:, 56:56 + 8], ACT.Exp).then_inc(S("exp_ready"), 1)
                act.wait_ge(S("l2_ready"), L + 1)
                s.activation(rt[:, 86:88], rt[:, 84:86], ACT.Exp).then_inc(S("exp_ready"), 1)
                n0 = MOE_BASE[L]

                def hg_evac(i):
                    act.wait_ge(S("gathered"), 10 * L + 1 + 2 * i)
                    for k in range(0, 4):
                        last = s.activation(hg[:, k, :], bank[0][:, k * P:(k + 1) * P], ACT.Identity,
                                            scale=modA[:, n, k:k + 1], bias=mod[:, L, SH_F, k:k + 1])
                    last.then_inc(S("hg_act"), 1)

                hg_evac(0)
                with act.Fori(0, NG) as i:
                    def silu(e):
                        act.wait_ge(S("a_ps"), 16 * L + 4 * i + e + 1)
                        act.wait_ge(S("he_ready"), 1 + 16 * L + 4 * i + e)
                        s.activation(sil[:, :], bank[0 + e % 2], ACT.Silu).then_inc(S("sil_ready"), 1)

                    def he_t(e):
                        act.wait_ge(S("heT_ps"), 16 * L + 4 * i + e + 1)
                        s.activation(heT[:, :], bank[6], ACT.Copy).then_inc(S("heT_ready"), 1)

                    silu(0)
                    silu(1)
                    he_t(0)
                    silu(2)
                    he_t(1)
                    silu(3)
                    he_t(2)
                    hg_evac(i + 1)
                    he_t(3)
                    act.wait_ge(S("y_ps"), 16 * L + 4 * i + 4)
                    s.activation(yg[:, bass.ds(i, 1), 0:HALF], bank[4].unsqueeze(1), ACT.Identity, scale=gcur[:, EPG:EPG + 1]).then_inc(
                        S("y_act"), 1)
                gate_row(n)
                act.wait_ge(S("over_known"), L + 1)
                n_over = act.value_load(rti[0:1, 0:1], min_val=0, max_val=T)
                with act.If(n_over > 0):
                    with act.Fori(0, EPG) as e:
                        act.wait_ge(S(f"over_used{L}"), e * 3 + SLOTS + 2)
                        s.activation(sil[:, :], bank[0], ACT.Silu).then_inc(S(f"over_sil{L}"), 1)
                        act.wait_ge(S(f"over_heT{L}"), e + 1)
                        s.activation(heT[:, :], bank[6], ACT.Copy).then_inc(S(f"over_hT{L}"), 1)

            ffn(0)

            norm(2)
            modulate(2)
            s.dma_start(glub, a["s5_glu_b"][0].rearrange("(r n) -> r n", r=4)).then_inc(S("glub_in"), 16)

            def cur(k, m):
                s.activation(ucur[:, m, :].unsqueeze(1), hT[:, bass.ds(k, 1), :], ACT.Copy)
                s.activation(bcur[:, m, :, :].unsqueeze(2), BT[:, :, bass.ds(k, 1), :], ACT.Copy)
                s.activation(ccur[:, m, :, :].unsqueeze(2), CT[:, :, bass.ds(k, 1), :], ACT.Copy)
                s.activation(dcur[:, m:m + 1], cols[:, bass.ds(k + ROWS["s5d"][0], 1)], ACT.Copy).then_inc(
                    S("cur_ready"), 1)

            act.wait_ge(S("hT_dve"), 4 * 3)
            act.wait_ge(S("hT_act"), 4 * 3)
            cur(0, 0)
            cur(1, 1)
            with act.Fori(0, KD // 2) as kk:
                for m in range(2):
                    t = 2 * kk + m
                    act.wait_ge(S("mod_ps"), A_UNITS + A_MOE + 2 * t + 1)
                    s.activation(arow, bank[7][0:1, :], ACT.Copy).then_inc(S("ada_act"), 1)
                    act.wait_ge(S("mod_ps"), A_UNITS + A_MOE + 2 * t + 2)
                    s.activation(mod[:, 1].rearrange("p s k -> p (s k)")[:, bass.ds(4 * t + 4 * A_MOE, 4)],
                                 bank[5][:, 0:4], ACT.Copy).then_inc(S("ada_act"), 1)
                    act.wait_ge(S("yv_ready"), 2 * kk + m + 2)
                    cur((2 * kk + m + 2) % KD, m)
                    s.activation(actT[:, bass.ds(2 * kk + m, 1), :], yv[:, :].unsqueeze(1),
                                 ACT.Gelu_apprx_tanh).then_inc(S("act_ready"), 1)
            gate_row(2)
            for h in range(2):
                for b in range(NB):
                    act.wait_ge(S("glu_ps"), 2 * h + 2)
                    s.activation(q_a[:, 2 * h + b, :], bank[4 * h + 2 + b], ACT.Sigmoid).then_inc(S("glu_sig"), 1)
            ffn(1)
            act.wait_ge(S("x_new"), 4)
            act.dma_start(fing, a["final_g"].rearrange("(o n) -> o n", o=1).to_broadcast([P, D])).then_inc(S("fg_in"), 16)
            norm(4)

        @block.vector
        def _(dve):
            v = nc.vector
            for name in ('yv_ready', 'q_ready', 'bu_used', 'he_ready', 'y_dve', 'mod1_evac', 'over_yg0', 'over_yg1'):
                dve.sem_inc(S(name), PRIMED[name])
            ch = Chain(dve, S("dve_order"))
            link = ch.link

            def gemv(r, j, use, done):
                dve.wait_ge(S(f"ada_in{j % ASLOTS}"), use)
                fold(r, aring[:, j % ASLOTS, :].rearrange("p (k c) -> p k c", c=HALF), done)

            def fold(r, w, done):
                u, kh = r // 2 % 3, r % 2
                if kh:
                    dve.wait_ge(S("gemv_done"), done)
                for kk in range(4):
                    k = kh * 4 + kk
                    if k == 0:
                        ins = v.tensor_scalar(acc[:, u, :], w[:, kk, :], condc[:, k:k + 1], None, ALU.mult)
                    else:
                        ins = v.scalar_tensor_tensor(acc[:, u, :], w[:, kk, :], condc[:, k:k + 1], acc[:, u, :],
                                                     ALU.mult, ALU.add)
                    if kk < 3:
                        link(ins)
                    else:
                        ins.then_inc(S("gemv_done"), 1)

            def gemv0(lo, hi):
                for r in range(lo, hi):
                    if r % 2 == 0 and r // 2 >= 3:
                        dve.wait_ge(S("mod_ps"), r // 2 - 2)
                    if r // 2 in RING_ADA:
                        slot, turn = RING_ADA[r // 2]
                        dve.wait_ge(S(f"ada_ring{slot}"), 16 * (turn + 1))
                        fold(r, u3(slot)[:, 4 * (r % 2):4 * (r % 2) + 4, :], r)
                    else:
                        j = A_HALF0.index(r)
                        gemv(r, j, 16 * (j // ASLOTS + 1), r)

            def reduce_angle(src, turns, lo, hi):
                link(v.tensor_scalar(turns, src, 1.0 / (2 * PI), MAGIC, ALU.mult, ALU.add))
                link(v.tensor_scalar(turns, turns, -MAGIC, None, ALU.add))
                link(v.scalar_tensor_tensor(hi, turns, -TWO_PI[0], src, ALU.mult, ALU.add))
                link(v.scalar_tensor_tensor(hi, turns, -TWO_PI[1], hi, ALU.mult, ALU.add))
                link(v.scalar_tensor_tensor(hi, turns, -TWO_PI[2], hi, ALU.mult, ALU.add))
                link(v.tensor_scalar(hi, hi, 3.1415925, -3.1415925, ALU.min, ALU.max))
                link(v.scalar_tensor_tensor(lo, hi, -1.0, hi, ALU.mult, ALU.max))

            dve.wait_ge(S("cond_ready"), 1)
            gemv0(0, 6)
            def norm(n):
                if n == 0:
                    dve.wait_ge(S("x_in"), 16)
                link(v.tensor_tensor_reduce(out=xhat[:, 1, :], in0=x[:, 1, :], in1=x[:, 1, :], scale=1.0, scalar=0.0,
                                            op0=ALU.mult, op1=ALU.add, accum_out=stat[:, 1:2]))
                dve.wait_ge(S("ss_act"), n + 1)
                v.tensor_scalar(stat[:, 2:4], stat[:, 0:2], 1.0 / D, EPS, ALU.mult, ALU.add).then_inc(S("var_ready"), 1)
                dve.wait_ge(S("std_ready"), n + 1)
                link(v.reciprocal(stat[:, 6:8], stat[:, 4:6]))
                for b in range(NB):
                    last = v.tensor_scalar(xhat[:, b, :], x[:, b, :], stat[:, 6 + b:7 + b], None, ALU.mult)
                    if n < 4:
                        last.then_inc(S("xhat_ready"), 1)
                    else:
                        link(last)

            norm(0)
            gemv0(6, 8)
            dve.wait_ge(S("cols_ready"), 1)

            def mod_evac(lo, hi):
                dve.wait_ge(S("mod_ps"), hi)
                v.tensor_tensor(mod[:, 0].rearrange("p s k -> p (s k)")[:, 4 * lo:4 * hi],
                                bank[7][:, 4 * lo:4 * hi], adab[:, 0, 4 * lo:4 * hi], ALU.add).then_inc(
                                    S("mod_cols"), 1)
                dve.wait_ge(S("mod_cols"), 1 if lo == 0 else 2)

            def mod_scale(n, done=True):
                L, sec = n // 2, (SC_M if n % 2 == 0 else SC_F)
                at = ROWS[("mix0", "ffn0", "mix1", "ffn1")[n]][0]
                v.scalar_tensor_tensor(modA[:, n, :], mod[:, L, sec, :], 1.0, cols[:, at:at + KD],
                                       ALU.add, ALU.mult).then_inc(S("modA_ready"), 1)
                dve.wait_ge(S("modA_ready"), n + 1)

            def modulate(n):
                L, sec = n // 2, (SH_M if n % 2 == 0 else SH_F)
                for k in (2, 3, 6, 7):
                    dve.wait_ge(S("xT_ps"), 4 * n + k // 2 + 1)
                    v.tensor_scalar(hT[:, k, :], bank[k // 2][:, (k % 2) * T:(k % 2 + 1) * T], modA[:, n, k:k + 1],
                                    mod[:, L, sec, k:k + 1], ALU.mult, ALU.add).then_inc(S("hT_dve"), 1)

            mod_evac(0, 4)
            mod_scale(0)
            modulate(0)
            dve.wait_ge(S("pos_in"), 16)
            pos = rope[:, 0, 0:NB]
            link(v.tensor_copy(pos, rti[:, 0:NB]))
            ang = rope[:, 1, :].rearrange("p (b i) -> p b i", b=NB)
            for i in range(RH):
                last = v.tensor_scalar(ang[:, :, i], pos, float(ROPE_THETA ** (-2.0 * i / ROT)), None, ALU.mult)
            link(last)

            reduce_angle(rope[:, 1, :], rope[:, 6, :], rope[:, 2, :], rope[:, 3, :])
            v.tensor_scalar(rope[:, 2, :], rope[:, 2, :], -1.0, PI / 2, ALU.mult, ALU.add).then_inc(S("rope_arg"), 1)

            at, n = ROWS["lam"]
            lam = cols[:, at:at + n]
            link(v.scalar_tensor_tensor(sp[:, 2, :], lam, -1.0, lam, ALU.mult, ALU.max))
            v.tensor_scalar(sp[:, 0, :], sp[:, 2, :], -1.0, None, ALU.mult).then_inc(S("sp_arg"), 1)
            link(v.tensor_scalar(sp[:, 3, :], lam, -1.0, 0.0, ALU.mult, ALU.max))
            dve.wait_ge(S("sp_ln"), 1)
            link(v.tensor_tensor(sp[:, 1, :], sp[:, 1, :], sp[:, 3, :], ALU.add))
            v.tensor_scalar(sp[:, 2, :], sp[:, 1, :], 8.0, None, ALU.mult)
            v.tensor_scalar(sp[:, 3, :], sp[:, 1, :], -8.0, None, ALU.mult).then_inc(S("sp_ready"), 1)
            gemv0(8, 14)
            dve.wait_ge(S("kv_ps"), 1)
            link(v.tensor_copy(qkv[:, :, HALF:768], bank[6].rearrange("p (b n) -> p b n", b=NB)))
            dve.wait_ge(S("q_evac"), 2)
            dve.wait_ge(S("rope_ready"), 1)
            for b in range(NB):
                hd = qkv[:, b, 0:640].rearrange("p (h n) -> p h n", n=HEAD)
                x1, x2 = hd[:, :, 0:RH], hd[:, :, RH:ROT]
                cc = rope[:, 4, b * RH:(b + 1) * RH].unsqueeze(1).to_broadcast([P, 10, RH])
                ss = rope[:, 5, b * RH:(b + 1) * RH].unsqueeze(1).to_broadcast([P, 10, RH])
                t = [rq[:, m, :].rearrange("p (h n) -> p h n", n=RH) for m in range(4)]
                v.tensor_tensor(t[0], x1, cc, ALU.mult)
                v.tensor_tensor(t[1], x2, ss, ALU.mult)
                v.tensor_tensor(t[2], x2, cc, ALU.mult)
                link(v.tensor_tensor(t[3], x1, ss, ALU.mult))
                v.tensor_tensor(x1, t[0], t[1], ALU.subtract)
                link(v.tensor_tensor(x2, t[2], t[3], ALU.add))
                kh = qkv[:, b, NQ * HEAD:640].rearrange("p (g n) -> p g n", g=NKV)
                v.tensor_copy(k2[:, b, :].rearrange("p (g u n) -> p g u n", g=NKV, u=2),
                              kh.unsqueeze(2).to_broadcast([P, NKV, 2, HEAD])).then_inc(S("rope_done"), 1)
                dve.wait_ge(S("rope_done"), b + 1)
            gemv0(14, 18)
            dve.wait_ge(S("kT_ps"), 1)
            v.tensor_copy(kT[:, :, :], bank[6].rearrange("p (g t) -> p g t", g=NKV)).then_inc(S("kT_ready"), 1)
            dve.wait_ge(S("small_in"), 16 * 9)
            sk = smx[:, 4, 0:NQ]
            link(v.tensor_scalar(sk.rearrange("p (r i) -> p r i", r=2), sink[:, :].rearrange("p (i r) -> p r i", r=2),
                                 1.0 / SCALE, None, ALU.mult))
            for b in range(NB):
                pp = P0 if b == 0 else P1
                n_k = P * (b + 1)
                dve.wait_ge(S("s_ps"), b + 1)
                if b == 0:
                    sc = [PS[:, r, :].rearrange("p (i n) -> p i n", n=P) for r in range(2)]
                    rng = [(0, 64, 0, 64), (64, P, 0, P)]
                    zero = [(0, 64, 64, P)]
                else:
                    sc = [PS[:, w:w + 2, :].rearrange("p b (i n) -> p (b i) n", n=T) for w in (4, 2)]
                    rng = [(0, 64, 64, 192), (64, P, P, T)]
                    zero = [(0, 64, 0, 64), (0, 64, 192, T), (64, P, 0, P)]
                for lo, hi, k0, k1 in zero:
                    v.memset(pp[lo:hi, :, k0:k1], 0.0)
                mx = smx[:, 0, b * NQ:(b + 1) * NQ]
                for lo, hi, k0, k1 in rng:
                    for r in range(2):
                        last = v.tensor_reduce(smx[lo:hi, 0, b * NQ + 4 * r:b * NQ + 4 * r + 4], sc[r][lo:hi, :, k0:k1],
                                               AX.X, ALU.max)
                link(last)
                link(v.tensor_tensor(mx, mx, sk, ALU.max))
                v.tensor_tensor(smx[:, 1, b * NQ:(b + 1) * NQ], sk, mx, ALU.subtract)
                for lo, hi, k0, k1 in rng:
                    for r in range(2):
                        m = smx[lo:hi, 0, b * NQ + 4 * r:b * NQ + 4 * r + 4].unsqueeze(2).to_broadcast(
                            [64, 4, k1 - k0])
                        last = v.tensor_tensor(pp[lo:hi, 4 * r:4 * r + 4, k0:k1], sc[r][lo:hi, :, k0:k1], m,
                                               ALU.subtract)
                last.then_inc(S("s_less_m"), 1)
            dve.wait_ge(S("xr_ready"), 1)
            for j in range(LT):
                link(v.tensor_scalar(xc[:, j, :], xr[:, j, :], col("conv_w", 3 * LT + j), col("conv_b", j),
                                     ALU.mult, ALU.add))
            for s_ in range(1, CONV):
                for j in range(LT):
                    last = v.scalar_tensor_tensor(xc[:, j, s_:], xr[:, j, 0:T - s_], col("conv_w", (3 - s_) * LT + j),
                                                  xc[:, j, s_:], ALU.mult, ALU.add)
                    if s_ < CONV - 1:
                        if j == LT - 1:
                            link(last)
            last.then_inc(S("xc_ready"), 1)
            for b in range(NB):
                pp = P0 if b == 0 else P1
                n_k = P * (b + 1)
                dve.wait_ge(S("p_exp"), b + 1)
                den = smx[:, 3, b * NQ:(b + 1) * NQ]
                link(v.tensor_reduce(den, pp[:, :, 0:n_k], AX.X, ALU.add))
                link(v.tensor_tensor(den, den, smx[:, 2, b * NQ:(b + 1) * NQ], ALU.add))
                link(v.reciprocal(den, den))
                v.tensor_tensor(pp[:, :, 0:n_k], pp[:, :, 0:n_k], den.unsqueeze(2).to_broadcast([P, NQ, n_k]),
                                ALU.mult).then_inc(S("p_ready"), 1)
            gemv0(18, 24)
            mod_evac(4, 12)
            mod_scale(1)
            dve.wait_ge(S("lru_a"), 1)
            link(v.tensor_tensor(lr_i, lr_i, xc[:, :, :], ALU.mult))
            link(v.tensor_tensor(lr_r, lr_u, lr_u, ALU.mult))
            v.scalar_tensor_tensor(lr_t.rearrange("p k t -> p (k t)"), lr_r.rearrange("p k t -> p (k t)"), 1.0,
                                   lr_t.rearrange("p k t -> p (k t)"), ALU.add, ALU.mult).then_inc(S("lru_b2"), 1)
            dve.wait_ge(S("lru_sq"), 1)
            link(v.tensor_tensor(lr_i, lr_i, lr_t, ALU.mult))
            for j in range(LT):
                last = v.tensor_tensor_scan(lr_r[:, j, :], lr_u[:, j, :], lr_i[:, j, :], 0.0, ALU.mult, ALU.add)
            link(last)
            v.tensor_tensor(mixT[:, 4:8, :], lr_r, gate[:, :, :], ALU.mult).then_inc(S("lru_ready"), 1)

            def residual(n, waits, psum):
                dve.wait_ge(S("grow_ready"), n + 1)
                tmp = acc
                for b in range(NB):
                    for h in range(2):
                        dve.wait_ge(S(waits), (2 * b + h + 1) + 4 * (n // 2))
                        gr = grow[:, h * HALF:(h + 1) * HALF]
                        link(v.tensor_tensor(tmp[:, h, :], psum(b, h), gr, ALU.mult))
                        last = v.tensor_tensor(x[:, b, h * HALF:(h + 1) * HALF], x[:, b, h * HALF:(h + 1) * HALF],
                                               tmp[:, h, :], ALU.add)
                return last

            R = s5r
            q = slice(0, NQT)
            dve.wait_ge(S("s5_act"), 1)
            dtb = R[q, 4, 0:2].unsqueeze(2).to_broadcast([NQT, 2, STATE])
            h2 = lambda r: R[q, r, :].rearrange("q (g p) -> q g p", g=2)
            link(v.tensor_copy(R[q, 0:2, :], s5i[q, 0:2, :]))
            link(v.tensor_tensor(h2(5), h2(0), dtb, ALU.mult))
            link(v.tensor_tensor(h2(6), h2(1), dtb, ALU.mult))
            reduce_angle(R[q, 6, :], R[q, 12, :], R[q, 10, :], R[q, 11, :])
            v.tensor_scalar(R[q, 10, :], R[q, 10, :], -1.0, PI / 2, ALU.mult, ALU.add).then_inc(S("s5_th"), 1)
            dve.wait_ge(S("s5_act"), 2)
            tt = lambda d, s1, s2, op: link(v.tensor_tensor(R[q, d, :], R[q, s1, :], R[q, s2, :], op))
            tt(12, 7, 8, ALU.mult)
            tt(13, 7, 9, ALU.mult)
            link(v.tensor_scalar(R[q, 12, :], R[q, 12, :], -1.0, None, ALU.add))
            tt(14, 0, 0, ALU.mult)
            tt(15, 1, 1, ALU.mult)
            tt(14, 14, 15, ALU.add)
            link(v.reciprocal(R[q, 14, :], R[q, 14, :]))
            tt(15, 12, 0, ALU.mult)
            tt(16, 13, 1, ALU.mult)
            tt(15, 15, 16, ALU.add)
            tt(16, 13, 0, ALU.mult)
            tt(17, 12, 1, ALU.mult)
            tt(16, 16, 17, ALU.subtract)
            tt(10, 15, 14, ALU.mult)
            v.tensor_tensor(R[q, 11, :], R[q, 16, :], R[q, 14, :], ALU.mult).then_inc(S("s5_rows"), 1)
            dve.wait_ge(S("s5_cols_ps"), 1)
            link(v.tensor_copy(s5c[:, :, :], bank[6][:, 0:5 * NQT].rearrange("p (r q) -> p r q", r=5)))
            cb = lambda r: s5c[:, r, :].unsqueeze(2).to_broadcast([P, NQT, CH])
            dve.wait_ge(S("tables_zero"), 2)
            for w, (s1, s2, op) in enumerate(((0, 1, ALU.subtract), (1, 0, ALU.add))):
                link(v.tensor_tensor(bt1[:, :, :], Bl[:, s1, :, :], cb(3), ALU.mult))
                link(v.tensor_tensor(bt2[:, :, :], Bl[:, s2, :, :], cb(4), ALU.mult))
                for u in range(2):
                    pr_ = slice(u * 64, u * 64 + 64)
                    dst = Bp[pr_, w].rearrange("p k (q g c) -> p (k q) g c", g=2, c=CH)[:, :, u, :]
                    v.tensor_tensor(dst, bt1[pr_, :, :], bt2[pr_, :, :], op).then_inc(S("bp_ready"), 1)
                dve.wait_ge(S("bp_ready"), 2 * w + 2)
            residual(0, "m_ps", lambda b, h: bank[2 * b + h]).then_inc(S("x_new"), 1)
            dve.wait_ge(S("x_new"), 1)

            def ffn(L):
                n = 2 * L + 1
                norm(n)
                modulate(n)
                lg = rt[:, 0:40].rearrange("p (b n) -> p b n", b=NB)
                dve.wait_ge(S("router_ps"), L + 1)
                psl = bank[4][:, 0:40].rearrange("p (b n) -> p b n", b=NB)
                link(v.tensor_tensor(lg, psl, rb[:, L:L + 1, :].to_broadcast([P, NB, 20]), ALU.add))
                lg4 = lg[:, :, 0:NG]
                r2 = lambda o: rt[:, o:o + NB]
                r8 = lambda o: rt[:, o:o + 8].rearrange("p (b g) -> p b g", b=NB)
                bc = lambda ap: ap.unsqueeze(2).to_broadcast([P, NB, 4])
                prio = r8(300)
                for g_ in range(4):
                    last = v.memset(prio[:, :, g_], float(4 - g_))
                link(last)

                def first_max(val, mx, oh, key):
                    link(v.tensor_reduce(mx, val, AX.X, ALU.max))
                    link(v.tensor_tensor(oh, val, bc(mx), ALU.is_equal))
                    link(v.tensor_tensor(oh, oh, prio, ALU.mult))
                    link(v.tensor_reduce(key, oh, AX.X, ALU.max))
                    link(v.tensor_tensor(oh, oh, bc(key), ALU.is_equal))

                oh = r8(48)
                first_max(lg4, r2(40), oh, r2(42))
                v.tensor_tensor(r8(56), lg4, bc(r2(40)), ALU.subtract).then_inc(S("lg_ready"), 1)
                le = lg[:, :, NG:].rearrange("p b (g e) -> p b g e", g=NG)
                sel = rt[:, 96:128].rearrange("p (b g e) -> p b g e", b=NB, g=NG)
                link(v.tensor_tensor(sel, le, oh.unsqueeze(3).to_broadcast([P, NB, NG, EPG]), ALU.mult))
                les = r8(128)
                link(v.tensor_reduce(les, sel.rearrange("p b g e -> p b e g"), AX.X, ALU.add))
                oh1, oh2 = r8(136), r8(144)
                first_max(les, r2(80), oh1, r2(42))
                link(v.scalar_tensor_tensor(rt[:, 152:160], rt[:, 136:144], -1e30, rt[:, 128:136], ALU.mult, ALU.add))
                first_max(r8(152), r2(82), oh2, r2(42))
                v.tensor_tensor(r2(84), r2(82), r2(80), ALU.subtract).then_inc(S("l2_ready"), 1)
                dve.wait_ge(S("exp_ready"), 2 * L + 1)
                link(v.tensor_reduce(r2(88), r8(64), AX.X, ALU.add))
                dve.wait_ge(S("exp_ready"), 2 * L + 2)
                link(v.tensor_scalar(r2(90), r2(86), 1.0, None, ALU.add))
                link(v.tensor_tensor(r2(88), r2(88), r2(90), ALU.mult))
                link(v.reciprocal(r2(88), r2(88)))
                link(v.tensor_tensor(r2(90), r2(88), r2(86), ALU.mult))
                gt = r8(160)
                link(v.tensor_tensor(gt, oh1, bc(r2(88)), ALU.mult))
                link(v.tensor_tensor(oh2, oh2, bc(r2(90)), ALU.mult))
                v.tensor_tensor(gt, gt, oh2, ALU.add).then_inc(S("gates_ready"), 1)
                dve.wait_ge(S("gates_ready"), L + 1)
                dve.wait_ge(S("rank_ps"), L + 1)
                rk = r2(168)
                nar = rt[:, 212:217]
                v.tensor_scalar(nar[:, 0:NG], bank[5][:, 8:12], 64.5, None, ALU.is_lt)
                link(v.tensor_reduce(rt[:, 218:219], bank[5][:, 8:12], AX.X, ALU.max))
                link(v.tensor_scalar(nar[:, NG:], rt[:, 218:219], P + 64.5, None, ALU.is_lt))
                v.tensor_copy(rti[:, 2:2 + NG], nar[:, 0:NG])
                for w in range(2):
                    v.tensor_scalar(gsl[:, :, EPG + w], nar, half_of[:, w:w + 1], 1.0, ALU.mult, ALU.add)
                link(v.tensor_scalar(rt[:, 220:225], nar, -1.0, None, ALU.mult))
                for g_ in range(NG + 1):
                    last = v.scalar_tensor_tensor(slotv[g_], slot_hi[:, :], rt[:, 220 + g_:221 + g_], slot_no[:, :],
                                                  ALU.mult, ALU.add)
                link(last)
                link(v.tensor_tensor(r8(176), oh, bank[5][:, 0:8].rearrange("p (b g) -> p b g", b=NB), ALU.mult))
                link(v.tensor_reduce(rk, r8(176), AX.X, ALU.add))
                for b in range(NB):
                    for g_ in range(NG):
                        v.tensor_scalar(pick[:, b, g_, :], slotv[g_], rt[:, 168 + b:169 + b], oh[:, b, g_:g_ + 1],
                                        ALU.is_equal, ALU.mult)
                link(v.tensor_scalar(r2(170), rk, -float(P), None, ALU.add))
                for b in range(NB):
                    last = v.tensor_scalar(pick[:, b, NG, :], slotv[NG], rt[:, 170 + b:171 + b], None, ALU.is_equal)
                last.then_inc(S("pick_ready"), 1)
                ov = rt[:, 192:196].rearrange("p (b n) -> p b n", b=NB)
                link(v.tensor_scalar(ov[:, :, 0], rk, float(P), None, ALU.is_ge))
                link(v.tensor_scalar(ov[:, :, 1], rk, float(P), None, ALU.is_equal))
                for g_ in range(NG):
                    last = v.tensor_scalar(r8(200)[:, :, g_], oh[:, :, g_], float(g_), None, ALU.mult)
                link(last)
                link(v.tensor_reduce(r2(208), r8(200), AX.X, ALU.add))
                v.tensor_tensor(ov[:, :, 1], ov[:, :, 1], r2(208), ALU.mult).then_inc(S("ov_ready"), 1)
                dve.wait_ge(S("gsl_ps"), L + 1)
                link(v.tensor_copy(gsl[:, :, 0:EPG], bank[5][:, 16:16 + 20].rearrange("p (g e) -> p g e", e=EPG)))
                v.tensor_copy(rti[:, 0:2], bank[5][:, 40:42]).then_inc(S("over_known"), 1)
                dve.wait_ge(S("over_known"), L + 1)

                def hg_evac(i):
                    dve.wait_ge(S("gathered"), 10 * L + 2 + 2 * i)
                    for k in range(4, KD):
                        last = v.tensor_scalar(hg[:, k, :], bank[2][:, (k - 4) * P:(k - 3) * P],
                                               modA[:, n, k:k + 1], mod[:, L, SH_F, k:k + 1], ALU.mult, ALU.add)
                    last.then_inc(S("hg_dve"), 1)

                hg_evac(0)
                n0 = MOE_BASE[L]
                per = 1 + (6 if L == 0 else 0)
                with dve.Fori(0, NG) as i:
                    ch.enter(i, per)
                    dve.wait_ge(S("y_act"), 1 + NG * L + i)
                    dve.wait_ge(S("y_dve"), 1 + NG * L + i)
                    link(v.tensor_copy(gcur[:, :], gsl[:, bass.ds(i, 1), :].rearrange("p a e -> p (a e)")))
                    j = 0
                    for e in range(EPG):
                        dve.wait_ge(S("sil_ready"), 1 + 16 * L + 4 * i + e + 1)
                        dve.wait_ge(S("b_ps"), 16 * L + 4 * i + e + 1)
                        if e or L:
                            dve.wait_ge(S("heT_ps"), 16 * L + 4 * i + e)
                        v.scalar_tensor_tensor(he[:, :], sil[:, :], gcur[:, e:e + 1], bank[2 + e % 2],
                                               ALU.mult, ALU.mult).then_inc(S("he_ready"), 1)
                        if L == 0 and e < 2:
                            if e == 0:
                                dve.wait_ge(S("mod_ps"), A_UNITS + i)
                            gemv(e, e, 16 + 16 * len(A_HALF0) // ASLOTS + i * 16, A_HALVES + e + 2 * i)
                    hg_evac(i + 1)
                    dve.wait_ge(S("y_ps"), 16 * L + 4 * i + 4)
                    v.tensor_scalar(yg[:, bass.ds(i, 1), HALF:], bank[5].unsqueeze(1), gcur[:, EPG + 1:EPG + 2], None,
                                    ALU.mult).then_inc(S("y_dve"), 1)
                    if L == 0:
                        dve.wait_ge(S("mod_ps"), A_UNITS + 1 + i)
                        v.tensor_copy(mod[:, 1].rearrange("p s k -> p (s k)")[:, bass.ds(i * 4, 4)],
                                      bank[7][:, 64:68]).then_inc(S("mod1_evac"), 1)
                ch.leave(NG)
                if L == 0:
                    dve.wait_ge(S("mod1_evac"), 1 + NG)
                    m1 = mod[:, 1].rearrange("p s k -> p (s k)")
                    v.tensor_tensor(m1[:, 0:4 * A_MOE], m1[:, 0:4 * A_MOE], adab[:, 1, 0:4 * A_MOE],
                                    ALU.add).then_inc(S("mod_cols"), 1)
                    dve.wait_ge(S("mod_cols"), 3)
                    mod_scale(2)
                dve.wait_ge(S("pickT_ps"), L + 1)
                v.tensor_copy(pickT[:, :, :], PS[:, 0:2, :].rearrange("p c (g t) -> p (c g) t", t=T)).then_inc(
                    S("pickT_ready"), 1)
                dve.wait_ge(S("grow_ready"), n + 1)
                tmp = w3(W0 + NB * (NG + 1) * P, 2, HALF)
                for b in range(NB):
                    for h in range(2):
                        dve.wait_ge(S("sc_ps"), 4 * L + 2 * b + h + 1)
                        link(v.tensor_tensor(tmp[:, h, :], bank[(0, 1, 2, 3)[2 * b + h]], grow[:, h * HALF:(h + 1) * HALF],
                                             ALU.mult))
                        last = v.tensor_tensor(x[:, b, h * HALF:(h + 1) * HALF], x[:, b, h * HALF:(h + 1) * HALF],
                                               tmp[:, h, :], ALU.add)
                last.then_inc(S("x_main"), 1)
                dve.wait_ge(S("x_main"), L + 1)
                n_over = dve.value_load(rti[0:1, 0:1], min_val=0, max_val=T)
                with dve.If(n_over > 0):
                    oc = Chain(dve, S(f"over_order{L}"))
                    oc.link(v.memset(yg[:, 0, :], 0.0))
                    with dve.Fori(0, EPG) as e:
                        oc.enter(e, 1)
                        dve.wait_ge(S(f"over_sil{L}"), e + 1)
                        oc.link(v.tensor_copy(gcur[:, 0:1], gsl[:, NG, bass.ds(e, 1)]))
                        v.scalar_tensor_tensor(he[:, :], sil[:, :], gcur[:, 0:1], bank[2], ALU.mult,
                                               ALU.mult).then_inc(S(f"over_he{L}"), 1)
                        dve.wait_ge(S(f"over_used{L}"), e * 3 + SLOTS + 3)
                        for h in range(2):
                            last = v.scalar_tensor_tensor(yg[:, 0, h * HALF:(h + 1) * HALF], bank[4 + h],
                                                          gsl[:, NG, EPG + h:EPG + h + 1],
                                                          yg[:, 0, h * HALF:(h + 1) * HALF], ALU.mult, ALU.add)
                        last.then_inc(S(f"over_yg{L}"), 1)
                        dve.wait_ge(S(f"over_yg{L}"), 1 + e + 1)
                    oc.leave(EPG)
                    dve.wait_ge(S(f"over_heT{L}"), EPG + 1)
                    v.tensor_copy(pickT[:, 0, :], bank[6][:, 0:T]).then_inc(S(f"over_he{L}"), 1)
                    dve.wait_ge(S(f"over_heT{L}"), EPG + 2)
                    for b in range(NB):
                        for h in range(2):
                            oc.link(v.tensor_tensor(tmp[:, h, :], bank[2 * b + h], grow[:, h * HALF:(h + 1) * HALF],
                                                    ALU.mult))
                            oc.link(v.tensor_tensor(x[:, b, h * HALF:(h + 1) * HALF],
                                                    x[:, b, h * HALF:(h + 1) * HALF], tmp[:, h, :], ALU.add))
                nc.vector.drain().then_inc(S("x_new"), 1)
                dve.wait_ge(S("x_new"), 2 * L + 2)

            ffn(0)

            norm(2)
            modulate(2)
            f2 = lambda ap: ap.rearrange("p (q t) -> p q t", q=2)
            per = 4 * 2

            def output(kk, m):
                dve.wait_ge(S("q_used"), 2 + 4 * kk + 2 * m + 2)
                dve.wait_ge(S("act_ready"), 1 + 2 * kk + m)
                v.scalar_tensor_tensor(yv[:, :], ucur[:, m, :], dcur[:, m:m + 1], bank[4][:, 0:T], ALU.mult,
                                       ALU.add).then_inc(S("yv_ready"), 1)

            with dve.Fori(0, KD // 2) as kk:
                ch.enter(kk, per)
                for m, j in ((0, 0), (0, 1), (1, 0), (1, 1)):
                    n = 4 * kk + 2 * m + j
                    bre = PS[:, 2 * j:2 * j + 2, 0:T]
                    bim = PS[:, 2 * j:2 * j + 2, T:2 * T]
                    c_, s_ = f2(cs[:, j, 0, :]), f2(cs[:, j, 1, :])
                    dve.wait_ge(S("bu_ready"), 1 + 2 * n + 2)
                    dve.wait_ge(S("tab_ready"), n + 1)
                    v.tensor_tensor(f2(pr[:, 0, :]), bre, c_, ALU.mult)
                    v.tensor_tensor(f2(pr[:, 1, :]), bim, s_, ALU.mult)
                    v.tensor_tensor(f2(pr[:, 2, :]), bim, c_, ALU.mult)
                    v.tensor_tensor(f2(pr[:, 3, :]), bre, s_, ALU.mult).then_inc(S("bu_used"), 1)
                    dve.wait_ge(S("bu_used"), 1 + n + 1)
                    v.tensor_tensor(pr[:, 0, :], pr[:, 0, :], pr[:, 1, :], ALU.add)
                    link(v.tensor_tensor(pr[:, 2, :], pr[:, 2, :], pr[:, 3, :], ALU.subtract))
                    for q_ in range(2):
                        r_ = s5c[:, 0, bass.ds(2 * n + q_, 1)].to_broadcast([P, T])
                        for w in range(2):
                            last = v.tensor_tensor_scan(gg[:, w, q_ * T:(q_ + 1) * T], r_,
                                                        pr[:, 2 * w, q_ * T:(q_ + 1) * T], 0.0, ALU.mult, ALU.add)
                    link(last)
                    if (m, j) == (1, 0):
                        output(kk, 0)
                    dve.wait_ge(S("q_used"), 2 + n - 1)
                    v.tensor_tensor(qq[j][:, 0, :], gg[:, 0, :], cs[:, j, 0, :], ALU.mult)
                    v.scalar_tensor_tensor(qq[j][:, 1, :], gg[:, 1, :], -1.0, cs[:, j, 1, :], ALU.mult, ALU.mult)
                    v.tensor_tensor(qq[j][:, 2, :], gg[:, 0, :], cs[:, j, 1, :], ALU.mult)
                    v.tensor_tensor(qq[j][:, 3, :], gg[:, 1, :], cs[:, j, 0, :], ALU.mult).then_inc(S("q_ready"), 1)
                    if (m, j) == (1, 1):
                        output(kk, 1)
            ch.leave(KD // 2)
            dve.wait_ge(S("ada_act"), 2 * KD)
            m1 = mod[:, 1].rearrange("p s k -> p (s k)")
            v.tensor_tensor(m1[:, 4 * A_MOE:], m1[:, 4 * A_MOE:], adab[:, 1, 4 * A_MOE:], ALU.add).then_inc(
                S("mod_cols"), 1)
            dve.wait_ge(S("mod_cols"), 4)
            mod_scale(3)
            dve.wait_ge(S("grow_ready"), 3)
            for h in range(2):
                for b in range(NB):
                    dve.wait_ge(S("glu_sig"), 2 * h + b + 1)
                    link(v.tensor_tensor(q_a[:, 2 * h + b, :], q_a[:, 2 * h + b, :], bank[4 * h + b], ALU.mult))
                    link(v.tensor_tensor(q_a[:, 2 * h + b, :], q_a[:, 2 * h + b, :], grow[:, h * HALF:(h + 1) * HALF],
                                         ALU.mult))
                    last = v.tensor_tensor(x[:, b, h * HALF:(h + 1) * HALF], x[:, b, h * HALF:(h + 1) * HALF],
                                           q_a[:, 2 * h + b, :], ALU.add)
            last.then_inc(S("x_new"), 1)
            dve.wait_ge(S("x_new"), 3)
            ffn(1)
            norm(4)
            dve.wait_ge(S("fg_in"), 16)
            for b in range(NB):
                v.tensor_tensor(xhat[:, b, :], xhat[:, b, :], fing, ALU.mult).then_inc(S("out_ready"), 1)

        @block.tensor
        def _(pe):
            mm = nc.tensor.matmul
            for name in ('bu_ready', 'q_used'):
                pe.sem_inc(S(name), PRIMED[name])

            def tr(dst, src, n=P):
                return nc.tensor.transpose(dst, src, ident[0:n, 0:n])

            def bcol(ap, n=P):
                return ap.to_broadcast([ap.shape[0], n])

            pe.wait_ge(S("c_in"), 16)
            pe.wait_ge(S("ident_ready"), 1)
            tr(bank[2][:, 0:KD], crow, KD).then_inc(S("c_ps"), 1)
            pe.wait_ge(S("rows_in"), 16 * (len(ROWS) + 2))
            tr(bank[0][:, 0:N_ROWS], rows, N_ROWS)
            tr(bank[1][:, 0:6 * KD], brow[:, 0, :], 6 * KD)
            tr(bank[1][:, 6 * KD:12 * KD], brow[:, 1, :], 6 * KD).then_inc(S("cols_ps"), 1)
            pe.wait_ge(S("consts_ready"), 2)
            pe.wait_ge(S("pool_order"), 3)

            def mod_cols(u, at):
                for c4 in range(4):
                    last = mm(bank[7][:, at + c4:at + c4 + 1], acc[:, u % 3, c4 * P:(c4 + 1) * P], ones[:, 0:1],
                              start=True, stop=True)
                last.then_inc(S("mod_ps"), 1)

            def mod0(lo, hi):
                if lo:
                    pe.wait_ge(S("mod_cols"), 1)
                for u in range(lo, hi):
                    pe.wait_ge(S("gemv_done"), 2 * u + 2)
                    mod_cols(u, 4 * u)

            def turn_x(n):
                pe.wait_ge(S("xhat_ready"), 2 * n + 2)
                for c in range(4):
                    for kk in range(2):
                        for b in range(NB):
                            last = tr(bank[c][:, kk * T + b * P:kk * T + (b + 1) * P],
                                      xhat[:, b, (2 * c + kk) * P:(2 * c + kk + 1) * P])
                    last.then_inc(S("xT_ps"), 1)

            def hT_ready(n):
                pe.wait_ge(S("hT_act"), 4 * n + 4)
                pe.wait_ge(S("hT_dve"), 4 * n + 4)

            def gate_row(n):
                L, sec = n // 2, (G_M if n % 2 == 0 else G_F)
                pe.wait_ge(S("mod_cols"), (2, 2, 4, 4)[n])
                for k in range(KD):
                    last = mm(bank[4 + k // 4][:, (k % 4) * P:(k % 4 + 1) * P], bcol(mod[:, L, sec, k:k + 1]),
                              ident[:, :], start=True, stop=True)
                last.then_inc(S("grow_ps"), 1)

            pe.wait_ge(S("cols_ready"), 1)
            turn_x(0)
            mod0(0, 4)
            hT_ready(0)
            loaded(pe, 0)
            for b in range(NB):
                for k in range(KD):
                    last = mm(bank[4 + b], hT[:, k, b * P:(b + 1) * P], u3(0)[:, k, :], start=k == 0, stop=k == KD - 1)
                last.then_inc(S("q_ps"), 1)
            loaded(pe, 1)
            for b in range(NB):
                for k in range(KD):
                    last = mm(bank[6][:, b * 256:(b + 1) * 256], hT[:, k, b * P:(b + 1) * P], u3(1)[:, k, 0:256],
                              start=k == 0, stop=k == KD - 1)
            last.then_inc(S("kv_ps"), 1)

            def feature_tile(dst, w):
                for k in range(KD):
                    last = mm(dst, w[:, k, :], hT[:, k, :], start=k == 0, stop=k == KD - 1)
                return last

            for j in range(LT):
                at = 768 + j * P
                if j == 2:
                    mod0(4, 6)
                    loaded(pe, 2)
                w = u3(at // HALF)[:, :, at % HALF:at % HALF + P]
                last = feature_tile(bank[j // 2][:, (j % 2) * T:(j % 2 + 1) * T], w)
                if j % 2:
                    last.then_inc(S("xr_ps"), 1)
            for j in range(LT):
                at = 1280 + j * P
                if j < 2:
                    mod0(6 + j, 7 + j)
                if j == 2:
                    loaded(pe, 3)
                w = u3(at // HALF)[:, :, at % HALF:at % HALF + P]
                last = feature_tile(bank[2 + j // 2][:, (j % 2) * T:(j % 2 + 1) * T], w)
                if j % 2:
                    last.then_inc(S("gate_ps"), 1)
            for b in range(NB):
                pe.wait_ge(S("rope_done"), b + 1)
                for t in range(4):
                    last = tr(bank[4 + t // 2][:, (t % 2) * T + b * P:(t % 2) * T + (b + 1) * P],
                              qkv[:, b, t * P:(t + 1) * P])
                if b == NB - 1:
                    last.then_inc(S("qT_ps"), 1)
                for g in range(NKV):
                    last = tr(bank[6][:, g * T + b * P:g * T + (b + 1) * P], k2[:, b, g * P:(g + 1) * P])
                if b == NB - 1:
                    last.then_inc(S("kT_ps"), 1)
            pe.wait_ge(S("qT_ready"), 1)
            pe.wait_ge(S("kT_ready"), 1)
            pe.wait_ge(S("xr_ready"), 1)
            pe.wait_ge(S("gate_ready"), 1)
            for b in range(NB):
                n_k = P * (b + 1)
                for i in range(4):
                    for r in range(2):
                        h = 2 * i + r
                        if b == 0:
                            dst = PS[:, r, i * P:(i + 1) * P]
                        else:
                            dst = PS[:, (4, 2)[r] + i // 2, (i % 2) * T:(i % 2 + 1) * T]
                        pp = slice(64 * r, 64 * r + 64)
                        last = mm(dst, qT[pp, i, b * P:(b + 1) * P], kT[pp, h // 4, 0:n_k], start=True, stop=True)
                last.then_inc(S("s_ps"), 1)
            mod0(8, 9)
            f = 0
            pieces = [(0, [(hh, 0) for hh in range(0, 4)]), (0, [(hh, 0) for hh in range(4, 8)])]
            pieces += [(1, [(hh, kb) for hh in (2 * m, 2 * m + 1) for kb in range(2)]) for m in range(4)]

            def turn_p(f):
                b, part = pieces[f]
                pe.wait_ge(S("p_ready"), b + 1)
                pe.wait_ge(S("s_less_m"), b + 1)
                if f >= 2:
                    pe.wait_ge(S("pT_ready"), f - 1)
                pp = P0 if b == 0 else P1
                for m, (hh, kb) in enumerate(part):
                    last = tr(bank[6 if f % 2 == 0 else 0][:, m * P:(m + 1) * P], pp[:, hh, kb * P:(kb + 1) * P])
                last.then_inc(S("pT_ps"), 1)

            def weigh(f):
                b, part = pieces[f]
                pe.wait_ge(S("pT_ready"), f + 1)
                for m, (hh, kb) in enumerate(part):
                    r, i = hh // 4, hh % 4
                    h = 2 * i + r
                    at = (NQ + NKV) * HEAD + (h // 4) * HEAD
                    last = mm(bank[(1, 4)[b]][64 * r:64 * r + 64, i * P:(i + 1) * P], qkv[:, kb, at:at + HEAD],
                              PT[:, f % 2, m * P:(m + 1) * P], start=kb == 0, stop=kb == b)
                last.then_inc(S("pv_done"), 1)

            turn_p(0)
            for f in range(6):
                if f < 5:
                    turn_p(f + 1)
                weigh(f)
            pe.wait_ge(S("xc_ready"), 1)
            pe.wait_ge(S("gaw_in"), 64)
            for v_ in range(2):
                for j in range(LT):
                    last = mm(PS[:, (2, 5)[v_] + j // 2, (j % 2) * T:(j % 2 + 1) * T], gaw[:, v_, j, :], xc[:, j, :],
                              start=True, stop=True)
            last.then_inc(S("lru_ps"), 1)
            mod0(9, 12)
            pe.wait_ge(S("lru_ri"), 1)
            pe.wait_ge(S("attn_ready"), 1)
            gate_row(0)
            pe.wait_ge(S("lru_ready"), 1)
            for h in range(2):
                loaded(pe, N_WIN + h)
            pe.wait_ge(S("grow_ready"), 1)
            for b in range(NB):
                for h in range(2):
                    for k in range(KD):
                        last = mm(bank[2 * b + h], mixT[:, k, b * P:(b + 1) * P], u3(N_WIN + h)[:, k, :],
                                  start=k == 0, stop=k == KD - 1)
                    last.then_inc(S("m_ps"), 1)
                    if (b, h) == (0, 0):
                        pe.wait_ge(S("s5_rows"), 1)
                        for m, r in enumerate((7, 8, 9, 10, 11)):
                            last = tr(bank[6][:, m * NQT:(m + 1) * NQT], s5r[0:NQT, r, :], NQT)
                        last.then_inc(S("s5_cols_ps"), 1)
                    if (b, h) == (0, 1):
                        pe.wait_ge(S("bp_ready"), 4)
                        for v_ in range(2):
                            for hf in range(2):
                                if v_:
                                    pe.wait_ge(S("bt_evac"), 1 + hf)
                                for kk in range(4):
                                    last = tr(bank[4 + hf][:, kk * P:(kk + 1) * P], Bp[:, v_, hf * 4 + kk, :])
                                last.then_inc(S("bt_ps"), 1)
            pe.wait_ge(S("cn_in"), 64)
            for v_ in range(2):
                for hf in range(2):
                    if v_ or hf:
                        pe.wait_ge(S("ct_evac"), 2 * (2 * v_ + hf))
                    for kk in range(4):
                        last = tr(bank[6][:, kk * P:(kk + 1) * P], Cn[:, v_, hf * 4 + kk, :])
                    last.then_inc(S("ct_ps"), 1)
            pe.wait_ge(S("bt_evac"), 4)
            pe.wait_ge(S("ct_evac"), 8)
            pe.wait_ge(S("x_new"), 1)

            def product_up(dst, w, narrow):
                for k in range(KD):
                    if narrow:
                        for u in range(2):
                            last = mm(dst[64 * u:64 * u + 64, 0:256], hg[:, k, 0:64], w[:, k, 256 * u:256 * u + 256],
                                      start=k == 0, stop=k == KD - 1)
                    else:
                        last = mm(dst, hg[:, k, :], w[:, k, :], start=k == 0, stop=k == KD - 1)
                return last

            def turn_he(narrow):
                for c4 in range(2 if narrow else 4):
                    last = tr(bank[6][:, c4 * P:(c4 + 1) * P], he[:, c4 * P:(c4 + 1) * P])
                return last

            def product_down(w, narrow, start, stop):
                steps = [(h, c4) for h in range(2) for c4 in range(KF)]
                if narrow:
                    steps = [(h, c4) for c4 in range(KF) for h in range(2)]
                for h, c4 in steps:
                    at = (c4 % 2) * P + (c4 // 2) * 64 if narrow else c4 * P
                    dst = bank[4 + h][64 * h:64 * h + 64, :] if narrow else bank[4 + h]
                    last = mm(dst, heT[:, at:at + (64 if narrow else P)], w[:, c4, h * HALF:(h + 1) * HALF],
                              start=start and c4 == 0, stop=stop and c4 == KF - 1)
                return last

            def ffn(L):
                n = 2 * L + 1
                n0 = MOE_BASE[L]
                turn_x(n)
                hT_ready(n)
                if L == 0:
                    pe.wait_ge(S("small_in"), 16 * 9)
                for b in range(NB):
                    for k in range(KD):
                        last = mm(bank[4][:, b * 20:b * 20 + 20], hT[:, k, b * P:(b + 1) * P], wr_sb[:, L, k, :],
                                  start=k == 0, stop=k == KD - 1)
                last.then_inc(S("router_ps"), 1)
                pe.wait_ge(S("l2_ready"), L + 1)
                oh = rt[:, 48:56].rearrange("p (b g) -> p b g", b=NB)
                mm(bank[5][:, 0:4], before[:, :], oh[:, 0, :], start=True, stop=True)
                mm(bank[5][:, 4:8], before[:, :], oh[:, 1, :], start=True, stop=False)
                mm(bank[5][:, 4:8], ones[:, :], oh[:, 0, :], start=False, stop=True)
                for b in range(NB):
                    last = mm(bank[5][:, 8:12], ones[:, :], oh[:, b, :], start=b == 0, stop=b == NB - 1)
                last.then_inc(S("rank_ps"), 1)
                pe.wait_ge(S("pick_ready"), L + 1)
                gt = rt[:, 160:168].rearrange("p (b g) -> p b g", b=NB)
                for g in range(NG + 1):
                    for b in range(NB):
                        last = mm(bank[5][:, 16 + 4 * g:20 + 4 * g], pick[:, b, g, :], gt[:, b, :], start=b == 0,
                                  stop=b == NB - 1)
                pe.wait_ge(S("ov_ready"), L + 1)
                ov = rt[:, 192:196].rearrange("p (b n) -> p b n", b=NB)
                for b in range(NB):
                    last = mm(bank[5][:, 40:42], ones[:, :], ov[:, b, :], start=b == 0, stop=b == NB - 1)
                last.then_inc(S("gsl_ps"), 1)

                def gather(i):
                    for k in range(KD):
                        for b in range(NB):
                            last = mm(bank[2 * (k // 4)][:, (k % 4) * P:(k % 4 + 1) * P],
                                      xhat[:, b, k * P:(k + 1) * P], pick[:, b, i, :], start=b == 0, stop=b == NB - 1)
                        if k in (3, 7):
                            last.then_inc(S("gathered"), 1)

                gather(0)
                with pe.Fori(0, NG) as i:
                    e0 = 16 * L + 4 * i

                    def up(e, narrow):
                        if e == 0:
                            pe.wait_ge(S("hg_act"), 5 * L + i + 1)
                            pe.wait_ge(S("hg_dve"), 5 * L + i + 1)
                        for w, sem, last_reader, bk in (("w1", "a_ps", "sil_ready", 0), ("w3", "b_ps", "he_ready", 2)):
                            j = AT[(w, e)]
                            loaded(pe, n0 + j, i)
                            if e >= 1 or L == 1:
                                pe.wait_ge(S(last_reader), e0 + e - 1 + PRIMED.get(last_reader, 0))
                            product_up(bank[bk + e % 2], u3(n0 + j), narrow).then_inc(S(sem), 1)

                    def down(e, narrow):
                        pe.wait_ge(S("he_ready"), 1 + e0 + e + 1)
                        pe.wait_ge(S("heT_ready"), 1 + e0 + e)
                        turn_he(narrow).then_inc(S("heT_ps"), 1)
                        j = AT[("w2", e)]
                        loaded(pe, n0 + j, i)
                        pe.wait_ge(S("heT_ready"), 1 + e0 + e + 1)
                        if e == 0:
                            pe.wait_ge(S("y_act"), 1 + NG * L + i)
                            pe.wait_ge(S("y_dve"), 1 + NG * L + i)
                        product_down(u3(n0 + j, D), narrow, e == 0, e == EPG - 1).then_inc(S("y_ps"), 1)

                    is_narrow = pe.value_load(rti[0:1, bass.ds(i + 2, 1)], min_val=0, max_val=1)
                    for narrow, branch in ((True, is_narrow > 0), (False, is_narrow < 1)):
                        with pe.If(branch):
                            up(0, narrow)
                            up(1, narrow)
                            down(0, narrow)
                            up(2, narrow)
                            down(1, narrow)
                            up(3, narrow)
                            down(2, narrow)
                            pe.wait_ge(S("sil_ready"), 1 + e0 + 3)
                            pe.wait_ge(S("he_ready"), 1 + e0 + 3)
                            gather(i + 1)
                            down(3, narrow)
                    if L == 0:
                        pe.wait_ge(S("gemv_done"), A_HALVES + 2 + 2 * i)
                        pe.wait_ge(S("mod_cols"), 2)
                        pe.wait_ge(S("mod1_evac"), 1 + i)
                        mod_cols(0, 64)
                pe.wait_ge(S("over_known"), L + 1)
                n_over = pe.value_load(rti[0:1, 0:1], min_val=0, max_val=T)
                pe.wait_ge(S("y_ps"), 16 * (L + 1))
                for _ in range(SLOTS):
                    pe.sem_inc(S(f"over_used{L}"), 1)
                pe.wait_ge(S("he_ready"), 1 + 16 * L + 16)
                pe.wait_ge(S("sil_ready"), 1 + 16 * L + 16)
                pe.wait_ge(S("hg_act"), 5 * L + 5)
                pe.wait_ge(S("hg_dve"), 5 * L + 5)
                for g in range(NG):
                    for b in range(NB):
                        last = tr(bank[g // 2][:, (g % 2) * T + b * P:(g % 2) * T + (b + 1) * P], pick[:, b, g, :])
                last.then_inc(S("pickT_ps"), 1)
                pe.wait_ge(S("y_act"), 1 + NG * (L + 1))
                pe.wait_ge(S("y_dve"), 1 + NG * (L + 1))
                gate_row(n)
                pe.wait_ge(S("pickT_ready"), L + 1)
                for b in range(NB):
                    for h in range(2):
                        for g in range(NG):
                            last = mm(bank[2 * b + h], pickT[:, g, b * P:(b + 1) * P],
                                      yg[:, g, h * HALF:(h + 1) * HALF], start=g == 0, stop=g == NG - 1)
                        last.then_inc(S("sc_ps"), 1)
                with pe.If(n_over > 0):
                    pe.wait_ge(S("x_main"), L + 1)
                    for narrow, branch in ((True, n_over < 65), (False, n_over > 64)):
                        with pe.If(branch):
                            with pe.Fori(0, EPG // 2) as ee:
                                for u in range(2):
                                    e = ee * 2 + u
                                    for j in range(2):
                                        pe.wait_ge(S(f"over_in{L}_{3 * u + j}"), 16 * (ee + 1))
                                        product_up(bank[2 * j], u3(3 * u + j), narrow).then_inc(
                                            S(f"over_used{L}"), 1)
                                    pe.wait_ge(S(f"over_he{L}"), e + 1)
                                    turn_he(narrow).then_inc(S(f"over_heT{L}"), 1)
                                    pe.wait_ge(S(f"over_hT{L}"), e + 1)
                                    pe.wait_ge(S(f"over_yg{L}"), 1 + e)
                                    pe.wait_ge(S(f"over_in{L}_{3 * u + 2}"), 16 * (ee + 1))
                                    product_down(u3(3 * u + 2, D), narrow, True, True).then_inc(
                                        S(f"over_used{L}"), 1)
                    pe.wait_ge(S(f"over_yg{L}"), 1 + EPG)
                    for b in range(NB):
                        last = tr(bank[6][:, b * P:(b + 1) * P], pick[:, b, NG, :])
                    last.then_inc(S(f"over_heT{L}"), 1)
                    pe.wait_ge(S(f"over_he{L}"), EPG + 1)
                    for b in range(NB):
                        for h in range(2):
                            last = mm(bank[2 * b + h], pickT[:, 0, b * P:(b + 1) * P],
                                      yg[:, 0, h * HALF:(h + 1) * HALF], start=True, stop=True)
                    last.then_inc(S(f"over_heT{L}"), 1)
                pe.wait_ge(S("x_new"), 2 * L + 2)

            ffn(0)

            turn_x(2)
            hT_ready(2)

            def bu(k, m, j):
                if j == 0:
                    pe.wait_ge(S("cur_ready"), k + 1)
                for q4 in (2 * j, 2 * j + 1):
                    pp = slice(32 * q4, 32 * q4 + 32)
                    for w in range(2):
                        last = mm(PS[:, q4, w * T:(w + 1) * T], bcur[pp, m, w, :], ucur[pp, m, :], start=True, stop=True)
                    last.then_inc(S("bu_ready"), 1)

            def fold_unit(m, lo, hi):
                for k in range(lo, hi):
                    last = mm(bank[7][0:1, :], condc[:, k:k + 1], u3(ADA_BASE + m)[:, k, :], start=k == 0,
                              stop=k == KD - 1)
                return last

            bu(0, 0, 0)
            bu(0, 0, 1)
            with pe.Fori(0, KD // 2) as kk:
                for m, j in ((0, 0), (0, 1), (1, 0), (1, 1)):
                    n = 4 * kk + 2 * m + j
                    pe.wait_ge(S("bu_used"), 1 + n + 1)
                    bu(2 * kk + m + 1, 1 - m, j)
                    if j == 0:
                        pe.wait_ge(S("yv_ready"), 1 + 2 * kk + m)
                    if j == 1:
                        fold_unit(m, 6, KD).then_inc(S("mod_ps"), 1)
                    pe.wait_ge(S("q_ready"), 2 + n + 1)
                    for w in range(4):
                        for q_ in range(2):
                            q4 = 2 * j + q_
                            last = mm(bank[4][32 * q4:32 * q4 + 32, 0:T], ccur[:, m, w // 2, 32 * q4:32 * q4 + 32],
                                      qq[j][:, w, q_ * T:(q_ + 1) * T], start=w == 0, stop=w == 3)
                    last.then_inc(S("q_used"), 1)
                    if j == 0:
                        pe.wait_ge(S(f"ada_ring{4 + m}"), 16 * 2 + 16 * (kk + 1))
                        fold_unit(m, 0, 6)
                    if j == 1:
                        pe.wait_ge(S("ada_act"), 4 * kk + 2 * m + 1)
                        for c4 in range(4):
                            last = mm(bank[5][:, c4:c4 + 1], arow[:, c4 * P:(c4 + 1) * P], ones[0:1, 0:1],
                                      start=True, stop=True)
                        last.then_inc(S("mod_ps"), 1)
            pe.wait_ge(S("yv_ready"), 1 + KD)
            gate_row(2)
            pe.wait_ge(S("act_ready"), 1 + KD)
            pe.wait_ge(S("glub_in"), 16)
            for h in range(2):
                if h:
                    pe.wait_ge(S("grow_ready"), 3)
                for part in range(2):
                    n = GLU_BASE + 2 * h + part
                    loaded(pe, n)
                    r = h + 2 * part
                    for b in range(NB):
                        dst = bank[4 * h + 2 * part + b]
                        mm(dst, bcol(ident[0:4, r:r + 1]), glub, start=True, stop=False)
                        for k in range(KD):
                            last = mm(dst, actT[:, k, b * P:(b + 1) * P], u3(n)[:, k, :], start=False, stop=k == KD - 1)
                    last.then_inc(S("glu_ps"), 1)
            pe.wait_ge(S("x_new"), 3)
            ffn(1)


_OUT = (1, T, D)


def kernel(**inputs):
    import numpy as np
    import concourse.bacc as bacc
    from concourse.bass_utils import run_bass_kernel_spmd

    nc = bacc.Bacc("TRN2", target_bir_lowering=False, num_devices=1)
    arrays, a = {}, {}
    for name, value in inputs.items():
        value = np.ascontiguousarray(value)
        arrays[f"in_{name}"] = value
        a[name] = nc.dram_tensor(f"in_{name}", value.shape, mybir.dt.from_np(value.dtype), kind="ExternalInput").ap()
    out = nc.dram_tensor("out", _OUT, F32, kind="ExternalOutput").ap()
    build(nc, a, out)
    r = run_bass_kernel_spmd(nc, [arrays], core_ids=[0])
    return r.results[0]["out"]
```
